# Optimizing a Trainium2 kernel written in Bass

```python
import math
import jax
import jax.numpy as jnp
from jax import lax
import numpy as np
import jax, jax.numpy as jnp

D_MODEL = 1024
BATCH = 1
SEQ = 512
DEPTH = 2

GRID_W = 64
CTX_LEN = 256
HEAD_DIM = 64
ATTN_W = D_MODEL // 2
N_Q_HEADS = ATTN_W // HEAD_DIM
N_KV_HEADS = max(1, N_Q_HEADS // 4)
GQA_GROUP = N_Q_HEADS // N_KV_HEADS
KV_W = N_KV_HEADS * HEAD_DIM
ROPE_AXIS_DIM = HEAD_DIM // 2
ROPE_THETA = 10000.0
Q_BLOCK = 128
FOURIER_W = D_MODEL // 4
FOURIER_GROUPS = 4
FOURIER_GROUP_DIM = FOURIER_W // FOURIER_GROUPS
HYENA_W = D_MODEL - ATTN_W - FOURIER_W
HYENA_BANDS = 16
HYENA_EMB = 1 + 2 * HYENA_BANDS
HYENA_FILTER_W = 64
HYENA_FAST_DECAY = 0.3
HYENA_SLOW_DECAY = 1.5
HYENA_TARGET = 1e-2
MIX_W = ATTN_W + FOURIER_W + HYENA_W
Q0 = 0
K0 = ATTN_W
V0 = K0 + KV_W
F0 = V0 + KV_W
H0 = F0 + FOURIER_W
IN_W = H0 + 3 * HYENA_W
D_FF = int(math.ceil(8 * D_MODEL / 3 / 128)) * 128
NORM_EPS = 1e-6


def rmsnorm(x, g):
    xf = x.astype(jnp.float32)
    y = xf * lax.rsqrt(jnp.mean(xf * xf, axis=-1, keepdims=True) + NORM_EPS)
    return (y * g.astype(jnp.float32)).astype(x.dtype)

def dwconv3(u, w, b):
    up = jnp.pad(u, ((0, 0), (1, 1), (0, 0)))
    return up[:, :-2] * w[0] + up[:, 1:-1] * w[1] + up[:, 2:] * w[2] + b

def rope2d(x, ang_r, ang_c):
    def rot(xa, ang):
        cos = jnp.cos(ang)[:, None, :].astype(xa.dtype)
        sin = jnp.sin(ang)[:, None, :].astype(xa.dtype)
        x1, x2 = jnp.split(xa, 2, axis=-1)
        return jnp.concatenate([x1 * cos - x2 * sin, x2 * cos + x1 * sin], axis=-1)
    xr, xc = jnp.split(x, 2, axis=-1)
    return jnp.concatenate([rot(xr, ang_r), rot(xc, ang_c)], axis=-1)

def attend(q, k, v):
    s = jnp.einsum('bqhgd,bkhd->bhgqk', q, k).astype(jnp.float32) * (HEAD_DIM ** -0.5)
    p = jax.nn.softmax(s, axis=-1).astype(v.dtype)
    return jnp.einsum('bhgqk,bkhd->bqhgd', p, v)

def blocked_attention(q, k, v):
    B, L = q.shape[0], q.shape[1]
    nb = L // Q_BLOCK
    qb = q.reshape(B, nb, Q_BLOCK, N_KV_HEADS, GQA_GROUP, HEAD_DIM).swapaxes(0, 1)
    ob = lax.map(lambda qq: attend(qq, k, v), qb)
    return ob.swapaxes(0, 1).reshape(B, L, ATTN_W)

def fourier_mix(f, w):
    B, L, _ = f.shape
    fg = f.astype(jnp.float32).reshape(B, L, FOURIER_GROUPS, FOURIER_GROUP_DIM)
    y = jnp.fft.fft2(fg, axes=(1, 3), norm='ortho').real.astype(f.dtype)
    return y.reshape(B, L, FOURIER_W) @ w

def hyena_filter(L, w1, b1, fr1, w2, b2, fr2, w3):
    f32 = jnp.float32
    t = jnp.linspace(0.0, 1.0, L, dtype=f32)[:, None]
    bands = jnp.linspace(1e-4, HYENA_BANDS - 1, HYENA_BANDS, dtype=f32)
    ang = (2.0 * math.pi) * jnp.arange(L, dtype=f32)[:, None] / L * bands[None, :]
    z = jnp.concatenate([t, jnp.cos(ang), -jnp.sin(ang)], axis=-1)
    h = jnp.sin(fr1.astype(f32) * (z @ w1.astype(f32) + b1.astype(f32)))
    h = jnp.sin(fr2.astype(f32) * (h @ w2.astype(f32) + b2.astype(f32)))
    h = h @ w3.astype(f32)
    deltas = jnp.abs(jnp.linspace(math.log(HYENA_TARGET) / HYENA_SLOW_DECAY,
                                  math.log(HYENA_TARGET) / HYENA_FAST_DECAY, HYENA_W, dtype=f32))
    decay = jnp.exp(-t * deltas[None, :])
    h_fwd = h[:, :HYENA_W] * decay
    h_bwd = h[:, HYENA_W:] * decay
    two = jnp.concatenate([h_fwd, jnp.zeros((1, HYENA_W), f32), h_bwd[:0:-1]], axis=0)
    return two / jnp.sum(jnp.abs(two), axis=0, keepdims=True)

def hyena_longconv(u, filt, bias):
    L = u.shape[1]
    n = 2 * L
    uf = jnp.fft.rfft(u.astype(jnp.float32), n=n, axis=1)
    kf = jnp.fft.rfft(filt, n=n, axis=0)
    y = jnp.fft.irfft(uf * kf[None], n=n, axis=1)[:, :L]
    return (y + u.astype(jnp.float32) * bias.astype(jnp.float32)).astype(u.dtype)

def hyena_mix(p, conv_w, conv_b, filt, bias):
    uc = dwconv3(p, conv_w, conv_b)
    x0, x1, v = jnp.split(uc, 3, axis=-1)
    return x0 * hyena_longconv(x1 * v, filt, bias)

def conv_ffn(h, w_up, w_c, b_c, w_down):
    u = dwconv3(h @ w_up, w_c, b_c)
    gate, val = jnp.split(u, 2, axis=-1)
    return (jax.nn.silu(gate) * val) @ w_down

def first_inputs(seed: int = 0) -> dict:
    key = jax.random.key(seed)
    ks = jax.random.split(key, 32)
    f32 = jnp.float32

    def nrm(k, shape, scale):
        return jax.random.normal(k, shape, f32) * scale

    def gain(k, shape):
        return 1.0 + 0.05 * jax.random.normal(k, shape, f32)

    return {
        'x': nrm(ks[0], (BATCH, SEQ, D_MODEL), 1.0),
        'c': nrm(ks[1], (BATCH, D_MODEL), 1.0),
        'ctx': nrm(ks[2], (BATCH, CTX_LEN, D_MODEL), 1.0),
        'c_ctx': nrm(ks[3], (D_MODEL,), 1.0),
        'w_mod': nrm(ks[4], (DEPTH, D_MODEL, 6 * D_MODEL), 0.5 * D_MODEL ** -0.5),
        'b_mod': nrm(ks[5], (DEPTH, 6 * D_MODEL), 0.02),
        'g_pre_mix': gain(ks[6], (DEPTH, D_MODEL)),
        'g_post_mix': gain(ks[7], (DEPTH, D_MODEL)),
        'g_pre_ffn': gain(ks[8], (DEPTH, D_MODEL)),
        'g_post_ffn': gain(ks[9], (DEPTH, D_MODEL)),
        'w_in': nrm(ks[10], (DEPTH, D_MODEL, IN_W), D_MODEL ** -0.5),
        'g_q': gain(ks[11], (DEPTH, HEAD_DIM)),
        'g_k': gain(ks[12], (DEPTH, HEAD_DIM)),
        'w_fourier': nrm(ks[13], (DEPTH, FOURIER_W, FOURIER_W), FOURIER_W ** -0.5),
        'w_hy_conv': nrm(ks[14], (DEPTH, 3, 3 * HYENA_W), 3 ** -0.5),
        'b_hy_conv': nrm(ks[15], (DEPTH, 3 * HYENA_W), 0.02),
        'hy_w1': nrm(ks[16], (DEPTH, HYENA_EMB, HYENA_FILTER_W), HYENA_EMB ** -0.5),
        'hy_b1': nrm(ks[17], (DEPTH, HYENA_FILTER_W), 0.1),
        'hy_fr1': gain(ks[18], (DEPTH, HYENA_FILTER_W)),
        'hy_w2': nrm(ks[19], (DEPTH, HYENA_FILTER_W, HYENA_FILTER_W), HYENA_FILTER_W ** -0.5),
        'hy_b2': nrm(ks[20], (DEPTH, HYENA_FILTER_W), 0.1),
        'hy_fr2': gain(ks[21], (DEPTH, HYENA_FILTER_W)),
        'hy_w3': nrm(ks[22], (DEPTH, HYENA_FILTER_W, 2 * HYENA_W), HYENA_FILTER_W ** -0.5),
        'hy_bias': nrm(ks[23], (DEPTH, HYENA_W), 0.1),
        'w_out': nrm(ks[24], (DEPTH, MIX_W, D_MODEL), MIX_W ** -0.5),
        'w_up': nrm(ks[25], (DEPTH, D_MODEL, 2 * D_FF), D_MODEL ** -0.5),
        'w_ffn_conv': nrm(ks[26], (DEPTH, 3, 2 * D_FF), 3 ** -0.5),
        'b_ffn_conv': nrm(ks[27], (DEPTH, 2 * D_FF), 0.02),
        'w_down': nrm(ks[28], (DEPTH, D_FF, D_MODEL), D_FF ** -0.5),
    }

def first_block(x, c, ctx, c_ctx, w_mod, b_mod, g_pre_mix, g_post_mix, g_pre_ffn, g_post_ffn,
              w_in, g_q, g_k, w_fourier, w_hy_conv, b_hy_conv, hy_w1, hy_b1, hy_fr1,
              hy_w2, hy_b2, hy_fr2, hy_w3, hy_bias, w_out, w_up, w_ffn_conv, b_ffn_conv, w_down):
    B, L, _ = x.shape
    C = ctx.shape[1]
    ROWS = L // GRID_W
    row = jnp.repeat(jnp.arange(ROWS, dtype=jnp.float32), GRID_W)
    col = jnp.tile(jnp.arange(GRID_W, dtype=jnp.float32), ROWS)
    inv = ROPE_THETA ** (-jnp.arange(0, ROPE_AXIS_DIM, 2, dtype=jnp.float32) / ROPE_AXIS_DIM)
    ang_r = row[:, None] * inv[None, :]
    ang_c = col[:, None] * inv[None, :]

    for i in range(DEPTH):
        last = i == DEPTH - 1
        mod_x = (jax.nn.silu(c) @ w_mod[i] + b_mod[i])[:, None, :]
        mod_c = (jax.nn.silu(c_ctx) @ w_mod[i] + b_mod[i])[None, None, :]
        sh1, sc1, ga1, sh2, sc2, ga2 = jnp.split(mod_x, 6, axis=-1)
        csh1, csc1, cga1, csh2, csc2, cga2 = jnp.split(mod_c, 6, axis=-1)
        hy_params = (hy_w1[i], hy_b1[i], hy_fr1[i], hy_w2[i], hy_b2[i], hy_fr2[i], hy_w3[i])

        hx = rmsnorm(x, g_pre_mix[i]) * (1.0 + sc1) + sh1
        hc = rmsnorm(ctx, g_pre_mix[i]) * (1.0 + csc1) + csh1
        px = hx @ w_in[i]
        pc = hc @ (w_in[i][:, K0:F0] if last else w_in[i])
        pc_kv = pc if last else pc[..., K0:F0]

        kc = rmsnorm(pc_kv[..., :KV_W].reshape(B, C, N_KV_HEADS, HEAD_DIM), g_k[i])
        vc = pc_kv[..., KV_W:].reshape(B, C, N_KV_HEADS, HEAD_DIM)
        q = rope2d(rmsnorm(px[..., Q0:K0].reshape(B, L, N_Q_HEADS, HEAD_DIM), g_q[i]), ang_r, ang_c)
        k = rope2d(rmsnorm(px[..., K0:V0].reshape(B, L, N_KV_HEADS, HEAD_DIM), g_k[i]), ang_r, ang_c)
        v = px[..., V0:F0].reshape(B, L, N_KV_HEADS, HEAD_DIM)
        k_all = jnp.concatenate([kc, k], axis=1)
        v_all = jnp.concatenate([vc, v], axis=1)
        attn_x = blocked_attention(q.reshape(B, L, N_KV_HEADS, GQA_GROUP, HEAD_DIM), k_all, v_all)
        four_x = fourier_mix(px[..., F0:H0], w_fourier[i])
        hy_x = hyena_mix(px[..., H0:], w_hy_conv[i], b_hy_conv[i], hyena_filter(L, *hy_params), hy_bias[i])
        mix_x = jnp.concatenate([attn_x, four_x, hy_x], axis=-1) @ w_out[i]
        x = x + ga1 * rmsnorm(mix_x, g_post_mix[i])

        if not last:
            qc = rmsnorm(pc[..., Q0:K0].reshape(B, C, N_Q_HEADS, HEAD_DIM), g_q[i])
            attn_c = attend(qc.reshape(B, C, N_KV_HEADS, GQA_GROUP, HEAD_DIM), kc, vc).reshape(B, C, ATTN_W)
            four_c = fourier_mix(pc[..., F0:H0], w_fourier[i])
            hy_c = hyena_mix(pc[..., H0:], w_hy_conv[i], b_hy_conv[i], hyena_filter(C, *hy_params), hy_bias[i])
            mix_c = jnp.concatenate([attn_c, four_c, hy_c], axis=-1) @ w_out[i]
            ctx = ctx + cga1 * rmsnorm(mix_c, g_post_mix[i])

        fx = rmsnorm(x, g_pre_ffn[i]) * (1.0 + sc2) + sh2
        yx = conv_ffn(fx, w_up[i], w_ffn_conv[i], b_ffn_conv[i], w_down[i])
        x = x + ga2 * rmsnorm(yx, g_post_ffn[i])
        if not last:
            fc = rmsnorm(ctx, g_pre_ffn[i]) * (1.0 + csc2) + csh2
            yc = conv_ffn(fc, w_up[i], w_ffn_conv[i], b_ffn_conv[i], w_down[i])
            ctx = ctx + cga2 * rmsnorm(yc, g_post_ffn[i])

    return x


DEPTH_2 = 1

N_HEADS_DIL = D_MODEL // (2 * HEAD_DIM)
N_HEADS_NA = D_MODEL // (2 * HEAD_DIM)
WIDTH_DIL = N_HEADS_DIL * HEAD_DIM
WIDTH_NA = N_HEADS_NA * HEAD_DIM
MIX_WIDTH = WIDTH_DIL + WIDTH_NA
DIL_PATTERNS = ((128, 1), (512, 4), (2048, 16))
DIL_BLOCK = 64
NA_WIN_ROWS = 8
NA_WIN_COLS = 16
NA_Q_ROWS = 4
NA_Q_COLS = 16
NA_K_COLS = 32
N_GROUPS = 4
EXPERTS_PER_GROUP = 4
N_EXPERTS = N_GROUPS * EXPERTS_PER_GROUP
TOP_K_EXPERT = 2
D_EXPERT = 256
RMS_EPS = 1e-6
NEG_INF = -1e30


def rms_norm(x, gain):
    xf = x.astype(jnp.float32)
    xf = xf * lax.rsqrt(jnp.mean(xf * xf, axis=-1, keepdims=True) + RMS_EPS)
    return (xf * gain.astype(jnp.float32)).astype(x.dtype)

def alibi_slopes(n_heads):
    return jnp.exp2(-8.0 * jnp.arange(1, n_heads + 1, dtype=jnp.float32) / n_heads)

def dilated_window_attention(q, k, v, slopes, window, dilation):
    B, H, S, Dh = q.shape
    L = S // dilation
    radius = (window // 2) // dilation
    blk = DIL_BLOCK
    n_blk = -(-L // blk)
    Lp = n_blk * blk

    def residue_major(t, lo, hi):
        t = t.reshape(B, H, L, dilation, Dh).transpose(0, 1, 3, 2, 4)
        return jnp.pad(t, ((0, 0), (0, 0), (0, 0), (lo, hi), (0, 0)))

    def key_blocks(t):
        tp = residue_major(t, blk, Lp - L + blk).reshape(B, H, dilation, n_blk + 2, blk, Dh)
        return jnp.concatenate([tp[:, :, :, i:i + n_blk] for i in range(3)], axis=4)

    qb = residue_major(q, 0, Lp - L).reshape(B, H, dilation, n_blk, blk, Dh)
    kb = key_blocks(k)
    vb = key_blocks(v)

    q_pos = jnp.arange(Lp).reshape(n_blk, blk)
    k_pos = (jnp.arange(n_blk)[:, None] - 1) * blk + jnp.arange(3 * blk)[None, :]
    off = jnp.abs(k_pos[:, None, :] - q_pos[:, :, None])
    valid = ((off <= radius) & (k_pos[:, None, :] >= 0) & (k_pos[:, None, :] < L)
             & (q_pos[:, :, None] < L))
    dist = (off * dilation).astype(jnp.float32)

    s = jnp.einsum('bhrnqd,bhrnkd->bhrnqk', qb, kb).astype(jnp.float32) * (HEAD_DIM ** -0.5)
    s = s - slopes[None, :, None, None, None, None] * dist
    s = jnp.where(valid, s, NEG_INF)
    mx = jnp.max(s, axis=-1, keepdims=True)
    p = jnp.exp(s - mx)
    den = jnp.sum(p, axis=-1)
    o = jnp.einsum('bhrnqk,bhrnkd->bhrnqd', p, vb.astype(jnp.float32)) / den[..., None]
    lse = mx[..., 0] + jnp.log(den)

    o = o.reshape(B, H, dilation, Lp, Dh)[:, :, :, :L].transpose(0, 1, 3, 2, 4).reshape(B, H, S, Dh)
    lse = lse.reshape(B, H, dilation, Lp)[..., :L].transpose(0, 1, 3, 2).reshape(B, H, S)
    return o, lse

def dilated_mixture_attention(q, k, v, slopes):
    results = [dilated_window_attention(q, k, v, slopes, w, d) for (w, d) in DIL_PATTERNS]
    outs = jnp.stack([r[0] for r in results])
    lses = jnp.stack([r[1] for r in results])
    weights = jax.nn.softmax(lses, axis=0)
    return jnp.sum(weights[..., None] * outs, axis=0).astype(q.dtype)

def neighbourhood_attention(q, k, v, rpb):
    B, H, S, Dh = q.shape
    rows = S // GRID_W
    wh = min(NA_WIN_ROWS, rows)
    q_rows = math.gcd(rows, NA_Q_ROWS)
    k_rows = min(wh + q_rows - 1, rows)
    n_rb = rows // q_rows
    n_cb = GRID_W // NA_Q_COLS

    r = jnp.arange(rows)
    c = jnp.arange(GRID_W)
    row_start = jnp.clip(r - wh // 2, 0, rows - wh)
    col_start = jnp.clip(c - NA_WIN_COLS // 2, 0, GRID_W - NA_WIN_COLS)
    key_row = jnp.clip(row_start[::q_rows], 0, rows - k_rows)[:, None] + jnp.arange(k_rows)
    key_col = (jnp.clip(jnp.arange(n_cb) * NA_Q_COLS - NA_WIN_COLS // 2, 0, GRID_W - NA_K_COLS)[:, None]
               + jnp.arange(NA_K_COLS))

    q_row = r.reshape(n_rb, q_rows)
    q_col = c.reshape(n_cb, NA_Q_COLS)
    rs = row_start.reshape(n_rb, q_rows)[:, :, None]
    cs = col_start.reshape(n_cb, NA_Q_COLS)[:, :, None]
    row_ok = (key_row[:, None, :] >= rs) & (key_row[:, None, :] < rs + wh)
    col_ok = (key_col[:, None, :] >= cs) & (key_col[:, None, :] < cs + NA_WIN_COLS)
    mask = row_ok[:, None, :, None, :, None] & col_ok[None, :, None, :, None, :]
    dr = jnp.clip(key_row[:, None, :] - q_row[:, :, None] + NA_WIN_ROWS - 1, 0, 2 * NA_WIN_ROWS - 2)
    dc = jnp.clip(key_col[:, None, :] - q_col[:, :, None] + NA_WIN_COLS - 1, 0, 2 * NA_WIN_COLS - 2)
    bias = rpb[:, dr[:, None, :, None, :, None], dc[None, :, None, :, None, :]].astype(jnp.float32)

    def grid(t):
        return t.reshape(B, H, rows, GRID_W, Dh)

    qb = grid(q).reshape(B, H, n_rb, q_rows, n_cb, NA_Q_COLS, Dh).transpose(0, 1, 2, 4, 3, 5, 6)
    ridx = key_row[:, None, :, None]
    cidx = key_col[None, :, None, :]
    kg = grid(k)[:, :, ridx, cidx]
    vg = grid(v)[:, :, ridx, cidx]

    s = jnp.einsum('bhijqcd,bhijkld->bhijqckl', qb, kg).astype(jnp.float32) * (HEAD_DIM ** -0.5)
    s = jnp.where(mask, s + bias[None], NEG_INF)
    p = jax.nn.softmax(s, axis=(-2, -1))
    o = jnp.einsum('bhijqckl,bhijkld->bhijqcd', p, vg.astype(jnp.float32))
    o = o.transpose(0, 1, 2, 4, 3, 5, 6).reshape(B, H, S, Dh)
    return o.astype(q.dtype)

def hierarchical_moe(x, w_group, b_group, w_router, b_router, w_gate, w_up, w_down):
    B, S, D = x.shape
    n_tok = B * S
    xf = x.reshape(n_tok, D)
    g_logits = (xf @ w_group).astype(jnp.float32) + b_group.astype(jnp.float32)
    g_weight, g_idx = lax.top_k(jax.nn.softmax(g_logits, axis=-1), 1)
    e_logits = ((xf @ w_router).astype(jnp.float32) + b_router.astype(jnp.float32)
                ).reshape(n_tok, N_GROUPS, EXPERTS_PER_GROUP)
    e_in_group = jnp.take_along_axis(e_logits, g_idx[:, :, None], axis=1)[:, 0]
    e_val, e_idx = lax.top_k(e_in_group, TOP_K_EXPERT)
    e_weight = jax.nn.softmax(e_val, axis=-1) * g_weight
    expert_id = g_idx * EXPERTS_PER_GROUP + e_idx
    combine = jnp.sum(jax.nn.one_hot(expert_id, N_EXPERTS, dtype=jnp.float32) * e_weight[..., None], axis=1)
    gate = jnp.einsum('nd,edf->nef', xf, w_gate)
    up = jnp.einsum('nd,edf->nef', xf, w_up)
    act = jax.nn.silu(gate) * up * combine[:, :, None].astype(x.dtype)
    out = jnp.einsum('nef,efd->nd', act, w_down)
    return out.reshape(B, S, D).astype(x.dtype)

def second_inputs(seed: int = 0) -> dict:
    key = jax.random.key(seed)
    ks = jax.random.split(key, 17)
    f32 = jnp.float32

    def nrm(k, shape, scale):
        return jax.random.normal(k, shape, f32) * scale

    return {
        'x': nrm(ks[0], (BATCH, SEQ, D_MODEL), 1.0),
        'norm_mix_g': 1.0 + nrm(ks[1], (DEPTH_2, D_MODEL), 0.02),
        'w_in': nrm(ks[2], (DEPTH_2, D_MODEL, 3 * MIX_WIDTH), D_MODEL ** -0.5),
        'rpb': nrm(ks[3], (DEPTH_2, N_HEADS_NA, 2 * NA_WIN_ROWS - 1, 2 * NA_WIN_COLS - 1), 0.1),
        'g_out_dil': 1.0 + nrm(ks[4], (DEPTH_2, WIDTH_DIL), 0.02),
        'g_out_na': 1.0 + nrm(ks[5], (DEPTH_2, WIDTH_NA), 0.02),
        'w_out': nrm(ks[6], (DEPTH_2, MIX_WIDTH, D_MODEL), MIX_WIDTH ** -0.5),
        'norm_ffn_g': 1.0 + nrm(ks[7], (DEPTH_2, D_MODEL), 0.02),
        'w_group': nrm(ks[8], (DEPTH_2, D_MODEL, N_GROUPS), D_MODEL ** -0.5),
        'b_group': nrm(ks[9], (DEPTH_2, N_GROUPS), 0.01),
        'w_router': nrm(ks[10], (DEPTH_2, D_MODEL, N_EXPERTS), D_MODEL ** -0.5),
        'b_router': nrm(ks[11], (DEPTH_2, N_EXPERTS), 0.01),
        'w_gate': nrm(ks[12], (DEPTH_2, N_EXPERTS, D_MODEL, D_EXPERT), D_MODEL ** -0.5),
        'w_up': nrm(ks[13], (DEPTH_2, N_EXPERTS, D_MODEL, D_EXPERT), D_MODEL ** -0.5),
        'w_down': nrm(ks[14], (DEPTH_2, N_EXPERTS, D_EXPERT, D_MODEL), D_EXPERT ** -0.5),
        'norm_final_g': 1.0 + nrm(ks[15], (D_MODEL,), 0.02),
    }

def second_block(x, norm_mix_g, w_in, rpb, g_out_dil, g_out_na, w_out, norm_ffn_g,
              w_group, b_group, w_router, b_router, w_gate, w_up, w_down, norm_final_g):
    B, S, _ = x.shape
    slopes = alibi_slopes(N_HEADS_DIL)
    h = x
    for layer in range(DEPTH_2):
        hn = rms_norm(h, norm_mix_g[layer])
        proj = hn @ w_in[layer]
        p_dil = proj[..., :3 * WIDTH_DIL].reshape(B, S, 3, N_HEADS_DIL, HEAD_DIM).transpose(2, 0, 3, 1, 4)
        p_na = proj[..., 3 * WIDTH_DIL:].reshape(B, S, 3, N_HEADS_NA, HEAD_DIM).transpose(2, 0, 3, 1, 4)
        y_dil = dilated_mixture_attention(p_dil[0], p_dil[1], p_dil[2], slopes)
        y_na = neighbourhood_attention(p_na[0], p_na[1], p_na[2], rpb[layer])
        y_dil = rms_norm(y_dil.transpose(0, 2, 1, 3).reshape(B, S, WIDTH_DIL), g_out_dil[layer])
        y_na = rms_norm(y_na.transpose(0, 2, 1, 3).reshape(B, S, WIDTH_NA), g_out_na[layer])
        h = h + jnp.concatenate([y_dil, y_na], axis=-1) @ w_out[layer]
        h = h + hierarchical_moe(rms_norm(h, norm_ffn_g[layer]), w_group[layer], b_group[layer],
                                 w_router[layer], b_router[layer], w_gate[layer], w_up[layer], w_down[layer])
    return rms_norm(h, norm_final_g)


def setup_inputs(seed=0):
    out = dict(first_inputs(seed))
    for name, value in second_inputs(seed + 1).items():
        if name != "x":
            out[name + "_2"] = value
    return out


def reference(
    x, c, ctx, c_ctx, w_mod, b_mod, g_pre_mix, g_post_mix, g_pre_ffn, g_post_ffn, w_in, g_q,
    g_k, w_fourier, w_hy_conv, b_hy_conv, hy_w1, hy_b1, hy_fr1, hy_w2, hy_b2, hy_fr2, hy_w3,
    hy_bias, w_out, w_up, w_ffn_conv, b_ffn_conv, w_down, norm_mix_g_2, w_in_2, rpb_2,
    g_out_dil_2, g_out_na_2, w_out_2, norm_ffn_g_2, w_group_2, b_group_2, w_router_2,
    b_router_2, w_gate_2, w_up_2, w_down_2, norm_final_g_2,
):
    x = first_block(
        x, c, ctx, c_ctx, w_mod, b_mod, g_pre_mix, g_post_mix, g_pre_ffn, g_post_ffn, w_in, g_q,
        g_k, w_fourier, w_hy_conv, b_hy_conv, hy_w1, hy_b1, hy_fr1, hy_w2, hy_b2, hy_fr2, hy_w3,
        hy_bias, w_out, w_up, w_ffn_conv, b_ffn_conv, w_down,
    )
    return second_block(
        x, norm_mix_g_2, w_in_2, rpb_2, g_out_dil_2, g_out_na_2, w_out_2, norm_ffn_g_2,
        w_group_2, b_group_2, w_router_2, b_router_2, w_gate_2, w_up_2, w_down_2,
        norm_final_g_2,
    )


_drawn_inputs = setup_inputs


def setup_inputs(seed=0):
    import zlib

    import numpy as np

    out = dict(_drawn_inputs(seed))
    spreads = {}
    factors = {'g_q': 8.0,
     'g_k': 8.0,
     'b_hy_conv': 7.871,
     'hy_b1': 2.955,
     'hy_fr1': 8.0,
     'hy_b2': 3.051,
     'hy_fr2': 8.0,
     'b_ffn_conv': 2.693,
     'g_out_dil_2': 3.976,
     'g_out_na_2': 4.962,
     'norm_ffn_g_2': 3.495,
     'b_group_2': 8.0,
     'b_router_2': 8.0,
     'norm_final_g_2': 2.915}
    for name, (base, spread) in spreads.items():
        noise = np.random.default_rng([zlib.crc32(name.encode()), seed]).standard_normal(out[name].shape)
        drawn = base * np.exp(spread * noise) if base else spread * noise
        out[name] = jnp.asarray(drawn.astype(out[name].dtype))
    for name, factor in factors.items():
        out[name] = (out[name] * factor).astype(out[name].dtype)
    return out
```

```python
import math
from contextlib import ExitStack

import numpy as np
import concourse.bass as bass
from concourse import mybir

F32 = mybir.dt.float32
F32R = mybir.dt.float32r
ALU = mybir.AluOpType
ACT = mybir.ActivationFunctionType
AX_X = mybir.AxisListType.X

P = 128
D = 1024
KT = D // P
TX, TC = 512, 256
T = TX + TC
DEPTH = 2
HD = 64
NQT = 4
NHY = 6
FF = 2816
PAIRS = 11
CHUNKS = FF // P // PAIRS
NEXP, DEXP = 16, 256
EPI = 4
EPS = 1e-6
SCALE = HD ** -0.5

SLAB = KT * P
RING = 3
MOD_SLABS = DEPTH * 6 * KT
MOD_GROUP = 6
IN_T, OUT_T = 14, KT
UP_T = 2 * PAIRS
FFN_SLABS = UP_T + PAIRS
FFN_TILES = UP_T + KT
LAYER_SLABS = IN_T + OUT_T + CHUNKS * FFN_SLABS
LAYER_TILES = IN_T + OUT_T + CHUNKS * FFN_TILES
IN2_T = 24
MOE_UP = EPI * 4
MOE_SLABS = MOE_UP + KT
MOE_TURNS = NEXP // EPI
B2_SLAB = DEPTH * LAYER_SLABS
B2_TILE = DEPTH * LAYER_TILES
N_SLABS = B2_SLAB + IN2_T + OUT_T + MOE_TURNS * MOE_SLABS
NH2 = 16

V_GPM, V_GQM, V_GPF, V_GQF, V_GQ, V_GK, V_HYC, V_FFC, V_HYB, V_BMOD, V_MLP = 0, 8, 16, 24, 32, 33, 34, 58, 234, 236, 284
V_LAYER = 288
V2 = DEPTH * V_LAYER
V2_MIX, V2_OUT, V2_FFN, V2_FIN = V2, V2 + 8, V2 + 16, V2 + 24
N_VEC = V2 + 32

MAGIC = 12582912.0
TWO_PI_HI = 6.28125
TWO_PI_LO = 2 * math.pi - TWO_PI_HI
PI_IN = 3.1415925

TABW = 3 * P + TX


def program(nc, dram, out):
    x_d, ctx_d, c_d = dram["xT"], dram["ctxT"], dram["cT"]
    base = (nc.sbuf_base + 31) // 32 * 32
    at = [base]

    def place(nbytes):
        o = at[0]
        at[0] += (nbytes + 31) // 32 * 32
        return o

    def sb(name, shape, off, dt=F32):
        return nc.alloc_sbuf_tensor_at(name, shape, dt, offset=off)

    X_O = place(KT * T * 4)
    WRAW_O = place(RING * SLAB * 4)
    WHI_O = place(RING * SLAB * 4)
    WLO_O = place(RING * SLAB * 4)
    HHI_O = place(KT * T * 4)
    HLO_O = place(KT * T * 4)
    BIG = place(KT * T * 4 + 2 * PAIRS * T * 4)
    SCR = place(5 * T * 4)

    x = sb("x", [P, KT, T], X_O)
    wraw = sb("wraw", [P, RING, SLAB], WRAW_O)
    whi = sb("whi", [P, RING, SLAB], WHI_O, F32R)
    wlo = sb("wlo", [P, RING, SLAB], WLO_O, F32R)
    hhi = sb("hhi", [P, KT, T], HHI_O, F32R)
    hlo = sb("hlo", [P, KT, T], HLO_O, F32R)
    ident = sb("ident", [P, P], place(P * 4))
    ones = sb("ones", [P, P], place(P * 4))
    headones = sb("headones", [P, P], place(P * 4))
    rot = sb("rot", [P, P], place(P * 4))
    vec = sb("vec", [P, N_VEC], place(N_VEC * 4))
    mod = sb("mod", [P, DEPTH, 6 * KT, 2], place(DEPTH * 6 * KT * 2 * 4))
    mv = sb("mv", [P, DEPTH, 4, KT, 2], place(DEPTH * 4 * KT * 2 * 4))
    cs = sb("cs", [P, KT, 2], place(KT * 2 * 4))
    consts = sb("consts", [P, 16], place(64))
    cconv = sb("cconv", [P, UP_T, 4], place(UP_T * 16))
    stat = sb("stat", [P, 2, 4], place(32))
    rnorm = sb("rnorm", [P, 2], place(8))
    bmod = sb("bmod", [P, DEPTH * 6 * KT * 2], place(DEPTH * 6 * KT * 2 * 4))
    assert at[0] <= nc.sbuf_usable_end, at[0]
    eps_c, zero_c = consts[:, 0:1], consts[:, 1:2]

    y = sb("y", [P, KT, T], BIG)
    ACT_O = BIG + KT * T * 4
    ahi = sb("ahi", [P, PAIRS, T], ACT_O, F32R)
    alo = sb("alo", [P, PAIRS, T], ACT_O + PAIRS * T * 4, F32R)
    nsq = sb("nsq", [P, 2, T], ACT_O)
    nrm = sb("nrm", [P, T], ACT_O + 2 * T * 4)
    nt = sb("nt", [P, 2, T], ACT_O + 3 * T * 4)
    nfull = sb("nfull", [P, 2, T], ACT_O + 5 * T * 4)
    up = sb("up", [P, 2, 2, T], SCR)
    sil = sb("sil", [P, T], SCR + 4 * T * 4)

    pxq = sb("pxq", [P, NQT + 2, T], BIG)
    PXK, PXV = NQT, NQT + 1
    pxf = sb("pxf", [P, 2, T], BIG + 6 * T * 4)
    pxh = sb("pxh", [P, NHY, T], BIG + 8 * T * 4)
    M0 = BIG + 14 * T * 4
    cosx = sb("cosx", [P, 2, TX], SCR)
    qsq = sb("qsq", [P, T], SCR + 2 * TX * 4)
    qrs = sb("qrs", [P, 2, T], SCR + 2 * TX * 4 + T * 4)
    qtmp = sb("qtmp", [P, TX], SCR + 2 * TX * 4 + 3 * T * 4)
    fl5 = sb("fl5", [P, 2, 4, TX], M0)
    fl2 = sb("fl2", [P, 2, 2, TC], M0 + 16384)
    fab = sb("fab", [P, 6, 512], M0 + 20480)
    fy = sb("fy", [P, 2, T], M0 + 32768)
    wfo = sb("wfo", [P, 2, 256], M0 + 38912)
    fch = sb("fch", [P, 256], M0 + 40960)
    pr = sb("pr", [P, 2, T], M0)
    pt = sb("pt", [P, 2, 6, TX], M0 + 6144)
    vt = sb("vt", [P, 6, P], BIG + 6 * T * 4)
    hd5 = sb("hd5", [P, 2, 4, TX], M0 + 32768)
    hi5 = sb("hi5", [P, 2, 4, TX], M0)
    hsp = sb("hsp", [P, 4, 512], M0 + 16384)
    hys = sb("hys", [P, 4, 512], M0 + 24576)
    hd2 = sb("hd2", [P, 4, 2, TC], BIG)
    hpm = sb("hpm", [P, 4, 512], BIG + 8192)
    hut = sb("hut", [P, 6, 256], BIG + 6 * T * 4)
    hw3 = sb("hw3", [P, 512], SCR)
    hz = sb("hz", [P, 512], SCR + 2048)
    hw12 = sb("hw12", [P, 128], SCR + 4096)
    hl = sb("hl", [P, 2, 512], SCR + 4608)
    ha = sb("ha", [P, 512], SCR + 8704)
    hb = sb("hb", [P, 512], SCR + 10752)
    hdel = sb("hdel", [P, 256], SCR + 12800)
    hsum = sb("hsum", [P, 256], SCR + 13824)
    hub = sb("hub", [P, 2, T], BIG + 12 * T * 4)

    px2 = sb("px2", [P, IN2_T, TX], BIG)
    tab = sb("tab", [P, 2, TABW], BIG + 49152)
    s2 = sb("s2", [P, 2, TX], BIG + 56320)
    p2 = sb("p2", [P, 2, TX], BIG + 60416)
    pt2 = sb("pt2", [P, 2, 4, TX], BIG + 64512)
    vt2 = sb("vt2", [P, 2, 4, P], BIG + 80896)
    namask = sb("namask", [P, HD], BIG + 84992)
    comb = sb("comb", [P, NEXP, TX], BIG + KT * T * 4)
    ehi = sb("ehi", [P, 2 * EPI, TX], BIG + KT * T * 4 + 32768, F32R)
    elo = sb("elo", [P, 2 * EPI, TX], BIG + KT * T * 4 + 49152, F32R)
    wgr = sb("wgr", [P, KT, 20], SCR)
    bgr = sb("bgr", [P, 20], SCR + 640)
    hf2 = sb("hf2", [P, KT, TX], BIG)
    rt = sb("rt", [P, 16, 4, 16], BIG + 32768)
    cmbT = sb("cmbT", [NEXP, TX], SCR + 1024)
    esel = sb("esel", [NEXP, NEXP, P], SCR + 4096)
    esil = sb("esil", [P, 2, TX], SCR)
    nsq2 = sb("nsq2", [P, 2, TX], BIG + 49152)
    nrm2 = sb("nrm2", [P, 2, TX], BIG + 53248)

    ps = nc.alloc_psum_tensor("ps", [P, 8, 512], F32)
    psf = ps[:, :, :].rearrange("p b n -> p (b n)")

    names = {}

    def sem(*key):
        if key not in names:
            names[key] = nc.alloc_semaphore("_".join(map(str, key)))
        return names[key]

    norms = [(L, n) for L in range(DEPTH) for n in ("premix", "postmix", "preffn", "postffn")]
    norms += [(2, "premix"), (2, "preffn"), (2, "final")]

    def nth(key):
        return norms.index(key)

    def pre_nth(key):
        return [k for k in norms if k[1][:3] == "pre"].index(key)

    def post_nth(key):
        return [k for k in norms if k[1][:4] == "post"].index(key)

    def seg_nth(L, s):
        return 2 * L + s

    def tile_nth(L, s):
        return (0, TX // P, T // P)[seg_nth(L, s)]

    raw = [sem("raw_landed", s) for s in range(RING)]
    hi_split, lo_split, slab_done = sem("hi_split"), sem("lo_split"), sem("slab_done")
    mod_used, acc_free, down_ready = sem("mod_used"), sem("acc_free"), sem("down_ready")
    consts_in = sem("consts_in")
    N_CONST = 9

    def bank2(t):
        return 2 * (t % 3)

    def wh(slot, k):
        return whi[:, slot, k * P:(k + 1) * P]

    def wl(slot, k):
        return wlo[:, slot, k * P:(k + 1) * P]

    segs = {T: [(0, TX, 0), (TX, TC, 1)], TX: [(0, TX, 0)]}

    def in_width(L, s):
        return T if L == 0 or s in (0, 5) else TX

    IN_DST = [PXK, 0, 1, 2, 3, PXV]

    def attn_steps(L):
        st = []
        for j in range(NQT):
            for g in range(2):
                st += [(j, g, q * P, 0, range(6), q == 3) for q in range(4)]
        if L == 0:
            for j in range(NQT):
                for g in range(2):
                    st += [(j, g, TX + q * P, TX, range(4, 6), q == 1) for q in range(2)]
        return st

    hsegs = {0: [(0, 0, 4), (1, TX, 2)], 1: [(0, 0, 4)]}

    blk = ExitStack()
    block = blk.enter_context(nc.Block())

    @block.sync
    def _(sp):
        sp.dma_start(cs[:, :, :], c_d).then_inc(consts_in, 16)
        sp.dma_start(vec[:, :], dram["vec"]).then_inc(consts_in, 16)
        sp.dma_start(bmod[:, :], dram["bmod"]).then_inc(consts_in, 16)
        for t, n in ((ident, "ident"), (headones, "headones"), (rot, "rot"), (consts, "consts")):
            sp.dma_start(t[:, :], dram[n]).then_inc(consts_in, 16)
        sp.dma_start(x[:, :, 0:TX], x_d).then_inc(consts_in, 16)
        sp.dma_start(x[:, :, TX:T], ctx_d).then_inc(consts_in, 16)
        for n in range(RING):
            sp.dma_start(wraw[:, n, :], dram["w_mod"][n, :, :]).then_inc(raw[n], 16)
        with sp.Fori(0, MOD_SLABS // RING - 1) as i:
            for j in range(RING):
                sp.wait_ge(mod_used, RING * i + j + 1)
                sp.dma_start(wraw[:, j, :], dram["w_mod"][RING * i + RING + j, :, :]).then_inc(raw[j], 16)
        for j in range(RING):
            sp.wait_ge(mod_used, MOD_SLABS - RING + j + 1)
            sp.dma_start(wraw[:, j, :], dram["w_all"][j, :, :]).then_inc(raw[j], 16)
        turns, rest = divmod(N_SLABS - RING, RING)
        with sp.Fori(0, turns) as i:
            for j in range(RING):
                sp.wait_ge(lo_split, RING * i + j + 1)
                sp.dma_start(wraw[:, j, :], dram["w_all"][RING * i + RING + j, :, :]).then_inc(raw[j], 16)
        for j in range(rest):
            sp.wait_ge(lo_split, RING * turns + j + 1)
            sp.dma_start(wraw[:, j, :], dram["w_all"][RING * turns + RING + j, :, :]).then_inc(raw[j], 16)
        sp.wait_ge(sem("out_ready"), KT)
        sp.dma_start(out, y[:, :, 0:TX]).then_inc(sem("stored"), 16)
        sp.wait_ge(sem("stored"), 16)

    @block.gpsimd
    def _(pool):
        pool.memset(ones[:, :], 1.0).then_inc(sem("ones_set"), 1)

        def low(n, slot):
            pool.wait_ge(hi_split, n + 1)
            pool.tensor_tensor(wlo[:, slot, :], wraw[:, slot, :], whi[:, slot, :].bitcast(F32),
                               ALU.subtract).then_inc(lo_split, 1)

        with pool.Fori(0, N_SLABS // RING) as i:
            for j in range(RING):
                low(RING * i + j, j)
        for n in range(N_SLABS // RING * RING, N_SLABS):
            low(n, n % RING)

    @block.tensor
    def _(pe):
        pe.wait_ge(consts_in, 16 * N_CONST)
        pe.wait_ge(sem("ones_set"), 1)

        def slab_ready(n):
            pe.wait_ge(lo_split, n + 1)

        def tile(n, t, bank, slot, rhs, width, first=False):
            if not first:
                pe.wait_ge(acc_free, t - 2)
            slab_ready(n)
            for k in range(KT):
                hi, lo = rhs(k)
                passes = [(wh(slot, k), hi), (wh(slot, k), lo), (wl(slot, k), hi)]
                for c0, w, b in segs[width]:
                    for q, (a, r) in enumerate(passes):
                        m = pe.matmul(ps[:, bank + b, 0:w], a, r[:, c0:c0 + w],
                                      start=k == 0 and q == 0, stop=k == KT - 1 and q == 2)
            m.then_inc(slab_done, 1)

        def down(slab0, t0, n0, tt0, rhs, width, ready0):
            for o in range(KT):
                bank = bank2(tt0 + o)
                pe.wait_ge(acc_free, t0 + o - 2)
                for k in range(PAIRS):
                    q = PAIRS * o + k
                    s, b8 = q // KT, q % KT
                    slot = (n0 + s) % RING
                    if b8 == 0:
                        slab_ready(slab0 + s)
                    if o == 0:
                        pe.wait_ge(sem("act_ready"), ready0 + k + 1)
                    hi, lo = rhs(k)
                    passes = [(wh(slot, b8), hi), (wh(slot, b8), lo), (wl(slot, b8), hi)]
                    for c0, w, b in segs[width]:
                        for z, (a, r) in enumerate(passes):
                            m = pe.matmul(ps[:, bank + b, 0:w], a, r[:, c0:c0 + w],
                                          start=k == 0 and z == 0, stop=k == PAIRS - 1 and z == 2)
                    if b8 == KT - 1:
                        m.then_inc(slab_done, 1)
                    elif k == PAIRS - 1:
                        m.then_inc(down_ready, 1)

        def squares(key, width):
            for k in range(KT):
                pe.wait_ge(sem("sq_ready"), KT * nth(key) + k + 1)
                for c0, w, b in segs[width]:
                    m = pe.matmul(ps[:, 6 + b, 0:w], ones[:, :], nsq[:, k % 2, c0:c0 + w],
                                  start=k == 0, stop=k == KT - 1)
                m.then_inc(sem("sq_used"), 1)

        squares((0, "premix"), T)
        pe.wait_ge(sem("c_silu"), 1)
        with pe.Fori(0, MOD_SLABS // (2 * MOD_GROUP)) as i:
            for g in range(2):
                for j in range(MOD_GROUP):
                    n = g * MOD_GROUP + j
                    if j == 0:
                        pe.wait_ge(sem("mod_taken"), 2 * i + g + 1)
                    pe.wait_ge(raw[n % RING], 16 * (2 * MOD_GROUP // RING) * i + 16 * (n // RING + 1))
                    for k in range(KT):
                        m = pe.matmul(ps[:, g, 2 * j:2 * j + 2], wraw[:, n % RING, k * P:(k + 1) * P],
                                      cs[:, k, :], start=k == 0, stop=k == KT - 1)
                    m.then_inc(mod_used, 1)

        def h_rhs(k):
            return hhi[:, k, :], hlo[:, k, :]

        for L in range(DEPTH):
            S0, T0 = L * LAYER_SLABS, L * LAYER_TILES
            if L:
                squares((L, "premix"), T)
            pe.wait_ge(sem("h_ready"), KT * pre_nth((L, "premix")) + KT)
            for s in range(IN_T):
                tile(S0 + s, T0 + s, bank2(T0 + s), (S0 + s) % RING, h_rhs, in_width(L, s), T0 + s < 3)
                if 1 <= s <= 5:
                    j = s - 1
                    pe.wait_ge(sem("qsq_ready", L), j + 1)
                    if j:
                        pe.wait_ge(sem("qstd_ready", L), j)
                    for c0, w, b in segs[in_width(L, j)]:
                        m = pe.matmul(ps[:, 6 + b, 0:w], headones[:, :], qsq[:, c0:c0 + w], start=True, stop=True)
                    m.then_inc(sem("qss_ready", L), 1)
            pe.wait_ge(acc_free, T0 + IN_T)
            for j in range(5):
                pe.wait_ge(sem("qn_ready", L), j + 1)
                pe.matmul(ps[:, j, :], rot[:, :], pxq[:, IN_DST[j], 0:TX], start=True, stop=True)\
                  .then_inc(sem("rot_ready", L), 1)
            fseg = hsegs[L]
            ntt = 6 if L == 0 else 4
            pe.wait_ge(sem("ftab_in", L), 16 * (4 if L == 0 else 3))
            for tt in range(ntt):
                if tt >= 2:
                    pe.wait_ge(sem("fab_ready", L), tt - 1)
                for f in range(2):
                    for ab in range(2):
                        m = pe.matmul(ps[:, 6 + tt % 2, ab * 256 + f * P:ab * 256 + f * P + P],
                                      pxf[:, f, tt * P:tt * P + P], fch[:, ab * P:ab * P + P],
                                      start=True, stop=True)
                m.then_inc(sem("fst1", L), 1)
            pe.wait_ge(sem("fab_ready", L), ntt)
            pe.wait_ge(sem("k_roped", L), 5)
            for f in range(2):
                for s, c0, nt_ in fseg:
                    w = nt_ * P
                    dst = ps[:, 6 + f, 0:w] if s == 0 else ps[:, 5 - f, 0:w]
                    tb = fl5 if s == 0 else fl2
                    for q in range(nt_):
                        for ab in range(2):
                            m = pe.matmul(dst, fab[:, c0 // P + q, ab * 256 + f * P:ab * 256 + f * P + P],
                                          tb[:, ab, q, 0:w], start=q == 0 and ab == 0, stop=q == nt_ - 1 and ab == 1)
                    m.then_inc(sem("fst2", L), 1)
            pe.wait_ge(sem("fy_ready", L), 2 * len(fseg))
            for o in range(2):
                for s, c0, nt_ in fseg:
                    w = nt_ * P
                    dst = ps[:, 6 + o, 0:w] if s == 0 else ps[:, 5 - o, 0:w]
                    for f in range(2):
                        m = pe.matmul(dst, wfo[:, f, o * P:o * P + P], fy[:, f, c0:c0 + w], start=f == 0, stop=f == 1)
                    m.then_inc(sem("fst3", L), 1)
            pe.wait_ge(sem("k_roped", L), 5)
            pe.wait_ge(sem("four_out", L), 2 * len(fseg))
            for tt in range(6):
                m = pe.transpose(ps[:, 4 + tt // 4, (tt % 4) * P:(tt % 4) * P + P], pxq[:, PXV, tt * P:tt * P + P],
                                 ident[:, :])
            m.then_inc(sem("vt_done", L), 1)
            steps = attn_steps(L)
            N = len(steps)
            heads = 0
            for i in range(N + 2):
                if i < N:
                    j, g, q0, k0, kts, last = steps[i]
                    h = slice(64 * g, 64 * g + 64)
                    if i >= 2:
                        pe.wait_ge(sem("exp_done", L), i - 1)
                    nk = len(kts) * P
                    for c in range(0, nk, 512):
                        w = min(512, nk - c)
                        m = pe.matmul(ps[:, 2 * (i % 2) + c // 512, 0:w], pxq[h, j, q0:q0 + P],
                                      pxq[h, PXK, k0 + c:k0 + c + w], start=True, stop=True)
                    m.then_inc(sem("s_ready", L), 1)
                if 1 <= i <= N:
                    kts = steps[i - 1][4]
                    pe.wait_ge(sem("p_ready", L), i)
                    pe.wait_ge(sem("pta", L), i)
                    pe.wait_ge(sem("ptb", L), i)
                    for c in range(len(kts)):
                        m = pe.transpose(ps[:, 4 + c // 4, (c % 4) * P:(c % 4) * P + P],
                                         pr[:, (i - 1) % 2, c * P:c * P + P], ident[:, :])
                    m.then_inc(sem("t_ready", L), 1)
                if i >= 2 and steps[i - 2][5]:
                    j, g, q0, k0, kts, last = steps[i - 2]
                    nq = TX if k0 == 0 else TC
                    ht = heads // 2
                    if ht >= 2:
                        pe.wait_ge(sem("attn_out", L), ht - 1)
                    pe.wait_ge(sem("pta", L), i)
                    pe.wait_ge(sem("ptb", L), i)
                    for c, kt in enumerate(kts):
                        m = pe.matmul(ps[64 * g:64 * g + 64, 6 + ht % 2, 0:nq], vt[:, kt, 64 * g:64 * g + 64],
                                      pt[:, heads % 2, c, 0:nq], start=c == 0, stop=c == len(kts) - 1)
                    m.then_inc(sem("o_ready", L), 1)
                    heads += 1
            pe.wait_ge(sem("attn_out", L), heads // 2)
            pe.wait_ge(sem("u_ready", L), 1)
            for tt in range(ntt):
                if tt >= 2:
                    pe.wait_ge(sem("ut_ready", L), tt - 1)
                for c in range(2):
                    m = pe.transpose(ps[:, tt % 2, c * P:c * P + P], pxh[:, 2 + c, tt * P:tt * P + P], ident[:, :])
                m.then_inc(sem("ut_done", L), 1)
            for s, c0, nt_ in hsegs[L]:
                w = nt_ * P
                K = (L, s)
                pe.wait_ge(sem("hfil_in", L), 16 * (5 + s))
                pe.wait_ge(sem("ut_ready", L), ntt)
                pe.matmul(ps[0:64, 2, 0:w], hw12[0:33, 0:64], hz[0:33, 0:w], start=True, stop=True)\
                  .then_inc(sem("h1_ready"), 1)
                pe.wait_ge(sem("h1_sin"), seg_nth(*K) + 1)
                pe.matmul(ps[0:64, 3, 0:w], hw12[0:64, 64:128], hl[0:64, 0, 0:w], start=True, stop=True)\
                  .then_inc(sem("h2_ready"), 1)
                pe.wait_ge(sem("h2_sin"), seg_nth(*K) + 1)
                for q in range(nt_):
                    if q >= 2:
                        pe.wait_ge(sem("hf_taken"), tile_nth(*K) + q - 1)
                    pe.matmul(ps[:, q % 2, :], hl[0:64, 1, q * P:q * P + P], hw3[0:64, :], start=True, stop=True)\
                      .then_inc(sem("hf_ready"), 1)
                pe.wait_ge(sem("hsum_ready"), seg_nth(*K) + 1)
                for c in range(2):
                    m = pe.matmul(ps[:, 2, c:c + 1], hsum[:, c * P:c * P + P], ones[:, 0:1], start=True, stop=True)
                m.then_inc(sem("hn_ready"), 1)
                fwd = hd5 if s == 0 else hd2
                pe.wait_ge(sem("hfwd_in", L), 16)
                if s == 1:
                    pe.wait_ge(sem("hd2_in", L), 16)
                for f in range(nt_):
                    if f >= 2:
                        pe.wait_ge(sem("hys_ready"), tile_nth(*K) + f - 1)
                    for cs_ in range(2):
                        for q in range(nt_):
                            m = pe.matmul(ps[:, 4 + f % 2, cs_ * 256:cs_ * 256 + 256],
                                          fwd[:, cs_, q, f * P:f * P + P], hpm[:, q, cs_ * 256:cs_ * 256 + 256],
                                          start=q == 0, stop=q == nt_ - 1)
                    m.then_inc(sem("hk_ready"), 1)
                    for cs_ in range(2):
                        for q in range(nt_):
                            m = pe.matmul(ps[:, 6 + f % 2, cs_ * 256:cs_ * 256 + 256],
                                          fwd[:, cs_, q, f * P:f * P + P], hut[:, c0 // P + q, :],
                                          start=q == 0, stop=q == nt_ - 1)
                    m.then_inc(sem("hu_ready"), 1)
                pe.wait_ge(sem("hys_ready"), tile_nth(*K) + nt_)
                pe.wait_ge(sem("hinv_in", L), 16)
                for c in range(2):
                    for f in range(nt_):
                        for cs_ in range(2):
                            iv = hi5[:, cs_, f, 0:w] if s == 0 else hd2[:, 2 + cs_, f, 0:w]
                            m = pe.matmul(ps[:, c, 0:w], hys[:, f, cs_ * 256 + c * P:cs_ * 256 + c * P + P], iv,
                                          start=f == 0 and cs_ == 0, stop=f == nt_ - 1 and cs_ == 1)
                    m.then_inc(sem("hy_ready"), 1)
                pe.wait_ge(sem("hy_out", L), 2 * (s + 1))
            W = T if L == 0 else TX
            for s in range(OUT_T):
                tile(S0 + IN_T + s, T0 + IN_T + s, bank2(T0 + IN_T + s), (S0 + IN_T + s) % RING, h_rhs, W)
            squares((L, "postmix"), W)
            squares((L, "preffn"), W)
            pe.wait_ge(sem("h_ready"), KT * pre_nth((L, "preffn")) + KT)
            F0, G0 = S0 + IN_T + OUT_T, T0 + IN_T + OUT_T
            with pe.Fori(0, CHUNKS) as i:
                for s in range(UP_T):
                    tile(i * FFN_SLABS + (F0 + s), i * FFN_TILES + (G0 + s), bank2(G0 + s), (F0 + s) % RING, h_rhs, W)
                down(i * FFN_SLABS + (F0 + UP_T), i * FFN_TILES + (G0 + UP_T), F0 + UP_T, G0 + UP_T,
                     lambda k: (ahi[:, k, :], alo[:, k, :]), W, i * PAIRS + L * CHUNKS * PAIRS)
            squares((L, "postffn"), W)

        squares((2, "premix"), TX)
        pe.wait_ge(sem("h_ready"), KT * pre_nth((2, "premix")) + KT)
        for s in range(IN2_T):
            tile(B2_SLAB + s, B2_TILE + s, bank2(B2_TILE + s), (B2_SLAB + s) % RING, h_rhs, TX)
        pe.wait_ge(acc_free, B2_TILE + IN2_T)
        N = 4 * NH2
        for i in range(N + 2):
            if i < N:
                h, q = i // 4, i % 4
                a, hh = h // 8, h % 8
                qt, half = 12 * a + hh // 2, slice(64 * (hh % 2), 64 * (hh % 2) + 64)
                if i % 8 == 0:
                    if i:
                        pe.wait_ge(sem("vt2_ready"), i // 8)
                    for tt in range(4):
                        m = pe.transpose(ps[:, 4, tt * P:tt * P + P], px2[:, qt + 8, tt * P:tt * P + P], ident[:, :])
                    m.then_inc(sem("vt2_done"), 1)
                if i >= 2:
                    pe.wait_ge(sem("s2_ready"), i - 1)
                pe.matmul(ps[:, i % 2, :], px2[half, qt, q * P:q * P + P], px2[half, qt + 4, :],
                          start=True, stop=True).then_inc(sem("s2_done"), 1)
            if 1 <= i <= N:
                pe.wait_ge(sem("p2_ready"), i)
                if i >= 3:
                    pe.wait_ge(sem("pt2_ready"), i - 2)
                for c in range(4):
                    m = pe.transpose(ps[:, 2 + (i - 1) % 2, c * P:c * P + P], p2[:, (i - 1) % 2, c * P:c * P + P],
                                     ident[:, :])
                m.then_inc(sem("t2_done"), 1)
            if i >= 2 and (i - 2) % 4 == 3:
                h = (i - 2) // 4
                g, tl = h % 2, h // 2
                pe.wait_ge(sem("pt2_ready"), i - 1)
                pe.wait_ge(sem("vt2_ready"), tl + 1)
                if tl >= 2 and g == 0:
                    pe.wait_ge(sem("o2_out"), tl - 1)
                for c in range(4):
                    m = pe.matmul(ps[64 * g:64 * g + 64, 6 + tl % 2, :], vt2[:, tl % 2, c, 64 * g:64 * g + 64],
                                  pt2[:, h % 2, c, :], start=c == 0, stop=c == 3)
                m.then_inc(sem("o2_done"), 1)
        for a in range(2):
            pe.wait_ge(sem("o2_out"), 8)
            for k in range(4):
                pe.wait_ge(sem("osq_ready"), 4 * a + k + 1)
                pe.matmul(ps[:, 4 + a, :], ones[:, :], nsq2[:, k % 2, :], start=k == 0, stop=k == 3)\
                  .then_inc(sem("osq_used"), 1)
        pe.wait_ge(sem("out_h_ready"), KT)
        for s in range(OUT_T):
            n, t = B2_SLAB + IN2_T + s, B2_TILE + IN2_T + s
            tile(n, t, bank2(t), n % RING, h_rhs, TX)
        squares((2, "preffn"), TX)
        pe.wait_ge(sem("h_ready"), KT * pre_nth((2, "preffn")) + KT)
        pe.wait_ge(sem("router_in"), 48)
        for tt in range(4):
            for k in range(KT):
                m = pe.matmul(ps[:, 7, tt * 32:tt * 32 + 20], hf2[:, k, tt * P:tt * P + P], wgr[:, k, :],
                              start=k == 0, stop=k == KT - 1)
        m.then_inc(sem("logits_done"), 1)
        pe.wait_ge(sem("comb_tok"), 1)
        for tt in range(4):
            m = pe.transpose(ps[0:16, 6, tt * P:tt * P + P], rt[:, 0, tt, :], ident[:, :])
        m.then_inc(sem("combT_done"), 1)
        pe.wait_ge(sem("combT_ready"), 1)
        for e in range(NEXP):
            if e >= 2:
                pe.wait_ge(sem("comb_ready"), e - 1)
            pe.matmul(ps[:, 6 + e % 2, :], esel[:, e, :], cmbT[:, :], start=True, stop=True)\
              .then_inc(sem("comb_done"), 1)
        E0, G0 = B2_SLAB + IN2_T + OUT_T, B2_TILE + IN2_T + OUT_T
        with pe.Fori(0, MOE_TURNS) as i:
            for s in range(MOE_UP):
                tile(i * MOE_SLABS + (E0 + s), i * MOE_SLABS + (G0 + s), bank2(G0 + s), (E0 + s) % RING, h_rhs, TX)
            pe.wait_ge(sem("eact_ready"), 2 * EPI * i + 2 * EPI)
            for o in range(KT):
                s = MOE_UP + o
                tile(i * MOE_SLABS + (E0 + s), i * MOE_SLABS + (G0 + s), bank2(G0 + s), (E0 + s) % RING,
                     lambda k: (ehi[:, k, :], elo[:, k, :]), TX)
        squares((2, "final"), TX)

    @block.scalar
    def _(act):
        def whi_split(n_expr, n_mod, landed, first=False):
            act.wait_ge(raw[n_mod], landed)
            if not first:
                act.wait_ge(slab_done, n_expr - 2)
            act.activation(whi[:, n_mod, :], wraw[:, n_mod, :], ACT.Copy).then_inc(hi_split, 1)

        RAW0 = MOD_SLABS // RING

        def split(n):
            if n < N_SLABS:
                whi_split(n, n % RING, 16 * (RAW0 + n // RING + 1), n < RING)

        def split_in(i, per, n):
            whi_split(i * per + n, n % RING, i * (16 * per // RING) + 16 * (RAW0 + n // RING + 1))

        def norm_stats(key, src, width):
            for k in range(KT):
                if k >= 2:
                    act.wait_ge(sem("sq_used"), KT * nth(key) + k - 1)
                act.activation(nsq[:, k % 2, 0:width], src[:, k, 0:width], ACT.Square)\
                   .then_inc(sem("sq_ready"), 1)
            act.wait_ge(sem("sq_used"), KT * nth(key) + KT)
            act.activation(nrm[:, 0:width], psf[:, 3072:3072 + width], ACT.Sqrt, bias=eps_c, scale=1.0 / D)\
               .then_inc(sem("std_ready"), 1)

        def norm_apply(key, width, afn, bfn):
            for k in range(KT):
                act.wait_ge(sem("scaled_ready"), KT * pre_nth(key) + k + 1)
                if k >= 2:
                    act.wait_ge(sem("h_ready"), KT * pre_nth(key) + k - 1)
                for c0, w, b in segs[width]:
                    act.activation(nfull[:, k % 2, c0:c0 + w], nt[:, k % 2, c0:c0 + w], ACT.Identity,
                                   bias=bfn(k, b), scale=afn(k, b))
                for c0, w, b in segs[width]:
                    m = act.activation(hhi[:, k, c0:c0 + w], nt[:, k % 2, c0:c0 + w], ACT.Identity,
                                       bias=bfn(k, b), scale=afn(k, b))
                m.then_inc(sem("full_ready"), 1)

        act.wait_ge(consts_in, 16 * N_CONST)
        act.activation(cs[:, :, :], cs[:, :, :], ACT.Silu).then_inc(sem("c_silu"), 1)
        norm_stats((0, "premix"), x, T)
        for n in range(RING):
            split(n)

        def mods(L, a, b):
            return (lambda k, s: mv[:, L, a, k, s:s + 1]), (lambda k, s: mod[:, L, b * KT + k, s:s + 1])

        for L in range(DEPTH):
            S0, T0 = L * LAYER_SLABS, L * LAYER_TILES
            if L == 0:
                act.wait_ge(sem("mv_ready"), 1)
            else:
                act.wait_ge(sem("x_ready"), KT * post_nth((L - 1, "postffn")) + KT)
                norm_stats((L, "premix"), x, T)
            norm_apply((L, "premix"), T, *mods(L, 0, 0))
            act.wait_ge(sem("h_ready"), KT * pre_nth((L, "premix")) + KT)
            act.dma_start(cosx[:, :, :], dram["rope"]).then_inc(sem("rope_in", L), 16)
            act.dma_start(fl5[:, :, :, :], dram["four512"]).then_inc(sem("ftab_in", L), 16)
            act.dma_start(wfo[:, :, :], dram["w_four"][L]).then_inc(sem("ftab_in", L), 16)
            act.dma_start(fch[:, :], dram["fourch"]).then_inc(sem("ftab_in", L), 16)
            if L == 0:
                act.dma_start(fl2[:, :, :, :], dram["four256"]).then_inc(sem("ftab_in", L), 16)

            def head_std(j):
                w = in_width(L, j)
                act.wait_ge(sem("qss_ready", L), j + 1)
                if j >= 2:
                    act.wait_ge(sem("qn_ready", L), j - 1)
                act.activation(qrs[:, j % 2, 0:w], psf[:, 3072:3072 + w], ACT.Sqrt, bias=eps_c, scale=1.0 / HD)\
                   .then_inc(sem("qstd_ready", L), 1)

            for s in range(IN_T):
                w, b = in_width(L, s), bank2(T0 + s)
                act.wait_ge(slab_done, S0 + s + 1)
                src = psf[:, b * 512:b * 512 + w]
                if s < 6:
                    if s < 5:
                        if s >= 1:
                            act.wait_ge(sem("qss_ready", L), s)
                        act.activation(qsq[:, 0:w], src, ACT.Square).then_inc(sem("qsq_ready", L), 1)
                    act.activation(pxq[:, IN_DST[s], 0:w], src, ACT.Copy).then_inc(acc_free, 1)
                elif s < 8:
                    act.activation(pxf[:, s - 6, 0:w], src, ACT.Copy).then_inc(acc_free, 1)
                else:
                    t = s - 8
                    v = V_HYC + L * V_LAYER + 4 * t
                    act.activation(pxh[:, t, 0:w], src, ACT.Identity, bias=vec[:, v + 3:v + 4],
                                   scale=vec[:, v + 1:v + 2]).then_inc(sem("hyc_mid", L), 1)
                split(S0 + s + RING)
                if 1 <= s <= 5:
                    head_std(s - 1)
            fseg = hsegs[L]
            ntt = 6 if L == 0 else 4
            for tt in range(ntt):
                act.wait_ge(sem("fst1", L), tt + 1)
                act.activation(fab[:, tt, :], ps[:, 6 + tt % 2, :], ACT.Copy).then_inc(sem("fab_ready", L), 1)
            n = 0
            for f in range(2):
                for s, c0, nt_ in fseg:
                    n += 1
                    w = nt_ * P
                    act.wait_ge(sem("fst2", L), n)
                    act.activation(fy[:, f, c0:c0 + w], ps[:, 6 + f, 0:w] if s == 0 else ps[:, 5 - f, 0:w],
                                   ACT.Copy).then_inc(sem("fy_ready", L), 1)
            n = 0
            for o in range(2):
                for s, c0, nt_ in fseg:
                    n += 1
                    w = nt_ * P
                    act.wait_ge(sem("fst3", L), n)
                    act.activation(hhi[:, 4 + o, c0:c0 + w], ps[:, 6 + o, 0:w] if s == 0 else ps[:, 5 - o, 0:w],
                                   ACT.Copy).then_inc(sem("four_hi", L), 1)
            act.wait_ge(sem("k_roped", L), 5)
            act.dma_start(hd5[:, :, :, :], dram["hyf512"]).then_inc(sem("hfwd_in", L), 16)
            act.dma_start(hw3[0:64, :], dram["hy_w3"][L]).then_inc(sem("hfil_in", L), 16)
            act.dma_start(hw12[0:33, 0:64], dram["hy_w1"][L]).then_inc(sem("hfil_in", L), 16)
            act.dma_start(hw12[0:64, 64:128], dram["hy_w2"][L]).then_inc(sem("hfil_in", L), 16)
            act.dma_start(hdel[:, :], dram["deltas"]).then_inc(sem("hfil_in", L), 16)
            act.dma_start(hz[0:33, :], dram["z512"]).then_inc(sem("hfil_in", L), 16)
            act.wait_ge(sem("vt_done", L), 1)
            act.activation(vt[:, :, :].rearrange("p a b -> p (a b)"), psf[:, 2048:2048 + 768], ACT.Copy)\
               .then_inc(sem("pta", L), 1)
            steps = attn_steps(L)
            N = len(steps)
            heads = 0
            for i in range(N + 2):
                if i < N:
                    nk = len(steps[i][4]) * P
                    act.wait_ge(sem("max_ready", L), i + 1)
                    if i >= 2:
                        act.wait_ge(sem("t_ready", L), i - 1)
                    act.activation(pr[:, i % 2, 0:nk], psf[:, 1024 * (i % 2):1024 * (i % 2) + nk], ACT.Exp,
                                   bias=stat[:, i % 2, 0:1], scale=SCALE, accum_out=stat[:, i % 2, 1:2])\
                       .then_inc(sem("exp_done", L), 1)
                if 1 <= i <= N:
                    j, g, q0, k0, kts, last = steps[i - 1]
                    act.wait_ge(sem("t_ready", L), i)
                    if heads >= 2:
                        act.wait_ge(sem("o_ready", L), heads - 1)
                    c = min(4, len(kts))
                    act.activation(pt[:, heads % 2, 0:c, q0 - k0:q0 - k0 + P],
                                   ps[:, 4, 0:c * P].rearrange("p (c n) -> p c n", c=c), ACT.Copy)\
                       .then_inc(sem("pta", L), 1)
                    if last:
                        heads += 1
                if i >= 2 and steps[i - 2][5] and steps[i - 2][1] == 1:
                    j, g, q0, k0, kts, last = steps[i - 2]
                    nq = TX if k0 == 0 else TC
                    ht = j + (NQT if k0 else 0)
                    act.wait_ge(sem("o_ready", L), 2 * ht + 2)
                    act.activation(hhi[:, j, k0:k0 + nq], ps[:, 6 + ht % 2, 0:nq], ACT.Copy)\
                       .then_inc(sem("attn_hi", L), 1)
            nht = NQT * (2 if L == 0 else 1)
            act.wait_ge(sem("attn_out", L), nht)
            act.dma_start(hi5[:, :, :, :], dram["hyi512"]).then_inc(sem("hinv_in", L), 16)
            if L == 0:
                act.dma_start(hd2[:, :, :, :], dram["hy256"]).then_inc(sem("hd2_in", L), 16)
            for tt in range(ntt):
                act.wait_ge(sem("ut_done", L), tt + 1)
                act.activation(hut[:, tt, :], ps[:, tt % 2, 0:256], ACT.Copy).then_inc(sem("ut_ready", L), 1)
            for s, c0, nt_ in hsegs[L]:
                w = nt_ * P
                K = (L, s)
                if s == 1:
                    act.wait_ge(sem("h1_ready"), seg_nth(L, 0) + 1)
                    act.dma_start(hz[0:33, 0:TC], dram["z256"]).then_inc(sem("hfil_in", L), 16)
                for r in range(2):
                    act.wait_ge(sem("harg"), 2 * seg_nth(*K) + r + 1)
                    act.activation(hl[0:64, r, 0:w], hb[0:64, 0:w], ACT.Sin)\
                       .then_inc(sem("h1_sin" if r == 0 else "h2_sin"), 1)
                for q in range(nt_):
                    if q >= 1:
                        act.wait_ge(sem("hf_taken"), tile_nth(*K) + q)
                    act.activation(ha[:, 0:256], hdel[:, :], ACT.Exp, scale=consts[:, 2 + c0 // P + q:3 + c0 // P + q])\
                       .then_inc(sem("dec_ready"), 1)
                for f in range(nt_):
                    act.wait_ge(sem("hk_ready"), tile_nth(*K) + f + 1)
                    act.activation(hsp[:, f, :], ps[:, 4 + f % 2, :], ACT.Copy).then_inc(sem("hsp_ready"), 1)
                for c in range(2):
                    act.wait_ge(sem("hyf"), 2 * seg_nth(*K) + c + 1)
                    act.activation(hhi[:, 6 + c, c0:c0 + w], hub[:, c, c0:c0 + w], ACT.Copy)\
                       .then_inc(sem("hy_hi"), 1)
            W = T if L == 0 else TX
            for s in range(OUT_T):
                act.wait_ge(slab_done, S0 + IN_T + s + 1)
                b = bank2(T0 + IN_T + s)
                act.activation(y[:, s, 0:W], psf[:, b * 512:b * 512 + W], ACT.Copy).then_inc(acc_free, 1)
                split(S0 + IN_T + s + RING)
            act.drain()
            norm_stats((L, "postmix"), y, W)
            act.wait_ge(sem("x_ready"), KT * post_nth((L, "postmix")) + KT)
            norm_stats((L, "preffn"), x, W)
            norm_apply((L, "preffn"), W, *mods(L, 2, 3))
            F0, G0 = S0 + IN_T + OUT_T, T0 + IN_T + OUT_T
            with act.Fori(0, CHUNKS) as i:
                act.wait_ge(sem("cconv_ready"), i + (L * CHUNKS + 1))
                for p in range(PAIRS):
                    for z in range(2):
                        s = 2 * p + z
                        b = bank2(G0 + s)
                        act.wait_ge(slab_done, i * FFN_SLABS + (F0 + s + 1))
                        act.activation(up[:, p % 2, z, 0:W], psf[:, b * 512:b * 512 + W], ACT.Identity,
                                       bias=cconv[:, s, 3:4], scale=cconv[:, s, 1:2]).then_inc(sem("up_mid"), 1)
                        split_in(i, FFN_SLABS, F0 + s + RING)
                    act.wait_ge(sem("gate_ready"), i * PAIRS + (L * CHUNKS * PAIRS + p + 1))
                    if p:
                        act.wait_ge(sem("act_ready"), i * PAIRS + (L * CHUNKS * PAIRS + p))
                    elif L:
                        act.wait_ge(sem("act_ready"), i * PAIRS + (L * CHUNKS * PAIRS))
                    act.activation(sil[:, 0:W], up[:, p % 2, 0, 0:W], ACT.Silu).then_inc(sem("silu_done"), 1)
                    act.wait_ge(sem("prod_ready"), i * PAIRS + (L * CHUNKS * PAIRS + p + 1))
                    act.activation(ahi[:, p, 0:W], sil[:, 0:W], ACT.Copy).then_inc(sem("ahi_ready"), 1)
                for o in range(KT):
                    for q in range(PAIRS * o // KT, PAIRS * (o + 1) // KT):
                        split_in(i, FFN_SLABS, F0 + UP_T + q + RING)
            act.wait_ge(acc_free, G0 + CHUNKS * FFN_TILES)
            norm_stats((L, "postffn"), y, W)

        act.wait_ge(sem("x_ready"), KT * post_nth((1, "postffn")) + KT)
        g2 = lambda v: ((lambda k, s: vec[:, v + k:v + k + 1]), (lambda k, s: zero_c))
        norm_stats((2, "premix"), x, TX)
        norm_apply((2, "premix"), TX, *g2(V2_MIX))
        act.wait_ge(sem("h_ready"), KT * pre_nth((2, "premix")) + KT)
        act.dma_start(namask[:, :], dram["namask"]).then_inc(sem("namask_in"), 16)

        def load_table(h):
            if h >= 2:
                act.wait_ge(sem("s2_ready"), 4 * (h - 1))
            for a in range(2):
                half = slice(64 * a, 64 * a + 64)
                src = dram["alibi"][h, half, :] if h < 8 else dram["rpbw"][h - 8, :, (1 - a) * HD:(15 - a) * HD]
                act.dma_start(tab[half, h % 2, :], src).then_inc(sem("tab_in", h % 2), 16)

        load_table(0)
        load_table(1)
        for s in range(IN2_T):
            n, t = B2_SLAB + s, B2_TILE + s
            act.wait_ge(slab_done, n + 1)
            act.activation(px2[:, s, :], ps[:, bank2(t), :], ACT.Copy).then_inc(acc_free, 1)
            split(n + RING)
        N = 4 * NH2
        for i in range(N + 2):
            if i < N:
                if i % 8 == 0:
                    act.wait_ge(sem("vt2_done"), i // 8 + 1)
                    if i >= 16:
                        act.wait_ge(sem("o2_done"), 2 * (i // 8 - 1))
                    act.activation(vt2[:, (i // 8) % 2, :, :].rearrange("p a b -> p (a b)"), ps[:, 4, :], ACT.Copy)\
                       .then_inc(sem("vt2_ready"), 1)
                act.wait_ge(sem("max2_ready"), i + 1)
                if i >= 2:
                    act.wait_ge(sem("t2_done"), i - 1)
                act.activation(p2[:, i % 2, :], s2[:, i % 2, :], ACT.Exp, bias=stat[:, i % 2, 0:1],
                               accum_out=stat[:, i % 2, 1:2]).then_inc(sem("exp2_done"), 1)
            if 1 <= i <= N:
                h = (i - 1) // 4
                act.wait_ge(sem("t2_done"), i)
                if h >= 2:
                    act.wait_ge(sem("o2_done"), h - 1)
                q = (i - 1) % 4
                act.activation(pt2[:, h % 2, :, q * P:q * P + P],
                               ps[:, 2 + (i - 1) % 2, :].rearrange("p (c n) -> p c n", c=4), ACT.Copy)\
                   .then_inc(sem("pt2_ready"), 1)
                if q == 3 and h + 2 < NH2:
                    load_table(h + 2)
            if i >= 2 and (i - 2) % 8 == 7:
                tl = (i - 2) // 8
                act.wait_ge(sem("o2_done"), 2 * tl + 2)
                act.activation(px2[:, 12 * (tl // 4) + tl % 4, :], ps[:, 6 + tl % 2, :], ACT.Copy)\
                   .then_inc(sem("o2_out"), 1)
        act.wait_ge(sem("o2_out"), 8)
        for a in range(2):
            for k in range(4):
                q = 4 * a + k
                if q >= 2:
                    act.wait_ge(sem("osq_used"), q - 1)
                act.activation(nsq2[:, k % 2, :], px2[:, 12 * a + k, :], ACT.Square).then_inc(sem("osq_ready"), 1)
            act.wait_ge(sem("osq_used"), 4 * a + 4)
            act.activation(nrm2[:, a, :], ps[:, 4 + a, :], ACT.Sqrt, bias=eps_c, scale=1.0 / 512)\
               .then_inc(sem("ostd_ready"), 1)
        for k in range(KT):
            a = k // 4
            act.wait_ge(sem("ot_ready"), k + 1)
            src = px2[:, 12 * a + k % 4, :]
            act.activation(hhi[:, k, 0:TX], src, ACT.Copy).then_inc(sem("ohi_ready"), 1)
        for s in range(OUT_T):
            n, t = B2_SLAB + IN2_T + s, B2_TILE + IN2_T + s
            act.wait_ge(slab_done, n + 1)
            split(n + RING)
        act.wait_ge(sem("x2_ready"), 1)
        act.dma_start(wgr[:, :, :], dram["wgr"]).then_inc(sem("router_in"), 16)
        act.dma_start(bgr[:, :], dram["bgr"]).then_inc(sem("router_in"), 16)
        act.dma_start(esel[:, :, :], dram["esel"]).then_inc(sem("router_in"), 16)
        key = (2, "preffn")
        for k in range(KT):
            if k >= 2:
                act.wait_ge(sem("sq_used"), KT * nth(key) + k - 1)
            act.activation(nsq[:, k % 2, 0:TX], x[:, k, 0:TX], ACT.Square).then_inc(sem("sq_ready"), 1)
        act.wait_ge(sem("sq_used"), KT * nth(key) + KT)
        act.activation(nrm[:, 0:TX], ps[:, 6, :], ACT.Sqrt, bias=eps_c, scale=1.0 / D)\
           .then_inc(sem("std_ready"), 1)
        for k in range(KT):
            act.wait_ge(sem("scaled_ready"), KT * pre_nth(key) + k + 1)
            act.activation(hhi[:, k, 0:TX], hf2[:, k, :], ACT.Copy).then_inc(sem("full_ready"), 1)
        act.wait_ge(sem("g_ready"), 1)
        act.activation(rt[:, 3, :, 0:4], rt[:, 2, :, 0:4], ACT.Exp).then_inc(sem("g_exp"), 1)
        act.wait_ge(sem("e_ready"), 1)
        act.activation(rt[:, 9, :, 0:1], rt[:, 8, :, 0:1], ACT.Exp).then_inc(sem("e_exp"), 1)
        act.wait_ge(sem("combT_done"), 1)
        act.activation(cmbT[:, :], ps[0:16, 6, :], ACT.Copy).then_inc(sem("combT_ready"), 1)
        for e in range(NEXP):
            act.wait_ge(sem("comb_done"), e + 1)
            act.activation(comb[:, e, :], ps[:, 6 + e % 2, :], ACT.Copy).then_inc(sem("comb_ready"), 1)
        E0, G0 = B2_SLAB + IN2_T + OUT_T, B2_TILE + IN2_T + OUT_T

        def moe_turn(i, last):
            for p in range(2 * EPI):
                act.wait_ge(slab_done, i * MOE_SLABS + (E0 + 2 * p + 1))
                b = bank2(G0 + 2 * p)
                if p >= 2:
                    act.wait_ge(sem("eact_ready"), i * (2 * EPI) + (p - 1))
                act.activation(esil[:, p % 2, :], ps[:, b, :], ACT.Silu).then_inc(sem("esil_ready"), 1)
                split_in(i, MOE_SLABS, E0 + 2 * p + RING)
                split_in(i, MOE_SLABS, E0 + 2 * p + 1 + RING)
                act.wait_ge(sem("eprod_ready"), i * (2 * EPI) + (p + 1))
                act.activation(ehi[:, p, :], esil[:, p % 2, :], ACT.Copy).then_inc(sem("ehi_ready"), 1)
            for o in range(KT):
                if last and o + RING >= KT:
                    continue
                split_in(i, MOE_SLABS, E0 + MOE_UP + o + RING)

        with act.Fori(0, MOE_TURNS - 1) as i:
            moe_turn(i, False)
        moe_turn(MOE_TURNS - 1, True)
        act.wait_ge(sem("moe_done"), 1)
        norm_stats((2, "final"), x, TX)

    @block.vector
    def _(dve):
        def norm_dve(key, src, width, lo_from_full=True):
            dve.wait_ge(sem("std_ready"), nth(key) + 1)
            dve.reciprocal(nrm[:, 0:width], nrm[:, 0:width])
            dve.drain()
            for k in range(KT + 1):
                if k < KT:
                    if k >= 2:
                        dve.wait_ge(sem("full_ready"), KT * pre_nth(key) + k - 1)
                    dve.tensor_tensor(nt[:, k % 2, 0:width], src[:, k, 0:width], nrm[:, 0:width], ALU.mult)\
                       .then_inc(sem("scaled_ready"), 1)
                if k >= 1:
                    dve.wait_ge(sem("full_ready"), KT * pre_nth(key) + k)
                    dve.tensor_tensor(hlo[:, k - 1, 0:width], nfull[:, (k - 1) % 2, 0:width],
                                      hhi[:, k - 1, 0:width].bitcast(F32), ALU.subtract)\
                       .then_inc(sem("h_ready"), 1)

        def post_norm(key, L, gate, width):
            dve.wait_ge(sem("std_ready"), nth(key) + 1)
            dve.reciprocal(nrm[:, 0:width], nrm[:, 0:width])
            dve.drain()
            for k in range(KT):
                dve.tensor_tensor(y[:, k, 0:width], y[:, k, 0:width], nrm[:, 0:width], ALU.mult)
            dve.drain()
            for k in range(KT):
                for c0, w, b in segs[width]:
                    m = dve.scalar_tensor_tensor(x[:, k, c0:c0 + w], y[:, k, c0:c0 + w], mv[:, L, gate, k, b:b + 1],
                                                 x[:, k, c0:c0 + w], ALU.mult, ALU.add)
                m.then_inc(sem("x_ready"), 1)

        def shifts(dst, bank, width, w0, w2):
            for c0, w, b in segs[width]:
                dve.scalar_tensor_tensor(dst[:, c0 + 1:c0 + w], ps[:, bank + b, 0:w - 1], w0, dst[:, c0 + 1:c0 + w],
                                         ALU.mult, ALU.add)
            dve.drain()
            for c0, w, b in segs[width]:
                m = dve.scalar_tensor_tensor(dst[:, c0:c0 + w - 1], ps[:, bank + b, 1:w], w2, dst[:, c0:c0 + w - 1],
                                             ALU.mult, ALU.add)
            return m

        modf = mod[:, :, :, :].rearrange("p l t s -> p (l t s)")
        dve.wait_ge(consts_in, 16 * N_CONST)
        dve.memset(stat[:, :, :], 0.0).then_inc(sem("mod_taken"), 2)
        GW = 2 * MOD_GROUP
        with dve.Fori(0, MOD_SLABS // GW) as i:
            for g in range(2):
                dve.wait_ge(mod_used, GW * i + MOD_GROUP * (g + 1))
                part = bass.ds(2 * GW * i + g * GW, GW)
                dve.tensor_tensor(modf[:, part], ps[:, g, 0:GW], bmod[:, part], ALU.add).then_inc(sem("mod_taken"), 1)
        dve.drain()
        for L in range(DEPTH):
            for s in range(2):
                for q, (g, mt, plus) in enumerate(((V_GPM, 1, 1.0), (V_GQM, 2, 0.0), (V_GPF, 4, 1.0), (V_GQF, 5, 0.0))):
                    g += L * V_LAYER
                    m = dve.scalar_tensor_tensor(mv[:, L, q, :, s], mod[:, L, mt * KT:(mt + 1) * KT, s], plus,
                                                 vec[:, g:g + KT], ALU.add, ALU.mult)
        m.then_inc(sem("mv_ready"), 1)

        for L in range(DEPTH):
            S0, T0 = L * LAYER_SLABS, L * LAYER_TILES
            V0 = L * V_LAYER
            norm_dve((L, "premix"), x, T)

            def head_norm(j):
                w = in_width(L, j)
                dve.wait_ge(sem("qstd_ready", L), j + 1)
                dve.reciprocal(qrs[:, j % 2, 0:w], qrs[:, j % 2, 0:w])
                dve.drain()
                g = V0 + (V_GK if j == 0 else V_GQ)
                dve.scalar_tensor_tensor(pxq[:, IN_DST[j], 0:w], pxq[:, IN_DST[j], 0:w], vec[:, g:g + 1],
                                         qrs[:, j % 2, 0:w], ALU.mult, ALU.mult).then_inc(sem("qn_ready", L), 1)

            for j in range(5):
                head_norm(j)
            for s in range(8, IN_T):
                t = s - 8
                v = V0 + V_HYC + 4 * t
                dve.wait_ge(sem("hyc_mid", L), t + 1)
                shifts(pxh[:, t, :], bank2(T0 + s), in_width(L, s), vec[:, v:v + 1], vec[:, v + 2:v + 3])\
                    .then_inc(acc_free, 1)
            dve.wait_ge(sem("rope_in", L), 16)
            for j in range(5):
                q = pxq[:, IN_DST[j], 0:TX]
                dve.wait_ge(sem("rot_ready", L), j + 1)
                dve.tensor_tensor(qtmp[:, :], ps[:, j, :], cosx[:, 1, :], ALU.mult)
                dve.tensor_tensor(q, q, cosx[:, 0, :], ALU.mult)
                dve.drain()
                dve.tensor_tensor(q, q, qtmp[:, :], ALU.add).then_inc(sem("k_roped", L), 1)
                dve.drain()
            W = T if L == 0 else TX
            for c in range(2):
                m = dve.tensor_tensor(pxh[:, 2 + c, 0:W], pxh[:, 2 + c, 0:W], pxh[:, 4 + c, 0:W], ALU.mult)
            m.then_inc(sem("u_ready", L), 1)
            dve.drain()
            for c in range(2):
                bv = V0 + V_HYB + c
                dve.tensor_scalar(hub[:, c, 0:W], pxh[:, 2 + c, 0:W], vec[:, bv:bv + 1], None, ALU.mult)
            fseg = hsegs[L]
            n = 0
            for o in range(2):
                for s, c0, nt_ in fseg:
                    n += 1
                    w = nt_ * P
                    dve.wait_ge(sem("four_hi", L), n)
                    dve.tensor_tensor(hlo[:, 4 + o, c0:c0 + w],
                                      ps[:, 6 + o, 0:w] if s == 0 else ps[:, 5 - o, 0:w],
                                      hhi[:, 4 + o, c0:c0 + w].bitcast(F32), ALU.subtract)\
                       .then_inc(sem("four_out", L), 1)
            dve.wait_ge(sem("pta", L), 1)
            dve.memset(stat[:, :, 2:3], 0.0).then_inc(sem("ptb", L), 1)
            steps = attn_steps(L)
            N = len(steps)
            heads = 0
            for i in range(N + 2):
                if i < N:
                    nk = len(steps[i][4]) * P
                    dve.wait_ge(sem("s_ready", L), i + 1)
                    dve.reduce_max(stat[:, i % 2, 3:4], psf[:, 1024 * (i % 2):1024 * (i % 2) + nk], AX_X)
                    dve.drain()
                    dve.tensor_scalar(stat[:, i % 2, 0:1], stat[:, i % 2, 3:4], -SCALE, None, ALU.mult)\
                       .then_inc(sem("max_ready", L), 1)
                if 1 <= i <= N:
                    j, g, q0, k0, kts, last = steps[i - 1]
                    if len(kts) > 4:
                        dve.wait_ge(sem("t_ready", L), i)
                        if heads >= 2:
                            dve.wait_ge(sem("o_ready", L), heads - 1)
                        dve.tensor_copy(pt[:, heads % 2, 4:6, q0:q0 + P],
                                        ps[:, 5, 0:256].rearrange("p (c n) -> p c n", c=2)).then_inc(sem("ptb", L), 1)
                    else:
                        dve.wait_ge(sem("t_ready", L), i)
                        dve.drain().then_inc(sem("ptb", L), 1)
                    if last:
                        heads += 1
                if i < N:
                    dve.wait_ge(sem("exp_done", L), i + 1)
                    dve.reciprocal(stat[:, i % 2, 2:3], stat[:, i % 2, 1:2])
                    dve.drain()
                    dve.tensor_scalar(pr[:, i % 2, 0:nk], pr[:, i % 2, 0:nk], stat[:, i % 2, 2:3], None, ALU.mult)\
                       .then_inc(sem("p_ready", L), 1)
                if i >= 2 and steps[i - 2][5] and steps[i - 2][1] == 1:
                    j, g, q0, k0, kts, last = steps[i - 2]
                    nq = TX if k0 == 0 else TC
                    ht = j + (NQT if k0 else 0)
                    dve.wait_ge(sem("attn_hi", L), ht + 1)
                    dve.tensor_tensor(hlo[:, j, k0:k0 + nq], ps[:, 6 + ht % 2, 0:nq],
                                      hhi[:, j, k0:k0 + nq].bitcast(F32), ALU.subtract).then_inc(sem("attn_out", L), 1)
            for s, c0, nt_ in hsegs[L]:
                w = nt_ * P
                K = (L, s)
                for r in range(2):
                    m0 = V0 + V_MLP + 2 * r
                    dve.wait_ge(sem("h1_ready" if r == 0 else "h2_ready"), seg_nth(*K) + 1)
                    if r == 1:
                        dve.wait_ge(sem("h1_sin"), seg_nth(*K) + 1)
                    a, b = ha[0:64, 0:w], hb[0:64, 0:w]
                    dve.tensor_scalar(a, ps[0:64, 2 + r, 0:w], vec[0:64, m0:m0 + 1], vec[0:64, m0 + 1:m0 + 2],
                                      ALU.add, ALU.mult)
                    dve.drain()
                    dve.tensor_scalar(b, a, 1 / (2 * math.pi), MAGIC, ALU.mult, ALU.add)
                    dve.drain()
                    dve.tensor_scalar(b, b, MAGIC, None, ALU.subtract)
                    dve.drain()
                    dve.scalar_tensor_tensor(a, b, -TWO_PI_HI, a, ALU.mult, ALU.add)
                    dve.drain()
                    dve.scalar_tensor_tensor(a, b, -TWO_PI_LO, a, ALU.mult, ALU.add)
                    dve.drain()
                    dve.tensor_scalar(b, a, PI_IN, -PI_IN, ALU.min, ALU.max).then_inc(sem("harg"), 1)
                for q in range(nt_):
                    dve.wait_ge(sem("hf_ready"), tile_nth(*K) + q + 1)
                    dve.wait_ge(sem("dec_ready"), tile_nth(*K) + q + 1)
                    if q == 0:
                        dve.wait_ge(sem("h2_sin"), seg_nth(*K) + 1)
                        dve.memset(hsum[:, :], 0.0)
                    dve.tensor_tensor(hb[:, 0:256], ps[:, q % 2, 0:256], ha[:, 0:256], ALU.mult)
                    dve.tensor_tensor(hb[:, 256:512], ps[:, q % 2, 256:512], ha[:, 0:256], ALU.mult)\
                       .then_inc(sem("hf_taken"), 1)
                    dve.drain()
                    if q == 0:
                        dve.memset(hb[0:1, 256:512], 0.0)
                        dve.drain()
                    dve.tensor_tensor(hpm[:, q, 0:256], hb[:, 0:256], hb[:, 256:512], ALU.add)
                    dve.tensor_tensor(hpm[:, q, 256:512], hb[:, 0:256], hb[:, 256:512], ALU.subtract)
                    dve.scalar_tensor_tensor(hsp[:, 3, :], hb[:, :], -1.0, hb[:, :], ALU.mult, ALU.max)
                    dve.drain()
                    dve.tensor_tensor(hsum[:, :], hsum[:, :], hsp[:, 3, 0:256], ALU.add)
                    dve.drain()
                    m = dve.tensor_tensor(hsum[:, :], hsum[:, :], hsp[:, 3, 256:512], ALU.add)
                    if q == nt_ - 1:
                        m.then_inc(sem("hsum_ready"), 1)
                    dve.drain()
                dve.wait_ge(sem("hn_ready"), seg_nth(*K) + 1)
                dve.reciprocal(rnorm[:, :], ps[:, 2, 0:2])
                for f in range(nt_):
                    dve.wait_ge(sem("hu_ready"), tile_nth(*K) + f + 1)
                    dve.wait_ge(sem("hsp_ready"), tile_nth(*K) + f + 1)
                    u = 6 + f % 2
                    dve.tensor_tensor(hb[:, :], hsp[:, f, :], ps[:, u, :], ALU.mult)
                    dve.tensor_tensor(ha[:, 0:256], hsp[:, f, 0:256], ps[:, u, 256:512], ALU.mult)
                    dve.tensor_tensor(ha[:, 256:512], hsp[:, f, 256:512], ps[:, u, 0:256], ALU.mult)
                    dve.drain()
                    dve.tensor_tensor(hys[:, f, 0:256], hb[:, 0:256], hb[:, 256:512], ALU.subtract)
                    dve.tensor_tensor(hys[:, f, 256:512], ha[:, 0:256], ha[:, 256:512], ALU.add)\
                       .then_inc(sem("hys_ready"), 1)
                    dve.drain()
                for c in range(2):
                    dst = hub[:, c, c0:c0 + w]
                    dve.wait_ge(sem("hy_ready"), 2 * seg_nth(*K) + c + 1)
                    dve.scalar_tensor_tensor(dst, ps[:, c, 0:w], rnorm[:, c:c + 1], dst, ALU.mult, ALU.add)
                    dve.drain()
                    dve.tensor_tensor(dst, dst, pxh[:, c, c0:c0 + w], ALU.mult).then_inc(sem("hyf"), 1)
                for c in range(2):
                    dve.wait_ge(sem("hy_hi"), 2 * seg_nth(*K) + c + 1)
                    dve.tensor_tensor(hlo[:, 6 + c, c0:c0 + w], hub[:, c, c0:c0 + w],
                                      hhi[:, 6 + c, c0:c0 + w].bitcast(F32), ALU.subtract).then_inc(sem("hy_out", L), 1)
            post_norm((L, "postmix"), L, 1, W)
            norm_dve((L, "preffn"), x, W)
            dve.memset(y[:, :, 0:W], 0.0)
            F0, G0 = S0 + IN_T + OUT_T, T0 + IN_T + OUT_T
            with dve.Fori(0, CHUNKS) as i:
                dve.wait_ge(acc_free, i * FFN_TILES + G0)
                dve.tensor_scalar(cconv[:, :, :].rearrange("p t v -> p (t v)"),
                                  vec[:, bass.ds(i * (UP_T * 4) + (V0 + V_FFC), UP_T * 4)], 1.0, None, ALU.mult)\
                   .then_inc(sem("cconv_ready"), 1)
                dve.drain()
                B = L * CHUNKS * PAIRS
                for p in range(PAIRS):
                    for z in range(2):
                        s = 2 * p + z
                        dve.wait_ge(sem("up_mid"), i * UP_T + (2 * B + s + 1))
                        shifts(up[:, p % 2, z, :], bank2(G0 + s), W, cconv[:, s, 0:1], cconv[:, s, 2:3])\
                            .then_inc(acc_free, 1)
                        if z == 0:
                            dve.drain().then_inc(sem("gate_ready"), 1)
                    dve.drain()
                    dve.wait_ge(sem("silu_done"), i * PAIRS + (B + p + 1))
                    dve.tensor_tensor(sil[:, 0:W], sil[:, 0:W], up[:, p % 2, 1, 0:W], ALU.mult)\
                       .then_inc(sem("prod_ready"), 1)
                    dve.wait_ge(sem("ahi_ready"), i * PAIRS + (B + p + 1))
                    dve.tensor_tensor(alo[:, p, 0:W], sil[:, 0:W], ahi[:, p, 0:W].bitcast(F32), ALU.subtract)\
                       .then_inc(sem("act_ready"), 1)
                for o in range(KT):
                    b = bank2(G0 + UP_T + o)
                    if o < KT - 1:
                        dve.wait_ge(down_ready, i * (KT - 1) + (L * CHUNKS * (KT - 1) + o + 1))
                    else:
                        dve.wait_ge(slab_done, i * FFN_SLABS + (F0 + FFN_SLABS))
                    dve.tensor_tensor(y[:, o, 0:W], y[:, o, 0:W], psf[:, b * 512:b * 512 + W], ALU.add)\
                       .then_inc(acc_free, 1)
            dve.drain()
            post_norm((L, "postffn"), L, 3, W)

        norm_dve((2, "premix"), x, TX)
        dve.wait_ge(sem("namask_in"), 16)
        for i in range(4 * NH2):
            h, q = i // 4, i % 4
            tb = tab[:, h % 2, :]
            if q == 0:
                dve.wait_ge(sem("tab_in", h % 2), 32 * (h // 2 + 1))
                if h >= 8:
                    t3 = tb.rearrange("p (r c) -> p r c", c=HD)
                    dve.tensor_tensor(t3, t3, namask[:, :].unsqueeze(1).to_broadcast([P, TABW // HD, HD]), ALU.add)
                    dve.drain()
            dve.wait_ge(sem("s2_done"), i + 1)
            if i >= 2:
                dve.wait_ge(sem("exp2_done"), i - 1)
            o = (3 - q) * P
            dve.scalar_tensor_tensor(s2[:, i % 2, :], ps[:, i % 2, :], SCALE, tb[:, o:o + TX], ALU.mult, ALU.add)\
               .then_inc(sem("s2_ready"), 1)
            dve.drain()
            dve.reduce_max(stat[:, i % 2, 3:4], s2[:, i % 2, :], AX_X)
            dve.drain()
            dve.tensor_scalar(stat[:, i % 2, 0:1], stat[:, i % 2, 3:4], -1.0, None, ALU.mult)\
               .then_inc(sem("max2_ready"), 1)
            dve.wait_ge(sem("exp2_done"), i + 1)
            dve.reciprocal(stat[:, i % 2, 2:3], stat[:, i % 2, 1:2])
            dve.drain()
            dve.tensor_scalar(p2[:, i % 2, :], p2[:, i % 2, :], stat[:, i % 2, 2:3], None, ALU.mult)\
               .then_inc(sem("p2_ready"), 1)
        for a in range(2):
            dve.wait_ge(sem("ostd_ready"), a + 1)
            dve.reciprocal(nrm2[:, a, :], nrm2[:, a, :])
            dve.drain()
            for k in range(4 * a, 4 * a + 4):
                src = px2[:, 12 * a + k % 4, :]
                dve.scalar_tensor_tensor(src, src, vec[:, V2_OUT + k:V2_OUT + k + 1], nrm2[:, a, :],
                                         ALU.mult, ALU.mult).then_inc(sem("ot_ready"), 1)
        dve.drain()
        for k in range(KT):
            dve.wait_ge(sem("ohi_ready"), k + 1)
            dve.tensor_tensor(hlo[:, k, 0:TX], px2[:, 12 * (k // 4) + k % 4, :], hhi[:, k, 0:TX].bitcast(F32),
                              ALU.subtract).then_inc(sem("out_h_ready"), 1)
        for s in range(OUT_T):
            n, t = B2_SLAB + IN2_T + s, B2_TILE + IN2_T + s
            dve.wait_ge(slab_done, n + 1)
            dve.tensor_tensor(x[:, s, 0:TX], x[:, s, 0:TX], ps[:, bank2(t), :], ALU.add).then_inc(acc_free, 1)
        dve.drain().then_inc(sem("x2_ready"), 1)
        K = (2, "preffn")
        dve.wait_ge(sem("std_ready"), nth(K) + 1)
        dve.reciprocal(nrm[:, 0:TX], nrm[:, 0:TX])
        dve.drain()
        for k in range(KT):
            dve.scalar_tensor_tensor(hf2[:, k, :], x[:, k, 0:TX], vec[:, V2_FFN + k:V2_FFN + k + 1], nrm[:, 0:TX],
                                     ALU.mult, ALU.mult).then_inc(sem("scaled_ready"), 1)
        dve.drain()
        for k in range(KT):
            dve.wait_ge(sem("full_ready"), KT * pre_nth(K) + k + 1)
            dve.tensor_tensor(hlo[:, k, 0:TX], hf2[:, k, :], hhi[:, k, 0:TX].bitcast(F32), ALU.subtract)\
               .then_inc(sem("h_ready"), 1)

        dve.wait_ge(sem("logits_done"), 1)
        lg = ps[:, 7, 0:128].rearrange("p (t n) -> p t n", t=4)
        first4 = consts[:, 8:12].unsqueeze(1).to_broadcast([P, 4, 4])

        def r(n, w=4, c=0):
            return rt[:, n, :, c:c + w]

        def wide(ap, w):
            return ap.to_broadcast([P, 4, w])

        def one_hot(dst, val, top, rank):
            dve.tensor_tensor(dst, val, wide(top, 4), ALU.is_equal)
            dve.drain()
            dve.tensor_tensor(dst, dst, first4, ALU.mult)
            dve.drain()
            dve.tensor_reduce(rank, dst, AX_X, ALU.max)
            dve.drain()
            dve.tensor_tensor(dst, dst, wide(rank, 4), ALU.is_equal)
            dve.drain()

        dve.tensor_tensor(r(1, 16), lg[:, :, 4:20], bgr[:, 4:20].unsqueeze(1).to_broadcast([P, 4, 16]), ALU.add)
        dve.tensor_tensor(r(2), lg[:, :, 0:4], bgr[:, 0:4].unsqueeze(1).to_broadcast([P, 4, 4]), ALU.add)
        dve.drain()
        dve.tensor_reduce(r(4, 1), r(2), AX_X, ALU.max)
        dve.drain()
        one_hot(r(5), r(2), r(4, 1), r(4, 1, 1))
        dve.tensor_tensor(r(2), r(2), wide(r(4, 1), 4), ALU.subtract).then_inc(sem("g_ready"), 1)
        e4 = rt[:, 1, :, :].rearrange("p t (g e) -> p t g e", g=4)
        w4 = rt[:, 7, :, :].rearrange("p t (g e) -> p t g e", g=4)
        dve.tensor_tensor(w4, e4, r(5).unsqueeze(3).to_broadcast([P, 4, 4, 4]), ALU.mult)
        dve.drain()
        dve.tensor_reduce(r(6), rt[:, 7, :, :].rearrange("p t (g e) -> p t e g", g=4), AX_X, ALU.add)
        dve.drain()
        dve.tensor_reduce(r(4, 1, 2), r(6), AX_X, ALU.max)
        dve.drain()
        one_hot(r(10), r(6), r(4, 1, 2), r(4, 1, 1))
        dve.scalar_tensor_tensor(r(11), r(10), -1e30, r(6), ALU.mult, ALU.add)
        dve.drain()
        dve.tensor_reduce(r(4, 1, 3), r(11), AX_X, ALU.max)
        dve.drain()
        one_hot(r(12), r(11), r(4, 1, 3), r(4, 1, 1))
        dve.tensor_tensor(r(8, 1), r(4, 1, 3), r(4, 1, 2), ALU.subtract).then_inc(sem("e_ready"), 1)
        dve.wait_ge(sem("g_exp"), 1)
        dve.tensor_reduce(r(4, 1, 4), r(3), AX_X, ALU.add)
        dve.wait_ge(sem("e_exp"), 1)
        dve.tensor_scalar(r(9, 1, 1), r(9, 1), 1.0, None, ALU.add)
        dve.drain()
        dve.tensor_tensor(r(9, 1, 1), r(9, 1, 1), r(4, 1, 4), ALU.mult)
        dve.drain()
        dve.reciprocal(r(9, 1, 2), r(9, 1, 1))
        dve.drain()
        dve.tensor_tensor(r(9, 1, 3), r(9, 1, 2), r(9, 1), ALU.mult)
        dve.tensor_tensor(r(10), r(10), wide(r(9, 1, 2), 4), ALU.mult)
        dve.drain()
        dve.tensor_tensor(r(12), r(12), wide(r(9, 1, 3), 4), ALU.mult)
        dve.drain()
        dve.tensor_tensor(r(10), r(10), r(12), ALU.add)
        dve.drain()
        c4 = rt[:, 0, :, :].rearrange("p t (g e) -> p t g e", g=4)
        dve.tensor_tensor(c4, r(5).unsqueeze(3).to_broadcast([P, 4, 4, 4]),
                          r(10).unsqueeze(2).to_broadcast([P, 4, 4, 4]), ALU.mult).then_inc(sem("comb_tok"), 1)
        E0, G0 = B2_SLAB + IN2_T + OUT_T, B2_TILE + IN2_T + OUT_T
        dve.wait_ge(sem("comb_ready"), NEXP)
        with dve.Fori(0, MOE_TURNS) as i:
            for p in range(2 * EPI):
                e = esil[:, p % 2, :]
                dve.wait_ge(sem("esil_ready"), i * (2 * EPI) + (p + 1))
                dve.tensor_tensor(e, e, comb[:, bass.ds(i * EPI + p // 2, 1), :].rearrange("p a n -> p (a n)"),
                                  ALU.mult).then_inc(acc_free, 1)
                dve.drain()
                dve.wait_ge(slab_done, i * MOE_SLABS + (E0 + 2 * p + 2))
                dve.tensor_tensor(e, e, ps[:, bank2(G0 + 2 * p + 1), :], ALU.mult).then_inc(acc_free, 1)
                dve.drain().then_inc(sem("eprod_ready"), 1)
                dve.wait_ge(sem("ehi_ready"), i * (2 * EPI) + (p + 1))
                dve.tensor_tensor(elo[:, p, :], e, ehi[:, p, :].bitcast(F32), ALU.subtract)\
                   .then_inc(sem("eact_ready"), 1)
            for o in range(KT):
                dve.wait_ge(slab_done, i * MOE_SLABS + (E0 + MOE_UP + o + 1))
                dve.tensor_tensor(x[:, o, 0:TX], x[:, o, 0:TX], ps[:, bank2(G0 + MOE_UP + o), :], ALU.add)\
                   .then_inc(acc_free, 1)
            dve.drain()
        dve.drain().then_inc(sem("moe_done"), 1)
        K = (2, "final")
        dve.wait_ge(sem("std_ready"), nth(K) + 1)
        dve.reciprocal(nrm[:, 0:TX], nrm[:, 0:TX])
        dve.drain()
        for k in range(KT):
            dve.scalar_tensor_tensor(y[:, k, 0:TX], x[:, k, 0:TX], vec[:, V2_FIN + k:V2_FIN + k + 1], nrm[:, 0:TX],
                                     ALU.mult, ALU.mult).then_inc(sem("out_ready"), 1)

    blk.close()


def shape_constants():
    f = np.float32
    c = {"ident": np.eye(P, dtype=f)}
    c["headones"] = np.kron(np.eye(2), np.ones((HD, HD))).astype(f)
    r = np.zeros((P, P), f)
    for p in range(P):
        r[p + 16 if p % 32 < 16 else p - 16, p] = -1.0 if p % 32 < 16 else 1.0
    c["rot"] = r
    inv = f(10000.0) ** (-np.arange(0, 32, 2, dtype=f) / f(32))
    tok = np.arange(TX)
    row, col = (tok // 64).astype(f), (tok % 64).astype(f)
    d = np.arange(P) % HD
    ang = np.where((d < 32)[:, None], row[None, :], col[None, :]) * inv[d % 16][:, None]
    c["rope"] = np.stack([np.cos(ang), np.sin(ang)], 1).astype(f)
    con = np.zeros((P, 16), f)
    con[:, 0] = EPS
    tt = {0: np.linspace(0.0, 1.0, TX, dtype=f), 1: np.linspace(0.0, 1.0, TC, dtype=f)}
    for q in range(4):
        con[:, 2 + q] = -tt[0][q * P:q * P + P]
    for q in range(2):
        con[:, 6 + q] = -tt[1][q * P:q * P + P]
    con[:, 8:12] = [4, 3, 2, 1]
    c["consts"] = con

    def tiles(m):
        return m.reshape(-1, P, m.shape[1]).transpose(1, 0, 2)

    for L in (TX, TC):
        n, k = np.arange(L)[:, None], np.arange(L)[None, :]
        a = 2 * np.pi * ((n * k) % L) / L
        c[f"four{L}"] = np.stack([tiles(np.cos(a)), tiles(np.sin(a))], 1) / math.sqrt(L * HD)
        a = 2 * np.pi * ((n * (2 * k + 1)) % (4 * L)) / (4 * L)
        fw = np.stack([tiles(np.cos(a)), tiles(np.sin(a))], 1)
        iv = np.stack([tiles(np.cos(a).T), tiles(np.sin(a).T)], 1) / L
        if L == TX:
            c["hyf512"], c["hyi512"] = fw, iv
        else:
            c["hy256"] = np.concatenate([fw, iv], 1)
    n = np.arange(HD)
    a = 2 * np.pi * ((n[:, None] * n[None, :]) % HD) / HD
    c["fourch"] = np.concatenate([np.kron(np.eye(2), np.cos(a)), -np.kron(np.eye(2), np.sin(a))], 1)
    bands = np.linspace(1e-4, 15, 16, dtype=f)
    for s, L in ((0, TX), (1, TC)):
        w = f(2 * math.pi) * np.arange(L, dtype=f)[:, None] / f(L) * bands[None, :]
        c[f"z{L}"] = np.concatenate([tt[s][:, None], np.cos(w), -np.sin(w)], -1).T
    de = np.abs(np.linspace(math.log(1e-2) / 1.5, math.log(1e-2) / 0.3, 256, dtype=f))
    c["deltas"] = np.broadcast_to(de, (P, 256))
    j = np.arange(TABW)[None, :] - 3 * P - np.arange(P)[:, None]
    m = (abs(j) <= 64) * 1 + ((j % 4 == 0) & (abs(j) <= 256)) * 1 + (j % 16 == 0) * 1
    lm = np.where(m > 0, np.log(np.maximum(m, 1)), -1e30)
    slopes = 2.0 ** (-np.arange(1, 9))
    c["alibi"] = lm[None] - slopes[:, None, None] * abs(j)[None]
    qc, kc = np.arange(P)[:, None] % 64, np.arange(64)[None, :]
    st = np.clip(qc - 8, 0, 48)
    c["namask"] = np.where((kc >= st) & (kc < st + 16), 0.0, -1e30)
    es = np.zeros((NEXP, NEXP, P))
    for e in range(NEXP):
        es[e, e] = 1.0
    c["esel"] = es
    return {k: np.ascontiguousarray(v, dtype=f) for k, v in c.items()}


def slab(w):
    return w.reshape(KT, P, P).transpose(1, 0, 2).reshape(P, SLAB)


def slabs(w):
    n = w.shape[1] // P
    return w.reshape(KT, P, n, P).transpose(2, 1, 0, 3).reshape(n, P, SLAB)


def blocks(w, kt):
    b = w.reshape(kt, P, KT, P).transpose(2, 0, 1, 3).reshape(-1, KT, P, P)
    return b.transpose(0, 2, 1, 3).reshape(-1, P, SLAB)


def cols(v):
    return v.reshape(-1, P).T


def layout(a):
    o = {}
    fm = lambda v: np.ascontiguousarray(v[0].T.reshape(KT, P, -1).transpose(1, 0, 2))
    o["xT"], o["ctxT"] = fm(a["x"]), fm(a["ctx"])
    o["cT"] = np.stack([cols(a["c"][0]), cols(a["c_ctx"])], 2)
    o["w_mod"] = np.concatenate([slabs(a["w_mod"][L]) for L in range(DEPTH)])
    order = np.concatenate([np.r_[j * HD:(j + 1) * HD, (j + NQT) * HD:(j + NQT + 1) * HD] for j in range(NQT)])
    parts, vec = [], np.zeros((P, N_VEC), np.float32)
    for L in range(DEPTH):
        w = a["w_in"][L]
        parts.append(slabs(np.concatenate([w[:, 512:640], w[:, order], w[:, 640:768], w[:, 768:]], 1)))
        w = a["w_out"][L]
        parts.append(slabs(np.concatenate([w[order], w[512:]])))
        vc = np.concatenate([a["w_ffn_conv"][L], a["b_ffn_conv"][L][None]])
        vc = vc.reshape(4, 2, CHUNKS, PAIRS, P).transpose(4, 2, 3, 1, 0)
        for c in range(CHUNKS):
            r = slice(c * PAIRS * P, (c + 1) * PAIRS * P)
            up = a["w_up"][L].reshape(D, 2, FF)[:, :, r].reshape(D, 2, PAIRS, P).transpose(0, 2, 1, 3).reshape(D, -1)
            parts += [slabs(up), blocks(a["w_down"][L][r], PAIRS)]
        v = vec[:, L * V_LAYER:]
        for at, n in ((V_GPM, "g_pre_mix"), (V_GQM, "g_post_mix"), (V_GPF, "g_pre_ffn"), (V_GQF, "g_post_ffn")):
            v[:, at:at + KT] = cols(a[n][L])
        v[:, V_GQ], v[:, V_GK] = np.tile(a["g_q"][L], 2), np.tile(a["g_k"][L], 2)
        hc = np.concatenate([a["w_hy_conv"][L], a["b_hy_conv"][L][None]])
        v[:, V_HYC:V_HYC + 4 * NHY] = hc.reshape(4, NHY, P).transpose(2, 1, 0).reshape(P, -1)
        v[:, V_FFC:V_FFC + CHUNKS * UP_T * 4] = vc.reshape(P, -1)
        v[:, V_HYB:V_HYB + 2] = cols(a["hy_bias"][L])
        for q, n in enumerate(("hy_b1", "hy_fr1", "hy_b2", "hy_fr2")):
            v[0:HD, V_MLP + q] = a[n][L]
    o["bmod"] = np.repeat(np.concatenate([cols(a["b_mod"][L]) for L in range(DEPTH)], 1), 2, axis=1)
    w = a["w_in_2"][0]
    parts += [slabs(w), slabs(a["w_out_2"][0])]
    for i in range(MOE_TURNS):
        for e in range(EPI * i, EPI * i + EPI):
            g, u = slabs(a["w_gate_2"][0, e]), slabs(a["w_up_2"][0, e])
            parts += [g[0:1], u[0:1], g[1:2], u[1:2]]
        dn = a["w_down_2"][0, EPI * i:EPI * i + EPI].reshape(EPI * DEXP, D)
        parts.append(blocks(dn, KT))
    o["w_all"] = np.concatenate(parts)
    vec[:, V2_MIX:V2_MIX + KT] = cols(a["norm_mix_g_2"][0])
    vec[:, V2_OUT:V2_OUT + 4] = cols(a["g_out_dil_2"][0])
    vec[:, V2_OUT + 4:V2_OUT + 8] = cols(a["g_out_na_2"][0])
    vec[:, V2_FFN:V2_FFN + KT] = cols(a["norm_ffn_g_2"][0])
    vec[:, V2_FIN:V2_FIN + KT] = cols(a["norm_final_g_2"])
    o["vec"] = vec
    o["w_four"] = a["w_fourier"].reshape(DEPTH, 2, P, 256).transpose(0, 2, 1, 3)
    for n in ("hy_w1", "hy_w2", "hy_w3"):
        o[n] = a[n]
    o["wgr"] = np.concatenate([a["w_group_2"][0], a["w_router_2"][0]], 1).reshape(KT, P, 20).transpose(1, 0, 2)
    o["bgr"] = np.broadcast_to(np.concatenate([a["b_group_2"][0], a["b_router_2"][0]]), (P, 20))
    rp = np.pad(a["rpb_2"][0], ((0, 0), (0, 0), (48, 48)))
    o["rpbw"] = np.stack([rp[:, :, 63 - q:127 - q] for q in range(64)], 1).reshape(8, 64, 15 * HD)
    return {k: np.ascontiguousarray(v) for k, v in o.items()}


def kernel(**inputs):
    import concourse.bacc as bacc
    from concourse.bass_utils import run_bass_kernel_spmd

    arrays = layout({k: np.asarray(v) for k, v in inputs.items()}) | shape_constants()
    nc = bacc.Bacc("TRN2", target_bir_lowering=False, num_devices=1, dynamic_dma_scratch_size=1024)
    dram = {n: nc.dram_tensor(f"in_{n}", a.shape, F32, kind="ExternalInput").ap() for n, a in arrays.items()}
    out = nc.dram_tensor("out_x", (P, KT, TX), F32, kind="ExternalOutput").ap()
    program(nc, dram, out)
    r = run_bass_kernel_spmd(nc, [{f"in_{n}": a for n, a in arrays.items()}], core_ids=[0])
    y = r.results[0]["out_x"]
    return np.ascontiguousarray(y.transpose(2, 1, 0).reshape(1, TX, D))
```

```python
import math
from contextlib import ExitStack

import numpy as np
import concourse.bass as bass
from concourse import mybir

F32 = mybir.dt.float32
F32R = mybir.dt.float32r
ALU = mybir.AluOpType
ACT = mybir.ActivationFunctionType
AX_X = mybir.AxisListType.X

P = 128
D = 1024
KT = D // P
TX, TC = 512, 256
T = TX + TC
DEPTH = 2
HD = 64
NQT = 4
NHY = 6
FF = 2816
PAIRS = 11
CHUNKS = FF // P // PAIRS
NEXP, DEXP = 16, 256
EPI = 4
EPS = 1e-6
SCALE = HD ** -0.5

SLAB = KT * P
RING = 3
MOD_SLABS = DEPTH * 6 * KT
MOD_RING = 12
MOD_SPLIT = 4
MOD_GROUP = 4
MOD_GROUPS = MOD_RING // MOD_GROUP
IN_T, OUT_T = 14, KT
UP_T = 2 * PAIRS
FFN_SLABS = UP_T + PAIRS
FFN_TILES = UP_T + KT
LAYER_SLABS = IN_T + OUT_T + CHUNKS * FFN_SLABS
LAYER_TILES = IN_T + OUT_T + CHUNKS * FFN_TILES
IN2_T = 24
MOE_UP = EPI * 4
MOE_SLABS = MOE_UP + KT
MOE_TURNS = NEXP // EPI
B2_SLAB = DEPTH * LAYER_SLABS
B2_TILE = DEPTH * LAYER_TILES
N_SLABS = B2_SLAB + IN2_T + OUT_T + MOE_TURNS * MOE_SLABS
NH2 = 16

V_GPM, V_GQM, V_GPF, V_GQF, V_GQ, V_GK, V_HYC, V_FFC, V_HYB, V_BMOD, V_MLP = 0, 8, 16, 24, 32, 33, 34, 58, 234, 236, 284
V_LAYER = 288
V2 = DEPTH * V_LAYER
V2_MIX, V2_OUT, V2_FFN, V2_FIN = V2, V2 + 8, V2 + 16, V2 + 24
N_VEC = V2 + 32

MAGIC = 12582912.0
TWO_PI_HI = 6.28125
TWO_PI_LO = 2 * math.pi - TWO_PI_HI
PI_IN = 3.1415925

TABW = 3 * P + TX


def program(nc, dram, out):
    x_d, ctx_d, c_d = dram["xT"], dram["ctxT"], dram["cT"]
    base = (nc.sbuf_base + 31) // 32 * 32
    at = [base]

    def place(nbytes):
        o = at[0]
        at[0] += (nbytes + 31) // 32 * 32
        return o

    def sb(name, shape, off, dt=F32):
        return nc.alloc_sbuf_tensor_at(name, shape, dt, offset=off)

    X_O = place(KT * T * 4)
    WRAW_O = place(RING * SLAB * 4)
    WHI_O = place(RING * SLAB * 4)
    WLO_O = place(RING * SLAB * 4)
    HHI_O = place(KT * T * 4)
    HLO_O = place(KT * T * 4)
    BIG = place(KT * T * 4 + 2 * PAIRS * T * 4)
    SCR = place(5 * T * 4)

    x = sb("x", [P, KT, T], X_O)
    wraw = sb("wraw", [P, RING, SLAB], WRAW_O)
    whi = sb("whi", [P, RING, SLAB], WHI_O, F32R)
    wlo = sb("wlo", [P, RING, SLAB], WLO_O, F32R)
    mraw = sb("mraw", [P, MOD_RING, SLAB], HHI_O)
    mrow = sb("mrow", [4, MOD_GROUPS, MOD_GROUP * P], BIG)
    mhi = sb("mhi", [P, MOD_SPLIT, SLAB], BIG + 8192, F32R)
    mlo = sb("mlo", [P, MOD_SPLIT, SLAB], BIG + 8192 + MOD_SPLIT * SLAB * 4, F32R)
    hhi = sb("hhi", [P, KT, T], HHI_O, F32R)
    hlo = sb("hlo", [P, KT, T], HLO_O, F32R)
    ident = sb("ident", [P, P], place(P * 4))
    ones = sb("ones", [P, P], place(P * 4))
    headones = sb("headones", [P, P], place(P * 4))
    rot = sb("rot", [P, P], place(P * 4))
    vec = sb("vec", [P, N_VEC], place(N_VEC * 4))
    mod = sb("mod", [P, DEPTH, 6 * KT, 2], place(DEPTH * 6 * KT * 2 * 4))
    mv = sb("mv", [P, DEPTH, 4, KT, 2], place(DEPTH * 4 * KT * 2 * 4))
    cs = sb("cs", [P, KT, 2], place(KT * 2 * 4))
    csr = sb("csr", [P, KT, 4], place(KT * 4 * 4), F32R)
    consts = sb("consts", [P, 16], place(64))
    cconv = sb("cconv", [P, UP_T, 4], place(UP_T * 16))
    stat = sb("stat", [P, 2, 4], place(32))
    rnorm = sb("rnorm", [P, 2], place(8))
    bmod = sb("bmod", [P, DEPTH * 6 * KT * 2], place(DEPTH * 6 * KT * 2 * 4))
    rcol = sb("rcol", [P, T // P], place(T // P * 4))
    diag = sb("diag", [P, 2, P], place(2 * P * 4))
    assert at[0] <= nc.sbuf_usable_end, at[0]
    eps_c, zero_c = consts[:, 0:1], consts[:, 1:2]

    y = sb("y", [P, KT, T], BIG)
    ACT_O = BIG + KT * T * 4
    ahi = sb("ahi", [P, PAIRS, T], ACT_O, F32R)
    alo = sb("alo", [P, PAIRS, T], ACT_O + PAIRS * T * 4, F32R)
    nsq = sb("nsq", [P, 2, T], ACT_O)
    rdiag = sb("rdiag", [P, T // P, P], ACT_O + 2 * T * 4)
    nt = sb("nt", [P, 2, T], ACT_O + 3 * T * 4)
    nfull = sb("nfull", [P, 2, T], ACT_O + 5 * T * 4)
    up = sb("up", [P, 2, 2, T], SCR)
    ysq = sb("ysq", [P, 2, T], SCR)
    yacc = sb("yacc", [P, T], SCR + 2 * T * 4)
    sil = sb("sil", [P, T], SCR + 4 * T * 4)

    pxq = sb("pxq", [P, NQT + 2, T], BIG)
    PXK, PXV = NQT, NQT + 1
    pxf = sb("pxf", [P, 2, T], BIG + 6 * T * 4)
    pxh = sb("pxh", [P, NHY, T], BIG + 8 * T * 4)
    M0 = BIG + 14 * T * 4
    cosx = sb("cosx", [P, 2, TX], SCR)
    qsq = sb("qsq", [P, T], SCR + 2 * TX * 4)
    qrs = sb("qrs", [P, 2, T], SCR + 2 * TX * 4 + T * 4)
    qtmp = sb("qtmp", [P, TX], SCR + 2 * TX * 4 + 3 * T * 4)
    fl5 = sb("fl5", [P, 2, 4, TX], M0)
    fl2 = sb("fl2", [P, 2, 2, TC], M0 + 16384)
    fab = sb("fab", [P, 6, 512], M0 + 20480)
    fy = sb("fy", [P, 2, T], M0 + 32768)
    wfo = sb("wfo", [P, 2, 256], M0 + 38912)
    fch = sb("fch", [P, 256], M0 + 40960)
    pr = sb("pr", [P, 3, T], BIG)
    pth = sb("pth", [P, 2, 6, TX], M0, F32R)
    ptl = sb("ptl", [P, 2, 6, TX], M0 + 24576, F32R)
    vth = sb("vth", [P, 2, 6, P], BIG + 4 * T * 4, F32R)
    vtl = sb("vtl", [P, 2, 6, P], BIG + 6 * T * 4, F32R)
    hd5 = sb("hd5", [P, 2, 4, TX], M0 + 32768)
    hi5 = sb("hi5", [P, 2, 4, TX], M0)
    hsp = sb("hsp", [P, 4, 512], M0 + 16384)
    hys = sb("hys", [P, 4, 512], M0 + 24576)
    hd2 = sb("hd2", [P, 4, 2, TC], BIG)
    hpm = sb("hpm", [P, 4, 512], BIG + 8192)
    hut = sb("hut", [P, 6, 256], BIG + 6 * T * 4)
    hw3 = sb("hw3", [P, 512], SCR)
    hz = sb("hz", [P, 512], SCR + 2048)
    hw12 = sb("hw12", [P, 128], SCR + 4096)
    hl = sb("hl", [P, 2, 512], SCR + 4608)
    ha = sb("ha", [P, 512], SCR + 8704)
    hb = sb("hb", [P, 512], SCR + 10752)
    hdel = sb("hdel", [P, 256], SCR + 12800)
    hsum = sb("hsum", [P, 256], SCR + 13824)
    hub = sb("hub", [P, 2, T], BIG + 12 * T * 4)

    px2 = sb("px2", [P, IN2_T, TX], BIG)
    px2r = sb("px2r", [P, IN2_T, TX], BIG, F32R)
    tab = sb("tab", [P, 2, TABW], BIG + 49152)
    qkh = sb("qkh", [P, 16, TX], BIG + 56320, F32R)
    namask = sb("namask", [P, HD], BIG + 89088)
    pt2h = sb("pt2h", [P, 2, 4, TX], HHI_O, F32R)
    pt2l = sb("pt2l", [P, 2, 4, TX], HHI_O + 16384, F32R)
    vt2h = sb("vt2h", [P, 2, 2, 4, P], HHI_O + 32768, F32R)
    vt2l = sb("vt2l", [P, 2, 2, 4, P], HHI_O + 40960, F32R)
    s2 = sb("s2", [P, 2, TX], SCR)
    p2 = sb("p2", [P, 3, TX], SCR + 4096)
    comb = sb("comb", [P, NEXP, TX], BIG + KT * T * 4)
    ehi = sb("ehi", [P, 2 * EPI, TX], BIG + KT * T * 4 + 32768, F32R)
    elo = sb("elo", [P, 2 * EPI, TX], BIG + KT * T * 4 + 49152, F32R)
    wgr = sb("wgr", [P, KT, 20], SCR)
    bgr = sb("bgr", [P, 20], SCR + 640)
    hf2 = sb("hf2", [P, KT, TX], BIG)
    rt = sb("rt", [P, 16, 4, 16], BIG + 32768)
    cmbT = sb("cmbT", [NEXP, TX], SCR + 1024)
    esel = sb("esel", [NEXP, NEXP, P], SCR + 4096)
    esil = sb("esil", [P, 2, TX], SCR)
    nsq2 = sb("nsq2", [P, 2, TX], BIG + 49152)
    nrm2 = sb("nrm2", [P, 2, TX], BIG + 53248)

    ps = nc.alloc_psum_tensor("ps", [P, 8, 512], F32)
    rbc = ps[:, 6:8, :].rearrange("p b n -> p (b n)")
    psf = ps[:, :, :].rearrange("p b n -> p (b n)")

    names = {}

    def sem(*key):
        if key not in names:
            names[key] = nc.alloc_semaphore("_".join(map(str, key)))
        return names[key]

    norms = [(L, n) for L in range(DEPTH) for n in ("premix", "postmix", "preffn", "postffn")]
    norms += [(2, "premix"), (2, "preffn"), (2, "final")]

    def nth(key):
        return norms.index(key)

    def pre_nth(key):
        return [k for k in norms if k[1][:4] != "post"].index(key)

    def post_nth(key):
        return [k for k in norms if k[1][:4] == "post"].index(key)

    def sum_nth(key):
        return 0 if key == norms[0] else 1 + post_nth(key)

    def sq_nth(key):
        return pre_nth(key) - 1

    def mix_nth(L):
        return 1 + (1 + CHUNKS) * L

    def ffn_nth(L):
        return mix_nth(L) + 1

    def seg_nth(L, s):
        return 2 * L + s

    def tile_nth(L, s):
        return (0, TX // P, T // P)[seg_nth(L, s)]

    raw = [sem("raw_landed", s) for s in range(RING)]
    mod_landed = [sem("mod_landed", s) for s in range(MOD_RING)]
    hi_split, lo_split, slab_done = sem("hi_split"), sem("lo_split"), sem("slab_done")
    mod_used, acc_free, down_ready = sem("mod_used"), sem("acc_free"), sem("down_ready")
    consts_in = sem("consts_in")
    N_CONST = 7
    small_in = sem("small_in")

    def bank2(t):
        return 2 * (t % 3)

    def wh(slot, k):
        return whi[:, slot, k * P:(k + 1) * P]

    def wl(slot, k):
        return wlo[:, slot, k * P:(k + 1) * P]

    segs = {T: [(0, TX, 0), (TX, TC, 1)], TX: [(0, TX, 0)]}

    def in_width(L, s):
        return T if L == 0 or s in (0, 5) else TX

    IN_DST = [PXK, 0, 1, 2, 3, PXV]
    QK_H = [6, 0, 1, 2, 3]

    def attn_steps(L):
        st = []
        for j in range(NQT):
            for g in range(2):
                st += [(j, g, q * P, 0, range(6), q == 3) for q in range(4)]
        if L == 0:
            for j in range(NQT):
                for g in range(2):
                    st += [(j, g, TX + q * P, TX, range(4, 6), q == 1) for q in range(2)]
        return st

    STEPS0 = len(attn_steps(0))

    def halves(L):
        hv, before = [], [0]
        for i, st in enumerate(attn_steps(L)):
            n = len(st[4])
            hv += [(i, 4 + b, 3 * b, min(3 * b + 3, n)) for b in range((n + 2) // 3)]
            before.append(len(hv))
        return hv, before

    V_STEPS = [0] + [8 * v + 6 for v in range(NH2 // 2 - 1)]
    def output_shares(L):
        steps, shares = attn_steps(L), {}
        ends = [i for i, st in enumerate(steps) if st[5]]
        for head, b in enumerate(ends):
            nxt = ends[head + 1] - b if head + 1 < len(ends) else b - ends[head - 1]
            n = len(steps[b][4])
            for q in range(nxt):
                shares[b + 3 + q] = (head, b, range(n * q // nxt, n * (q + 1) // nxt), q == 0, q == nxt - 1)
        return shares

    HALVES0 = len(halves(0)[0])
    hsegs = {0: [(0, 0, 4), (1, TX, 2)], 1: [(0, 0, 4)]}

    blk = ExitStack()
    block = blk.enter_context(nc.Block())

    @block.sync
    def _(sp):
        sp.dma_start(cs[:, :, :], c_d).then_inc(small_in, 16)
        sp.dma_start(consts[:, :], dram["consts"]).then_inc(small_in, 16)
        for n in range(MOD_RING):
            sp.dma_start(mraw[:, n, :], dram["w_mod"][n, :, :]).then_inc(mod_landed[n], 16)
            if n == MOD_GROUP - 1:
                sp.dma_start(x[:, :, 0:TX], x_d).then_inc(consts_in, 16)
                sp.dma_start(x[:, :, TX:T], ctx_d).then_inc(consts_in, 16)
                sp.dma_start(vec[:, :], dram["vec"]).then_inc(consts_in, 16)
                sp.dma_start(bmod[:, :], dram["bmod"]).then_inc(consts_in, 16)
                for t, name in ((ident, "ident"), (headones, "headones"), (rot, "rot")):
                    sp.dma_start(t[:, :], dram[name]).then_inc(consts_in, 16)
        for j in range(RING):
            sp.dma_start(wraw[:, j, :], dram["w_all"][j, :, :]).then_inc(raw[j], 16)
        with sp.Fori(0, MOD_SLABS // MOD_RING - 1) as i:
            for j in range(MOD_RING):
                sp.wait_ge(sem("mod_lo"), MOD_RING * i + j + 1)
                sp.dma_start(mraw[:, j, :], dram["w_mod"][MOD_RING * i + MOD_RING + j, :, :])\
                  .then_inc(mod_landed[j], 16)
        turns, rest = divmod(N_SLABS - RING, RING)
        with sp.Fori(0, turns) as i:
            for j in range(RING):
                sp.wait_ge(lo_split, RING * i + j + 1)
                sp.dma_start(wraw[:, j, :], dram["w_all"][RING * i + RING + j, :, :]).then_inc(raw[j], 16)
        for j in range(rest):
            sp.wait_ge(lo_split, RING * turns + j + 1)
            sp.dma_start(wraw[:, j, :], dram["w_all"][RING * turns + RING + j, :, :]).then_inc(raw[j], 16)
        sp.wait_ge(sem("out_ready"), KT)
        sp.dma_start(out, y[:, :, 0:TX]).then_inc(sem("stored"), 16)
        sp.wait_ge(sem("stored"), 16)

    @block.gpsimd
    def _(pool):
        pool.memset(ones[:, :], 1.0).then_inc(sem("ones_set"), 1)

        def low(n, slot):
            pool.wait_ge(hi_split, n + 1)
            pool.tensor_tensor(wlo[:, slot, :], wraw[:, slot, :], whi[:, slot, :].bitcast(F32),
                               ALU.subtract).then_inc(lo_split, 1)

        with pool.Fori(0, N_SLABS // RING) as i:
            for j in range(RING):
                low(RING * i + j, j)
        for n in range(N_SLABS // RING * RING, N_SLABS):
            low(n, n % RING)

    @block.tensor
    def _(pe):

        def slab_ready(n):
            pe.wait_ge(lo_split, n + 1)

        def tile(n, t, bank, slot, rhs, width, first=False):
            if not first:
                pe.wait_ge(acc_free, t - 2)
            slab_ready(n)
            for k in range(KT):
                hi, lo = rhs(k)
                passes = [(wh(slot, k), hi), (wh(slot, k), lo), (wl(slot, k), hi)]
                for c0, w, b in segs[width]:
                    for q, (a, r) in enumerate(passes):
                        m = pe.matmul(ps[:, bank + b, 0:w], a, r[:, c0:c0 + w],
                                      start=k == 0 and q == 0, stop=k == KT - 1 and q == 2)
            m.then_inc(slab_done, 1)

        def first_tiles(n, t, n0, t0, rhs, widths, first, ready, before):
            for z in range(2):
                if not first:
                    pe.wait_ge(acc_free, t + z - 2)
            slab_ready(n + 1)
            for k in range(KT):
                pe.wait_ge(ready, before + k + 1)
                hi, lo = rhs(k)
                for z, width in enumerate(widths):
                    slot, bank = (n0 + z) % RING, bank2(t0 + z)
                    passes = [(wh(slot, k), hi), (wh(slot, k), lo), (wl(slot, k), hi)]
                    for c0, w, b in segs[width]:
                        for q, (a, r) in enumerate(passes):
                            m = pe.matmul(ps[:, bank + b, 0:w], a, r[:, c0:c0 + w],
                                          start=k == 0 and q == 0, stop=k == KT - 1 and q == 2)
                    if k == KT - 1:
                        m.then_inc(slab_done, 1)

        def down(slab0, t0, n0, tt0, rhs, width, ready0):
            for o in range(KT):
                bank = bank2(tt0 + o)
                pe.wait_ge(acc_free, t0 + o - 2)
                for k in range(PAIRS):
                    q = PAIRS * o + k
                    s, b8 = q // KT, q % KT
                    slot = (n0 + s) % RING
                    if b8 == 0:
                        slab_ready(slab0 + s)
                    if o == 0:
                        pe.wait_ge(sem("act_ready"), ready0 + k + 1)
                    hi, lo = rhs(k)
                    passes = [(wh(slot, b8), hi), (wh(slot, b8), lo), (wl(slot, b8), hi)]
                    for c0, w, b in segs[width]:
                        for z, (a, r) in enumerate(passes):
                            m = pe.matmul(ps[:, bank + b, 0:w], a, r[:, c0:c0 + w],
                                          start=k == 0 and z == 0, stop=k == PAIRS - 1 and z == 2)
                    if b8 == KT - 1:
                        m.then_inc(slab_done, 1)
                    elif k == PAIRS - 1:
                        m.then_inc(down_ready, 1)

        def sums(src, width, first, last):
            for tt in range(width // P):
                m = pe.matmul(ps[:, 5, tt:tt + 1], src[:, tt * P:tt * P + P], ones[:, 0:1],
                              start=first and tt == 0, stop=last and tt == width // P - 1)
            return m

        def squares(key, width):
            for k in range(KT):
                pe.wait_ge(sem("sq_ready"), KT * sq_nth(key) + k + 1)
                sums(nsq[:, k % 2, :], width, k == 0, k == KT - 1).then_inc(sem("sq_used"), 1)

        def summed_squares(key, width):
            pe.wait_ge(sem("ysum_ready"), sum_nth(key) + 1)
            sums(yacc, width, True, True).then_inc(sem("ysum_used"), 1)

        def spread(key, width):
            pe.wait_ge(sem("rdiag_ready"), nth(key) + 1)
            rd = rdiag[:, :, :].rearrange("p t n -> p (t n)")
            for c0, w, b in segs[width]:
                m = pe.matmul(ps[:, 6 + b, 0:w], ones[:, :], rd[:, c0:c0 + w], start=True, stop=True)
            m.then_inc(sem("r_ready"), 1)

        def mod_turn(i, first):
            def turn(g, i):
                if g == 0 and not first:
                    pe.wait_ge(sem("mod_taken"), i)
                pe.wait_ge(sem("mod_rows"), MOD_GROUPS * i + (g + 1))
                for j in range(MOD_GROUP):
                    c = MOD_GROUP * g + j
                    m = pe.matmul(ps[:, 3, 2 * c:2 * c + 2], mrow[0:4, g, j * P:j * P + P], consts[0:4, 12:14],
                                  start=True, stop=True)
                if g == MOD_GROUPS - 1:
                    m.then_inc(sem("mod_turned"), 1)

            for n in range(MOD_RING):
                g, j = n // MOD_GROUP, n % MOD_GROUP
                pe.wait_ge(sem("mod_lo"), MOD_RING * i + (n + 1))
                for kk in range(2):
                    k = 2 * j + kk
                    col = slice(kk * 512, kk * 512 + 512)
                    passes = [(4, mhi), (2, mlo)] if k < KT - 1 else [(2, mlo), (4, mhi)]
                    for rows, w in passes:
                        m = pe.matmul(ps[0:rows, g, :], csr[:, k, 0:rows], w[:, n % MOD_SPLIT, col],
                                      start=k == 0 and rows == 4, stop=k == KT - 1 and rows == 4)
                m.then_inc(mod_used, 1)
                if n == 3 and not first:
                    turn(2, i - 1)
                if n == 7 or n == 11:
                    turn(n // MOD_GROUP - 1, i)
            return turn

        MOD_TURNS = MOD_SLABS // MOD_RING
        pe.wait_ge(small_in, 32)
        pe.wait_ge(sem("c_split"), 1)
        mod_turn(0, True)
        with pe.Fori(1, MOD_TURNS) as i:
            turn = mod_turn(i, False)
        turn(2, MOD_TURNS - 1)
        pe.wait_ge(consts_in, 16 * N_CONST)
        pe.wait_ge(sem("ones_set"), 1)
        summed_squares((0, "premix"), T)
        spread((0, "premix"), T)

        def h_rhs(k):
            return hhi[:, k, :], hlo[:, k, :]

        for L in range(DEPTH):
            S0, T0 = L * LAYER_SLABS, L * LAYER_TILES
            if L:
                squares((L, "premix"), T)
                spread((L, "premix"), T)
            first_tiles(S0, T0, S0, T0, h_rhs, [in_width(L, 0), in_width(L, 1)], L == 0,
                        sem("h_ready"), KT * pre_nth((L, "premix")))
            for s in range(IN_T):
                if s >= 2:
                    tile(S0 + s, T0 + s, bank2(T0 + s), (S0 + s) % RING, h_rhs, in_width(L, s), T0 + s < 3)
                if 1 <= s <= 5:
                    j = s - 1
                    pe.wait_ge(sem("qsq_ready"), 5 * L + j + 1)
                    if j:
                        pe.wait_ge(sem("qstd_ready"), 5 * L + j)
                    for c0, w, b in segs[in_width(L, j)]:
                        m = pe.matmul(ps[:, 6 + b, 0:w], headones[:, :], qsq[:, c0:c0 + w], start=True, stop=True)
                    m.then_inc(sem("qss_ready"), 1)
            pe.wait_ge(acc_free, T0 + IN_T)
            for j in range(5):
                pe.wait_ge(sem("qn_ready"), 5 * L + j + 1)
                pe.matmul(ps[:, j, :], rot[:, :], pxq[:, IN_DST[j], 0:TX], start=True, stop=True)\
                  .then_inc(sem("rot_ready"), 1)
            fseg = hsegs[L]
            ntt = 6 if L == 0 else 4
            pe.wait_ge(sem("ftab_in", L), 16 * (4 if L == 0 else 3))
            for tt in range(ntt):
                if tt >= 2:
                    pe.wait_ge(sem("fab_ready"), T // P * L + tt - 1)
                for f in range(2):
                    for ab in range(2):
                        m = pe.matmul(ps[:, 6 + tt % 2, ab * 256 + f * P:ab * 256 + f * P + P],
                                      pxf[:, f, tt * P:tt * P + P], fch[:, ab * P:ab * P + P],
                                      start=True, stop=True)
                m.then_inc(sem("fst1"), 1)
            pe.wait_ge(sem("fab_ready"), T // P * L + ntt)
            pe.wait_ge(sem("k_roped"), 5 * L + 5)
            for f in range(2):
                for s, c0, nt_ in fseg:
                    w = nt_ * P
                    dst = ps[:, 6 + f, 0:w] if s == 0 else ps[:, 5 - f, 0:w]
                    tb = fl5 if s == 0 else fl2
                    for q in range(nt_):
                        for ab in range(2):
                            m = pe.matmul(dst, fab[:, c0 // P + q, ab * 256 + f * P:ab * 256 + f * P + P],
                                          tb[:, ab, q, 0:w], start=q == 0 and ab == 0, stop=q == nt_ - 1 and ab == 1)
                    m.then_inc(sem("fst2"), 1)
            pe.wait_ge(sem("fy_ready"), 4 * L + 2 * len(fseg))
            for o in range(2):
                for s, c0, nt_ in fseg:
                    w = nt_ * P
                    dst = ps[:, 6 + o, 0:w] if s == 0 else ps[:, 5 - o, 0:w]
                    for f in range(2):
                        m = pe.matmul(dst, wfo[:, f, o * P:o * P + P], fy[:, f, c0:c0 + w], start=f == 0, stop=f == 1)
                    m.then_inc(sem("fst3"), 1)
            pe.wait_ge(sem("k_roped"), 5 * L + 5)
            pe.wait_ge(sem("four_out"), 4 * L + 2 * len(fseg))
            pe.wait_ge(sem("qk_lo"), 5 * L + 5)
            for tt in range(6):
                m = pe.transpose(ps[:, 4 + tt // 4, (tt % 4) * P:(tt % 4) * P + P], pxq[:, PXV, tt * P:tt * P + P],
                                 ident[:, :])
            m.then_inc(sem("vt_done"), 1)
            steps = attn_steps(L)
            hv, before = halves(L)
            shares = output_shares(L)
            N = len(steps)
            for i in range(max(shares) + 1):
                if i < N:
                    j, g, q0, k0, kts, last = steps[i]
                    h = slice(64 * g, 64 * g + 64)
                    if i >= 2:
                        pe.wait_ge(sem("exp_done"), STEPS0 * L + i - 1)
                    nk = len(kts) * P
                    for c in range(0, nk, 512):
                        w = min(512, nk - c)
                        for z, (a, b) in enumerate(((hhi, hhi), (hhi, hlo), (hlo, hhi))):
                            m = pe.matmul(ps[:, 2 * (i % 2) + c // 512, 0:w], a[h, j, q0:q0 + P],
                                          b[h, QK_H[0], k0 + c:k0 + c + w], start=z == 0, stop=z == 2)
                    m.then_inc(sem("s_ready"), 1)
                if 2 <= i < N + 2:
                    pe.wait_ge(sem("p_ready"), STEPS0 * L + i - 1)
                    for n in range(before[i - 2], before[i - 1]):
                        _, bank, c0, c1 = hv[n]
                        last_in = max([e + 1 for e in range(n) if hv[e][1] == bank], default=0)
                        pe.wait_ge(sem("pt_lo"), (HALVES0 + 1) * L + 1 + last_in)
                        for c in range(c0, c1):
                            m = pe.matmul(ps[:, bank, (c - c0) * P:(c - c0 + 1) * P],
                                          pr[:, (i - 2) % 3, c * P:c * P + P], diag[:, i % 2, :],
                                          start=True, stop=True)
                        m.then_inc(sem("t_ready"), 1)
                if i in shares:
                    head, b, tiles, first, last = shares[i]
                    j, g, q0, k0, kts, _ = steps[b]
                    nq = TX if k0 == 0 else TC
                    ht = head // 2
                    if first:
                        if ht >= 2:
                            pe.wait_ge(sem("attn_out"), 2 * NQT * L + ht - 1)
                        pe.wait_ge(sem("pt_lo"), (HALVES0 + 1) * L + 1 + before[b + 1])
                    for c in tiles:
                        for z, (u, w) in enumerate(((vth, pth), (vth, ptl), (vtl, pth))):
                            m = pe.matmul(ps[:, 6 + ht % 2, 0:nq], u[:, g, kts[c], :], w[:, head % 2, c, 0:nq],
                                          start=g == 0 and c == 0 and z == 0,
                                          stop=g == 1 and c == len(kts) - 1 and z == 2)
                    if last:
                        m.then_inc(sem("o_ready"), 1)
            pe.wait_ge(sem("attn_out"), 2 * NQT * L + NQT * (2 if L == 0 else 1))
            pe.wait_ge(sem("u_ready"), L + 1)
            for tt in range(ntt):
                if tt >= 2:
                    pe.wait_ge(sem("ut_ready"), T // P * L + tt - 1)
                for c in range(2):
                    m = pe.transpose(ps[:, tt % 2, c * P:c * P + P], pxh[:, 2 + c, tt * P:tt * P + P], ident[:, :])
                m.then_inc(sem("ut_done"), 1)
            for s, c0, nt_ in hsegs[L]:
                w = nt_ * P
                K = (L, s)
                pe.wait_ge(sem("hfil_in", L), 16 * (5 + s))
                pe.wait_ge(sem("ut_ready"), T // P * L + ntt)
                pe.matmul(ps[0:64, 2, 0:w], hw12[0:33, 0:64], hz[0:33, 0:w], start=True, stop=True)\
                  .then_inc(sem("h1_ready"), 1)
                pe.wait_ge(sem("h1_sin"), seg_nth(*K) + 1)
                pe.matmul(ps[0:64, 3, 0:w], hw12[0:64, 64:128], hl[0:64, 0, 0:w], start=True, stop=True)\
                  .then_inc(sem("h2_ready"), 1)
                pe.wait_ge(sem("h2_sin"), seg_nth(*K) + 1)
                for q in range(nt_):
                    if q >= 2:
                        pe.wait_ge(sem("hf_taken"), tile_nth(*K) + q - 1)
                    pe.matmul(ps[:, q % 2, :], hl[0:64, 1, q * P:q * P + P], hw3[0:64, :], start=True, stop=True)\
                      .then_inc(sem("hf_ready"), 1)
                pe.wait_ge(sem("hsum_ready"), seg_nth(*K) + 1)
                for c in range(2):
                    m = pe.matmul(ps[:, 2, c:c + 1], hsum[:, c * P:c * P + P], ones[:, 0:1], start=True, stop=True)
                m.then_inc(sem("hn_ready"), 1)
                fwd = hd5 if s == 0 else hd2
                pe.wait_ge(sem("hfwd_in"), 16 * L + 16)
                if s == 1:
                    pe.wait_ge(sem("hd2_in", L), 16)
                for f in range(nt_):
                    if f >= 2:
                        pe.wait_ge(sem("hys_ready"), tile_nth(*K) + f - 1)
                    for cs_ in range(2):
                        for q in range(nt_):
                            m = pe.matmul(ps[:, 4 + f % 2, cs_ * 256:cs_ * 256 + 256],
                                          fwd[:, cs_, q, f * P:f * P + P], hpm[:, q, cs_ * 256:cs_ * 256 + 256],
                                          start=q == 0, stop=q == nt_ - 1)
                    m.then_inc(sem("hk_ready"), 1)
                    for cs_ in range(2):
                        for q in range(nt_):
                            m = pe.matmul(ps[:, 6 + f % 2, cs_ * 256:cs_ * 256 + 256],
                                          fwd[:, cs_, q, f * P:f * P + P], hut[:, c0 // P + q, :],
                                          start=q == 0, stop=q == nt_ - 1)
                    m.then_inc(sem("hu_ready"), 1)
                pe.wait_ge(sem("hys_ready"), tile_nth(*K) + nt_)
                pe.wait_ge(sem("hinv_in"), 16 * L + 16)
                for c in range(2):
                    for f in range(nt_):
                        for cs_ in range(2):
                            iv = hi5[:, cs_, f, 0:w] if s == 0 else hd2[:, 2 + cs_, f, 0:w]
                            m = pe.matmul(ps[:, c, 0:w], hys[:, f, cs_ * 256 + c * P:cs_ * 256 + c * P + P], iv,
                                          start=f == 0 and cs_ == 0, stop=f == nt_ - 1 and cs_ == 1)
                    m.then_inc(sem("hy_ready"), 1)
                pe.wait_ge(sem("hy_out"), 4 * L + 2 * (s + 1))
            W = T if L == 0 else TX
            for s in range(OUT_T):
                tile(S0 + IN_T + s, T0 + IN_T + s, bank2(T0 + IN_T + s), (S0 + IN_T + s) % RING, h_rhs, W)
            summed_squares((L, "postmix"), W)
            spread((L, "postmix"), W)
            squares((L, "preffn"), W)
            spread((L, "preffn"), W)
            F0, G0 = S0 + IN_T + OUT_T, T0 + IN_T + OUT_T
            with pe.Fori(0, CHUNKS) as i:
                first_tiles(i * FFN_SLABS + F0, i * FFN_TILES + G0, F0, G0, h_rhs, [W, W], False,
                            sem("h_ready"), KT * pre_nth((L, "preffn")))
                for s in range(2, UP_T):
                    tile(i * FFN_SLABS + (F0 + s), i * FFN_TILES + (G0 + s), bank2(G0 + s), (F0 + s) % RING, h_rhs, W)
                down(i * FFN_SLABS + (F0 + UP_T), i * FFN_TILES + (G0 + UP_T), F0 + UP_T, G0 + UP_T,
                     lambda k: (ahi[:, k, :], alo[:, k, :]), W, i * PAIRS + L * CHUNKS * PAIRS)
            summed_squares((L, "postffn"), W)
            spread((L, "postffn"), W)

        squares((2, "premix"), TX)
        spread((2, "premix"), TX)
        first_tiles(B2_SLAB, B2_TILE, B2_SLAB, B2_TILE, h_rhs, [TX, TX], False,
                    sem("h_ready"), KT * pre_nth((2, "premix")))
        for s in range(2, IN2_T):
            tile(B2_SLAB + s, B2_TILE + s, bank2(B2_TILE + s), (B2_SLAB + s) % RING, h_rhs, TX)
        pe.wait_ge(acc_free, B2_TILE + IN2_T)
        N = 4 * NH2
        for i in range(N + 6):
            if i < N:
                h, q = i // 4, i % 4
                a, hh = h // 8, h % 8
                qt, half = 12 * a + hh // 2, slice(64 * (hh % 2), 64 * (hh % 2) + 64)
                if i >= 2:
                    pe.wait_ge(sem("s2_ready"), i - 1)
                ht = 8 * a + hh // 2
                for z, (u, w) in enumerate(((qkh[half, ht, q * P:q * P + P], qkh[half, ht + 4, :]),
                                            (qkh[half, ht, q * P:q * P + P], px2r[half, qt + 4, :]),
                                            (px2r[half, qt, q * P:q * P + P], qkh[half, ht + 4, :]))):
                    m = pe.matmul(ps[:, i % 2, :], u, w, start=z == 0, stop=z == 2)
                m.then_inc(sem("s2_done"), 1)
                if i in V_STEPS:
                    v = V_STEPS.index(i)
                    if v:
                        pe.wait_ge(sem("vt2_ready"), v)
                    for tt in range(4):
                        m = pe.transpose(ps[:, 4, tt * P:tt * P + P], px2[:, 12 * (v // 4) + 8 + v % 4, tt * P:tt * P + P],
                                         ident[:, :])
                    m.then_inc(sem("vt2_done"), 1)
            if 2 <= i < N + 2:
                pe.wait_ge(sem("p2_ready"), i - 1)
                if i >= 4:
                    pe.wait_ge(sem("pt2_ready"), i - 3)
                for c in range(4):
                    m = pe.matmul(ps[:, 2 + i % 2, c * P:c * P + P], p2[:, (i - 2) % 3, c * P:c * P + P],
                                  diag[:, i % 2, :], start=True, stop=True)
                m.then_inc(sem("t2_done"), 1)
            if i >= 6:
                h, c = (i - 6) // 4, (i - 6) % 4
                g, tl = h % 2, h // 2
                if c == 0:
                    pe.wait_ge(sem("pt2_ready"), 4 * h + 4)
                    pe.wait_ge(sem("vt2_ready"), tl + 1)
                    if tl >= 2 and g == 0:
                        pe.wait_ge(sem("o2_out"), tl - 1)
                for z, (u, w) in enumerate(((vt2h, pt2h), (vt2h, pt2l), (vt2l, pt2h))):
                    m = pe.matmul(ps[:, 6 + tl % 2, :], u[:, tl % 2, g, c, :], w[:, h % 2, c, :],
                                  start=g == 0 and c == 0 and z == 0, stop=g == 1 and c == 3 and z == 2)
                if c == 3:
                    m.then_inc(sem("o2_done"), 1)
        for a in range(2):
            pe.wait_ge(sem("o2_out"), 8)
            for k in range(4):
                pe.wait_ge(sem("osq_ready"), 4 * a + k + 1)
                pe.matmul(ps[:, 4 + a, :], ones[:, :], nsq2[:, k % 2, :], start=k == 0, stop=k == 3)\
                  .then_inc(sem("osq_used"), 1)
        n, t = B2_SLAB + IN2_T, B2_TILE + IN2_T
        first_tiles(n, t, n, t, h_rhs, [TX, TX], False, sem("out_h_ready"), 0)
        for s in range(2, OUT_T):
            n, t = B2_SLAB + IN2_T + s, B2_TILE + IN2_T + s
            tile(n, t, bank2(t), n % RING, h_rhs, TX)
        squares((2, "preffn"), TX)
        spread((2, "preffn"), TX)
        pe.wait_ge(sem("h_ready"), KT * pre_nth((2, "preffn")) + KT)
        pe.wait_ge(sem("router_in"), 48)
        for tt in range(4):
            for k in range(KT):
                m = pe.matmul(ps[:, 7, tt * 32:tt * 32 + 20], hf2[:, k, tt * P:tt * P + P], wgr[:, k, :],
                              start=k == 0, stop=k == KT - 1)
        m.then_inc(sem("logits_done"), 1)
        pe.wait_ge(sem("comb_tok"), 1)
        for tt in range(4):
            m = pe.transpose(ps[0:16, 6, tt * P:tt * P + P], rt[:, 0, tt, :], ident[:, :])
        m.then_inc(sem("combT_done"), 1)
        pe.wait_ge(sem("combT_ready"), 1)
        for e in range(NEXP):
            if e >= 2:
                pe.wait_ge(sem("comb_ready"), e - 1)
            pe.matmul(ps[:, 6 + e % 2, :], esel[:, e, :], cmbT[:, :], start=True, stop=True)\
              .then_inc(sem("comb_done"), 1)
        E0, G0 = B2_SLAB + IN2_T + OUT_T, B2_TILE + IN2_T + OUT_T
        with pe.Fori(0, MOE_TURNS) as i:
            for s in range(MOE_UP):
                tile(i * MOE_SLABS + (E0 + s), i * MOE_SLABS + (G0 + s), bank2(G0 + s), (E0 + s) % RING, h_rhs, TX)
            pe.wait_ge(sem("eact_ready"), 2 * EPI * i + 2 * EPI)
            for o in range(KT):
                s = MOE_UP + o
                tile(i * MOE_SLABS + (E0 + s), i * MOE_SLABS + (G0 + s), bank2(G0 + s), (E0 + s) % RING,
                     lambda k: (ehi[:, k, :], elo[:, k, :]), TX)
        squares((2, "final"), TX)
        spread((2, "final"), TX)

    @block.scalar
    def _(act):
        def whi_split(n_expr, n_mod, landed, first=False):
            act.wait_ge(raw[n_mod], landed)
            if not first:
                act.wait_ge(slab_done, n_expr - 2)
            act.activation(whi[:, n_mod, :], wraw[:, n_mod, :], ACT.Copy).then_inc(hi_split, 1)

        def split(n):
            if n < N_SLABS:
                whi_split(n, n % RING, 16 * (n // RING + 1), n < RING)

        def split_in(i, per, n):
            whi_split(i * per + n, n % RING, i * (16 * per // RING) + 16 * (n // RING + 1))

        def rms(key, width):
            act.activation(rcol[:, 0:width // P], ps[:, 5, 0:width // P], ACT.Sqrt, bias=eps_c, scale=1.0 / D)\
               .then_inc(sem("std_ready"), 1)

        def norm_stats(key, src, width, ready=None, before=0):
            for k in range(KT):
                if ready is not None:
                    act.wait_ge(ready, before + k + 1)
                if k >= 2:
                    act.wait_ge(sem("sq_used"), KT * sq_nth(key) + k - 1)
                act.activation(nsq[:, k % 2, 0:width], src[:, k, 0:width], ACT.Square)\
                   .then_inc(sem("sq_ready"), 1)
            act.wait_ge(sem("sq_used"), KT * sq_nth(key) + KT)
            rms(key, width)

        def summed_rms(key, width):
            act.wait_ge(sem("ysum_used"), sum_nth(key) + 1)
            rms(key, width)

        def norm_apply(key, width, afn, bfn):
            for k in range(KT):
                act.wait_ge(sem("scaled_ready"), KT * pre_nth(key) + k + 1)
                if k >= 2:
                    act.wait_ge(sem("h_ready"), KT * pre_nth(key) + k - 1)
                for c0, w, b in segs[width]:
                    act.activation(nfull[:, k % 2, c0:c0 + w], nt[:, k % 2, c0:c0 + w], ACT.Identity,
                                   bias=bfn(k, b), scale=afn(k, b))
                for c0, w, b in segs[width]:
                    m = act.activation(hhi[:, k, c0:c0 + w], nt[:, k % 2, c0:c0 + w], ACT.Identity,
                                       bias=bfn(k, b), scale=afn(k, b))
                m.then_inc(sem("full_ready"), 1)

        act.wait_ge(small_in, 32)
        act.activation(cs[:, :, :], cs[:, :, :], ACT.Silu).then_inc(sem("c_silu"), 1)
        act.wait_ge(sem("c_silu"), 1)
        act.activation(csr[:, :, 0:2], cs[:, :, :], ACT.Copy).then_inc(sem("c_hi"), 1)

        def rows(i, g):
            act.wait_ge(mod_used, MOD_RING * i + MOD_GROUP * (g + 1))
            act.activation(mrow[:, g, :], ps[0:4, g, :], ACT.Copy).then_inc(sem("mod_rows"), 1)

        def mod_turn(i, first):
            for n in range(MOD_RING):
                act.wait_ge(mod_landed[n], 16 * i + 16)
                if not first or n >= MOD_SPLIT:
                    act.wait_ge(mod_used, MOD_RING * i + (n + 1 - MOD_SPLIT))
                act.activation(mhi[:, n % MOD_SPLIT, :], mraw[:, n, :], ACT.Copy).then_inc(sem("mod_hi"), 1)
                if n == 1 and not first:
                    rows(i - 1, 2)
                if n == 5 or n == 9:
                    rows(i, n // MOD_GROUP - 1)

        MOD_TURNS = MOD_SLABS // MOD_RING
        mod_turn(0, True)
        act.wait_ge(consts_in, 16 * N_CONST)
        for k in range(KT):
            if k >= 2:
                act.wait_ge(sem("ysq_used"), k - 1)
            act.activation(ysq[:, k % 2, :], x[:, k, :], ACT.Square).then_inc(sem("ysq_ready"), 1)
        with act.Fori(1, MOD_TURNS) as i:
            mod_turn(i, False)
        rows(MOD_TURNS - 1, 2)
        summed_rms((0, "premix"), T)
        for n in range(RING):
            split(n)

        def mods(L, a, b):
            return (lambda k, s: mv[:, L, a, k, s:s + 1]), (lambda k, s: mod[:, L, b * KT + k, s:s + 1])

        for L in range(DEPTH):
            S0, T0 = L * LAYER_SLABS, L * LAYER_TILES
            if L == 0:
                act.wait_ge(sem("mv_ready"), 1)
            else:
                norm_stats((L, "premix"), x, T, sem("x_ready"), KT * post_nth((L - 1, "postffn")))
            norm_apply((L, "premix"), T, *mods(L, 0, 0))
            act.wait_ge(sem("h_ready"), KT * pre_nth((L, "premix")) + KT)
            act.dma_start(cosx[:, :, :], dram["rope"]).then_inc(sem("rope_in"), 16)
            act.dma_start(fl5[:, :, :, :], dram["four512"]).then_inc(sem("ftab_in", L), 16)
            act.dma_start(wfo[:, :, :], dram["w_four"][L]).then_inc(sem("ftab_in", L), 16)
            act.dma_start(fch[:, :], dram["fourch"]).then_inc(sem("ftab_in", L), 16)
            if L == 0:
                act.dma_start(fl2[:, :, :, :], dram["four256"]).then_inc(sem("ftab_in", L), 16)

            def head_std(j):
                w = in_width(L, j)
                act.wait_ge(sem("qss_ready"), 5 * L + j + 1)
                if j >= 2:
                    act.wait_ge(sem("qn_ready"), 5 * L + j - 1)
                act.activation(qrs[:, j % 2, 0:w], psf[:, 3072:3072 + w], ACT.Sqrt, bias=eps_c, scale=1.0 / HD)\
                   .then_inc(sem("qstd_ready"), 1)

            for s in range(IN_T):
                w, b = in_width(L, s), bank2(T0 + s)
                act.wait_ge(slab_done, S0 + s + 1)
                src = psf[:, b * 512:b * 512 + w]
                if s < 6:
                    if s < 5:
                        if s >= 1:
                            act.wait_ge(sem("qss_ready"), 5 * L + s)
                        act.activation(qsq[:, 0:w], src, ACT.Square).then_inc(sem("qsq_ready"), 1)
                    act.activation(pxq[:, IN_DST[s], 0:w], src, ACT.Copy).then_inc(acc_free, 1)
                elif s < 8:
                    act.activation(pxf[:, s - 6, 0:w], src, ACT.Copy).then_inc(acc_free, 1)
                else:
                    t = s - 8
                    v = V_HYC + L * V_LAYER + 4 * t
                    act.activation(pxh[:, t, 0:w], src, ACT.Identity, bias=vec[:, v + 3:v + 4],
                                   scale=vec[:, v + 1:v + 2]).then_inc(sem("hyc_mid"), 1)
                split(S0 + s + RING)
                if 1 <= s <= 5:
                    head_std(s - 1)
            fseg = hsegs[L]
            ntt = 6 if L == 0 else 4
            for tt in range(ntt):
                act.wait_ge(sem("fst1"), T // P * L + tt + 1)
                act.activation(fab[:, tt, :], ps[:, 6 + tt % 2, :], ACT.Copy).then_inc(sem("fab_ready"), 1)
            for j in range(5):
                w = in_width(L, j)
                act.wait_ge(sem("k_roped"), 5 * L + j + 1)
                act.activation(hhi[:, QK_H[j], 0:w], pxq[:, IN_DST[j], 0:w], ACT.Copy, scale=-SCALE if j else 1.0)\
                   .then_inc(sem("qk_hi"), 1)
            n = 0
            for f in range(2):
                for s, c0, nt_ in fseg:
                    n += 1
                    w = nt_ * P
                    act.wait_ge(sem("fst2"), 4 * L + n)
                    act.activation(fy[:, f, c0:c0 + w], ps[:, 6 + f, 0:w] if s == 0 else ps[:, 5 - f, 0:w],
                                   ACT.Copy).then_inc(sem("fy_ready"), 1)
            n = 0
            for o in range(2):
                for s, c0, nt_ in fseg:
                    n += 1
                    w = nt_ * P
                    act.wait_ge(sem("fst3"), 4 * L + n)
                    act.activation(hhi[:, 4 + o, c0:c0 + w], ps[:, 6 + o, 0:w] if s == 0 else ps[:, 5 - o, 0:w],
                                   ACT.Copy).then_inc(sem("four_hi"), 1)
            act.wait_ge(sem("k_roped"), 5 * L + 5)
            act.dma_start(hw3[0:64, :], dram["hy_w3"][L]).then_inc(sem("hfil_in", L), 16)
            act.dma_start(hw12[0:33, 0:64], dram["hy_w1"][L]).then_inc(sem("hfil_in", L), 16)
            act.dma_start(hw12[0:64, 64:128], dram["hy_w2"][L]).then_inc(sem("hfil_in", L), 16)
            act.dma_start(hdel[:, :], dram["deltas"]).then_inc(sem("hfil_in", L), 16)
            act.dma_start(hz[0:33, :], dram["z512"]).then_inc(sem("hfil_in", L), 16)
            act.wait_ge(sem("vt_done"), L + 1)
            for g in range(2):
                h = slice(64 * g, 64 * g + 64)
                m = act.activation(vth[:, g, :, h], psf[:, 2048:2048 + 768].rearrange("p (t n) -> p t n", t=6)[:, :, h],
                                   ACT.Copy)
            m.then_inc(sem("pt_hi"), 1)
            steps = attn_steps(L)
            hv, before = halves(L)
            shares = output_shares(L)
            N = len(steps)
            heads = 0
            for i in range(max(shares) + 1):
                if i < N:
                    nk = len(steps[i][4]) * P
                    act.wait_ge(sem("min_ready"), STEPS0 * L + i + 1)
                    if i >= 3:
                        act.wait_ge(sem("t_ready"), HALVES0 * L + before[i - 2])
                    act.activation(pr[:, i % 3, 0:nk], psf[:, 1024 * (i % 2):1024 * (i % 2) + nk], ACT.Exp,
                                   bias=stat[:, i % 2, 0:1], scale=-1.0, accum_out=stat[:, i % 2, 1:2])\
                       .then_inc(sem("exp_done"), 1)
                if i in shares and shares[i][4] and steps[shares[i][1]][1] == 1:
                    j, g, q0, k0, kts, last = steps[shares[i][1]]
                    nq = TX if k0 == 0 else TC
                    ht = j + (NQT if k0 else 0)
                    act.wait_ge(sem("o_ready"), 4 * NQT * L + 2 * ht + 2)
                    act.activation(hhi[:, j, k0:k0 + nq], ps[:, 6 + ht % 2, 0:nq], ACT.Copy)\
                       .then_inc(sem("attn_hi"), 1)
                if 1 <= i <= N:
                    j, g, q0, k0, kts, last = steps[i - 1]
                    if heads >= 2:
                        act.wait_ge(sem("o_ready"), 4 * NQT * L + heads - 1)
                    for n in range(before[i - 1], before[i]):
                        _, bank, c0, c1 = hv[n]
                        act.wait_ge(sem("t_ready"), HALVES0 * L + n + 1)
                        act.activation(pth[:, heads % 2, c0:c1, q0 - k0:q0 - k0 + P],
                                       ps[:, bank, 0:(c1 - c0) * P].rearrange("p (c n) -> p c n", n=P), ACT.Copy)\
                           .then_inc(sem("pt_hi"), 1)
                    if last:
                        heads += 1
            nht = NQT * (2 if L == 0 else 1)
            act.wait_ge(sem("attn_out"), 2 * NQT * L + nht)
            act.dma_start(hd5[:, :, :, :], dram["hyf512"]).then_inc(sem("hfwd_in"), 16)
            act.dma_start(hi5[:, :, :, :], dram["hyi512"]).then_inc(sem("hinv_in"), 16)
            if L == 0:
                act.dma_start(hd2[:, :, :, :], dram["hy256"]).then_inc(sem("hd2_in", L), 16)
            for tt in range(ntt):
                act.wait_ge(sem("ut_done"), T // P * L + tt + 1)
                act.activation(hut[:, tt, :], ps[:, tt % 2, 0:256], ACT.Copy).then_inc(sem("ut_ready"), 1)
            for s, c0, nt_ in hsegs[L]:
                w = nt_ * P
                K = (L, s)
                if s == 1:
                    act.wait_ge(sem("h1_ready"), seg_nth(L, 0) + 1)
                    act.dma_start(hz[0:33, 0:TC], dram["z256"]).then_inc(sem("hfil_in", L), 16)
                for r in range(2):
                    act.wait_ge(sem("harg"), 2 * seg_nth(*K) + r + 1)
                    act.activation(hl[0:64, r, 0:w], hb[0:64, 0:w], ACT.Sin)\
                       .then_inc(sem("h1_sin" if r == 0 else "h2_sin"), 1)
                for q in range(nt_):
                    if q >= 1:
                        act.wait_ge(sem("hf_taken"), tile_nth(*K) + q)
                    act.activation(ha[:, 0:256], hdel[:, :], ACT.Exp, scale=consts[:, 2 + c0 // P + q:3 + c0 // P + q])\
                       .then_inc(sem("dec_ready"), 1)
                for f in range(nt_):
                    act.wait_ge(sem("hk_ready"), tile_nth(*K) + f + 1)
                    act.activation(hsp[:, f, :], ps[:, 4 + f % 2, :], ACT.Copy).then_inc(sem("hsp_ready"), 1)
                for c in range(2):
                    act.wait_ge(sem("hyf"), 2 * seg_nth(*K) + c + 1)
                    act.activation(hhi[:, 6 + c, c0:c0 + w], hub[:, c, c0:c0 + w], ACT.Copy)\
                       .then_inc(sem("hy_hi"), 1)
            W = T if L == 0 else TX
            for s in range(OUT_T):
                act.wait_ge(slab_done, S0 + IN_T + s + 1)
                b = bank2(T0 + IN_T + s)
                if s >= 2:
                    act.wait_ge(sem("ysq_used"), KT * mix_nth(L) + s - 1)
                act.activation(ysq[:, s % 2, 0:W], psf[:, b * 512:b * 512 + W], ACT.Square)\
                   .then_inc(sem("ysq_ready"), 1)
                act.activation(y[:, s, 0:W], psf[:, b * 512:b * 512 + W], ACT.Copy).then_inc(acc_free, 1)
                split(S0 + IN_T + s + RING)
            summed_rms((L, "postmix"), W)
            norm_stats((L, "preffn"), x, W, sem("x_ready"), KT * post_nth((L, "postmix")))
            norm_apply((L, "preffn"), W, *mods(L, 2, 3))
            F0, G0 = S0 + IN_T + OUT_T, T0 + IN_T + OUT_T
            with act.Fori(0, CHUNKS) as i:
                act.wait_ge(sem("cconv_ready"), i + (L * CHUNKS + 1))
                for p in range(PAIRS):
                    for z in range(2):
                        s = 2 * p + z
                        b = bank2(G0 + s)
                        act.wait_ge(slab_done, i * FFN_SLABS + (F0 + s + 1))
                        act.activation(up[:, p % 2, z, 0:W], psf[:, b * 512:b * 512 + W], ACT.Identity,
                                       bias=cconv[:, s, 3:4], scale=cconv[:, s, 1:2]).then_inc(sem("up_mid"), 1)
                        split_in(i, FFN_SLABS, F0 + s + RING)
                    act.wait_ge(sem("gate_ready"), i * PAIRS + (L * CHUNKS * PAIRS + p + 1))
                    if p:
                        act.wait_ge(sem("act_ready"), i * PAIRS + (L * CHUNKS * PAIRS + p))
                    elif L:
                        act.wait_ge(sem("act_ready"), i * PAIRS + (L * CHUNKS * PAIRS))
                    act.activation(sil[:, 0:W], up[:, p % 2, 0, 0:W], ACT.Silu).then_inc(sem("silu_done"), 1)
                    act.wait_ge(sem("prod_ready"), i * PAIRS + (L * CHUNKS * PAIRS + p + 1))
                    act.activation(ahi[:, p, 0:W], sil[:, 0:W], ACT.Copy).then_inc(sem("ahi_ready"), 1)
                for o in range(KT):
                    for q in range(PAIRS * o // KT, PAIRS * (o + 1) // KT):
                        split_in(i, FFN_SLABS, F0 + UP_T + q + RING)
                    act.wait_ge(acc_free, i * FFN_TILES + (G0 + UP_T + o + 1))
                    if o >= 2:
                        act.wait_ge(sem("ysq_used"), i * KT + (KT * ffn_nth(L) + o - 1))
                    act.activation(ysq[:, o % 2, 0:W], y[:, o, 0:W], ACT.Square).then_inc(sem("ysq_ready"), 1)
            summed_rms((L, "postffn"), W)

        g2 = lambda v: ((lambda k, s: vec[:, v + k:v + k + 1]), (lambda k, s: zero_c))
        norm_stats((2, "premix"), x, TX, sem("x_ready"), KT * post_nth((1, "postffn")))
        norm_apply((2, "premix"), TX, *g2(V2_MIX))
        act.wait_ge(sem("h_ready"), KT * pre_nth((2, "premix")) + KT)
        act.dma_start(namask[:, :], dram["namask"]).then_inc(sem("namask_in"), 16)

        def load_table(h):
            if h >= 2:
                act.wait_ge(sem("s2_ready"), 4 * (h - 1))
            for a in range(2):
                half = slice(64 * a, 64 * a + 64)
                src = dram["alibi"][h, half, :] if h < 8 else dram["rpbw"][h - 8, :, (1 - a) * HD:(15 - a) * HD]
                act.dma_start(tab[half, h % 2, :], src).then_inc(sem("tab_in", h % 2), 16)

        load_table(0)
        load_table(1)
        for s in range(IN2_T):
            n, t = B2_SLAB + s, B2_TILE + s
            act.wait_ge(slab_done, n + 1)
            if s % 12 < 8:
                act.activation(qkh[:, 8 * (s // 12) + s % 12, :], ps[:, bank2(t), :], ACT.Copy,
                               scale=-SCALE if s % 12 < 4 else 1.0)\
                   .then_inc(sem("qk2_hi"), 1)
            split(n + RING)
        N = 4 * NH2
        for i in range(N + 6):
            if i < N:
                act.wait_ge(sem("s2_ready"), i + 1)
                if i >= 3:
                    act.wait_ge(sem("t2_done"), i - 2)
                act.activation(p2[:, i % 3, :], s2[:, i % 2, :], ACT.Exp, bias=stat[:, i % 2, 0:1], scale=-1.0,
                               accum_out=stat[:, i % 2, 1:2]).then_inc(sem("exp2_done"), 1)
                if i in V_STEPS:
                    v = V_STEPS.index(i)
                    act.wait_ge(sem("vt2_done"), v + 1)
                    if v >= 2:
                        act.wait_ge(sem("o2_done"), 2 * (v - 1))
                    for g in range(2):
                        h = slice(64 * g, 64 * g + 64)
                        m = act.activation(vt2h[:, v % 2, g, :, h],
                                           ps[:, 4, :].rearrange("p (t n) -> p t n", t=4)[:, :, h], ACT.Copy)
                    m.then_inc(sem("vt2_hi"), 1)
            if i >= 13 and (i - 13) % 8 == 0:
                tl = (i - 13) // 8
                act.wait_ge(sem("o2_done"), 2 * tl + 2)
                act.activation(px2[:, 12 * (tl // 4) + tl % 4, :], ps[:, 6 + tl % 2, :], ACT.Copy)\
                   .then_inc(sem("o2_out"), 1)
            if 1 <= i <= N:
                h = (i - 1) // 4
                act.wait_ge(sem("t2_done"), i)
                if h >= 2:
                    act.wait_ge(sem("o2_done"), h - 1)
                q = (i - 1) % 4
                act.activation(pt2h[:, h % 2, :, q * P:q * P + P],
                               ps[:, 2 + (i - 1) % 2, :].rearrange("p (c n) -> p c n", c=4), ACT.Copy)\
                   .then_inc(sem("pt2_hi"), 1)
                if q == 3 and h + 2 < NH2:
                    load_table(h + 2)
        act.wait_ge(sem("o2_out"), 8)
        for a in range(2):
            for k in range(4):
                q = 4 * a + k
                if q >= 2:
                    act.wait_ge(sem("osq_used"), q - 1)
                act.activation(nsq2[:, k % 2, :], px2[:, 12 * a + k, :], ACT.Square).then_inc(sem("osq_ready"), 1)
            act.wait_ge(sem("osq_used"), 4 * a + 4)
            act.activation(nrm2[:, a, :], ps[:, 4 + a, :], ACT.Sqrt, bias=eps_c, scale=1.0 / 512)\
               .then_inc(sem("ostd_ready"), 1)
        for k in range(KT):
            a = k // 4
            act.wait_ge(sem("ot_ready"), k + 1)
            src = px2[:, 12 * a + k % 4, :]
            act.activation(hhi[:, k, 0:TX], src, ACT.Copy).then_inc(sem("ohi_ready"), 1)
        for s in range(OUT_T):
            n, t = B2_SLAB + IN2_T + s, B2_TILE + IN2_T + s
            act.wait_ge(slab_done, n + 1)
            split(n + RING)
        act.dma_start(wgr[:, :, :], dram["wgr"]).then_inc(sem("router_in"), 16)
        act.dma_start(bgr[:, :], dram["bgr"]).then_inc(sem("router_in"), 16)
        act.dma_start(esel[:, :, :], dram["esel"]).then_inc(sem("router_in"), 16)
        key = (2, "preffn")
        norm_stats(key, x, TX, sem("x2_ready"))
        for k in range(KT):
            act.wait_ge(sem("scaled_ready"), KT * pre_nth(key) + k + 1)
            act.activation(hhi[:, k, 0:TX], hf2[:, k, :], ACT.Copy).then_inc(sem("full_ready"), 1)
        act.wait_ge(sem("g_ready"), 1)
        act.activation(rt[:, 3, :, 0:4], rt[:, 2, :, 0:4], ACT.Exp).then_inc(sem("g_exp"), 1)
        act.wait_ge(sem("e_ready"), 1)
        act.activation(rt[:, 9, :, 0:1], rt[:, 8, :, 0:1], ACT.Exp).then_inc(sem("e_exp"), 1)
        act.wait_ge(sem("combT_done"), 1)
        act.activation(cmbT[:, :], ps[0:16, 6, :], ACT.Copy).then_inc(sem("combT_ready"), 1)
        for e in range(NEXP):
            act.wait_ge(sem("comb_done"), e + 1)
            act.activation(comb[:, e, :], ps[:, 6 + e % 2, :], ACT.Copy).then_inc(sem("comb_ready"), 1)
        E0, G0 = B2_SLAB + IN2_T + OUT_T, B2_TILE + IN2_T + OUT_T

        def moe_turn(i, last):
            for p in range(2 * EPI):
                act.wait_ge(slab_done, i * MOE_SLABS + (E0 + 2 * p + 1))
                b = bank2(G0 + 2 * p)
                if p >= 2:
                    act.wait_ge(sem("eact_ready"), i * (2 * EPI) + (p - 1))
                act.activation(esil[:, p % 2, :], ps[:, b, :], ACT.Silu).then_inc(sem("esil_ready"), 1)
                split_in(i, MOE_SLABS, E0 + 2 * p + RING)
                split_in(i, MOE_SLABS, E0 + 2 * p + 1 + RING)
                act.wait_ge(sem("eprod_ready"), i * (2 * EPI) + (p + 1))
                act.activation(ehi[:, p, :], esil[:, p % 2, :], ACT.Copy).then_inc(sem("ehi_ready"), 1)
            for o in range(KT):
                if last and o + RING >= KT:
                    continue
                split_in(i, MOE_SLABS, E0 + MOE_UP + o + RING)

        with act.Fori(0, MOE_TURNS - 1) as i:
            moe_turn(i, False)
        moe_turn(MOE_TURNS - 1, True)
        act.wait_ge(sem("moe_done"), 1)
        norm_stats((2, "final"), x, TX)

    @block.vector
    def _(dve):
        def inverse_rms(key, width):
            dve.wait_ge(sem("std_ready"), nth(key) + 1)
            n = width // P
            dve.reciprocal(rcol[:, 0:n], rcol[:, 0:n])
            dve.drain()
            dve.tensor_tensor(rdiag[:, 0:n, :], ident[:, :].unsqueeze(1).to_broadcast([P, n, P]),
                              rcol[:, 0:n].unsqueeze(2).to_broadcast([P, n, P]), ALU.mult)\
               .then_inc(sem("rdiag_ready"), 1)
            dve.wait_ge(sem("r_ready"), nth(key) + 1)

        def add_squares(k, before, width):
            dve.wait_ge(sem("ysq_ready"), before + (k + 1))
            if k == 0:
                m = dve.tensor_copy(yacc[:, 0:width], ysq[:, 0, 0:width])
            else:
                m = dve.tensor_tensor(yacc[:, 0:width], yacc[:, 0:width], ysq[:, k % 2, 0:width], ALU.add)
            m.then_inc(sem("ysq_used"), 1)
            dve.drain()

        def norm_dve(key, src, width):
            inverse_rms(key, width)
            for k in range(KT + 1):
                if k < KT:
                    if k >= 2:
                        dve.wait_ge(sem("full_ready"), KT * pre_nth(key) + k - 1)
                    dve.tensor_tensor(nt[:, k % 2, 0:width], src[:, k, 0:width], rbc[:, 0:width], ALU.mult)\
                       .then_inc(sem("scaled_ready"), 1)
                if k >= 1:
                    dve.wait_ge(sem("full_ready"), KT * pre_nth(key) + k)
                    dve.tensor_tensor(hlo[:, k - 1, 0:width], nfull[:, (k - 1) % 2, 0:width],
                                      hhi[:, k - 1, 0:width].bitcast(F32), ALU.subtract)\
                       .then_inc(sem("h_ready"), 1)

        def post_norm(key, L, gate, width):
            inverse_rms(key, width)
            for k in range(KT + 1):
                if k < KT:
                    dve.tensor_tensor(y[:, k, 0:width], y[:, k, 0:width], rbc[:, 0:width], ALU.mult)
                if k:
                    for c0, w, b in segs[width]:
                        m = dve.scalar_tensor_tensor(x[:, k - 1, c0:c0 + w], y[:, k - 1, c0:c0 + w],
                                                     mv[:, L, gate, k - 1, b:b + 1], x[:, k - 1, c0:c0 + w],
                                                     ALU.mult, ALU.add)
                    m.then_inc(sem("x_ready"), 1)
                dve.drain()

        def shifts(dst, bank, width, w0, w2):
            for c0, w, b in segs[width]:
                dve.scalar_tensor_tensor(dst[:, c0 + 1:c0 + w], ps[:, bank + b, 0:w - 1], w0, dst[:, c0 + 1:c0 + w],
                                         ALU.mult, ALU.add)
            dve.drain()
            for c0, w, b in segs[width]:
                m = dve.scalar_tensor_tensor(dst[:, c0:c0 + w - 1], ps[:, bank + b, 1:w], w2, dst[:, c0:c0 + w - 1],
                                             ALU.mult, ALU.add)
            return m

        modf = mod[:, :, :, :].rearrange("p l t s -> p (l t s)")
        dve.wait_ge(sem("c_hi"), 1)
        dve.tensor_tensor(csr[:, :, 2:4], cs[:, :, :], csr[:, :, 0:2].bitcast(F32), ALU.subtract)\
           .then_inc(sem("c_split"), 1)

        def bias(i):
            GW = 2 * MOD_RING
            dve.wait_ge(sem("mod_turned"), i + 1)
            part = bass.ds(i * GW, GW)
            dve.tensor_tensor(modf[:, part], ps[:, 3, 0:GW], bmod[:, part], ALU.add).then_inc(sem("mod_taken"), 1)

        def mod_turn(i, first):
            for n in range(MOD_RING):
                dve.wait_ge(sem("mod_hi"), MOD_RING * i + (n + 1))
                dve.tensor_tensor(mlo[:, n % MOD_SPLIT, :], mraw[:, n, :], mhi[:, n % MOD_SPLIT, :].bitcast(F32),
                                  ALU.subtract).then_inc(sem("mod_lo"), 1)
                if n == 6 and not first:
                    bias(i - 1)

        MOD_TURNS = MOD_SLABS // MOD_RING
        mod_turn(0, True)
        dve.wait_ge(consts_in, 16 * N_CONST)
        for k in range(KT):
            add_squares(k, 0, T)
        dve.drain().then_inc(sem("ysum_ready"), 1)
        with dve.Fori(1, MOD_TURNS) as i:
            mod_turn(i, False)
        bias(MOD_TURNS - 1)
        dve.drain()
        for L in range(DEPTH):
            for s in range(2):
                for q, (g, mt, plus) in enumerate(((V_GPM, 1, 1.0), (V_GQM, 2, 0.0), (V_GPF, 4, 1.0), (V_GQF, 5, 0.0))):
                    g += L * V_LAYER
                    m = dve.scalar_tensor_tensor(mv[:, L, q, :, s], mod[:, L, mt * KT:(mt + 1) * KT, s], plus,
                                                 vec[:, g:g + KT], ALU.add, ALU.mult)
        m.then_inc(sem("mv_ready"), 1)

        for L in range(DEPTH):
            S0, T0 = L * LAYER_SLABS, L * LAYER_TILES
            V0 = L * V_LAYER
            norm_dve((L, "premix"), x, T)

            def head_norm(j):
                w = in_width(L, j)
                dve.wait_ge(sem("qstd_ready"), 5 * L + j + 1)
                dve.reciprocal(qrs[:, j % 2, 0:w], qrs[:, j % 2, 0:w])
                dve.drain()
                g = V0 + (V_GK if j == 0 else V_GQ)
                dve.scalar_tensor_tensor(pxq[:, IN_DST[j], 0:w], pxq[:, IN_DST[j], 0:w], vec[:, g:g + 1],
                                         qrs[:, j % 2, 0:w], ALU.mult, ALU.mult).then_inc(sem("qn_ready"), 1)

            for j in range(5):
                head_norm(j)
            for s in range(8, IN_T):
                t = s - 8
                v = V0 + V_HYC + 4 * t
                dve.wait_ge(sem("hyc_mid"), NHY * L + t + 1)
                shifts(pxh[:, t, :], bank2(T0 + s), in_width(L, s), vec[:, v:v + 1], vec[:, v + 2:v + 3])\
                    .then_inc(acc_free, 1)
            dve.wait_ge(sem("rope_in"), 16 * L + 16)
            for j in range(5):
                q = pxq[:, IN_DST[j], 0:TX]
                dve.wait_ge(sem("rot_ready"), 5 * L + j + 1)
                dve.tensor_tensor(qtmp[:, :], ps[:, j, :], cosx[:, 1, :], ALU.mult)
                dve.tensor_tensor(q, q, cosx[:, 0, :], ALU.mult)
                dve.drain()
                dve.tensor_tensor(q, q, qtmp[:, :], ALU.add).then_inc(sem("k_roped"), 1)
                dve.drain()
            for j in range(5):
                w = in_width(L, j)
                dve.wait_ge(sem("qk_hi"), 5 * L + j + 1)
                dve.scalar_tensor_tensor(hlo[:, QK_H[j], 0:w], pxq[:, IN_DST[j], 0:w], -SCALE if j else 1.0,
                                         hhi[:, QK_H[j], 0:w].bitcast(F32), ALU.mult, ALU.subtract)\
                   .then_inc(sem("qk_lo"), 1)
            W = T if L == 0 else TX
            for c in range(2):
                m = dve.tensor_tensor(pxh[:, 2 + c, 0:W], pxh[:, 2 + c, 0:W], pxh[:, 4 + c, 0:W], ALU.mult)
            m.then_inc(sem("u_ready"), 1)
            dve.drain()
            for c in range(2):
                bv = V0 + V_HYB + c
                dve.tensor_scalar(hub[:, c, 0:W], pxh[:, 2 + c, 0:W], vec[:, bv:bv + 1], None, ALU.mult)
            fseg = hsegs[L]
            n = 0
            for o in range(2):
                for s, c0, nt_ in fseg:
                    n += 1
                    w = nt_ * P
                    dve.wait_ge(sem("four_hi"), 4 * L + n)
                    dve.tensor_tensor(hlo[:, 4 + o, c0:c0 + w],
                                      ps[:, 6 + o, 0:w] if s == 0 else ps[:, 5 - o, 0:w],
                                      hhi[:, 4 + o, c0:c0 + w].bitcast(F32), ALU.subtract)\
                       .then_inc(sem("four_out"), 1)
            dve.wait_ge(sem("pt_hi"), (HALVES0 + 1) * L + 1)
            for g in range(2):
                h, other = slice(64 * g, 64 * g + 64), slice(64 - 64 * g, 128 - 64 * g)
                dve.memset(vth[:, g, :, other].bitcast(F32), 0.0)
                dve.memset(vtl[:, g, :, other].bitcast(F32), 0.0)
                m = dve.tensor_tensor(vtl[:, g, :, h], psf[:, 2048:2048 + 768].rearrange("p (t n) -> p t n", t=6)[:, :, h],
                                      vth[:, g, :, h].bitcast(F32), ALU.subtract)
            m.then_inc(sem("pt_lo"), 1)
            steps = attn_steps(L)
            hv, before = halves(L)
            shares = output_shares(L)
            N = len(steps)
            heads = 0
            for i in range(max(shares) + 1):
                if i < N:
                    nk = len(steps[i][4]) * P
                    dve.wait_ge(sem("s_ready"), STEPS0 * L + i + 1)
                    dve.tensor_reduce(stat[:, i % 2, 0:1], psf[:, 1024 * (i % 2):1024 * (i % 2) + nk], AX_X, ALU.min)\
                       .then_inc(sem("min_ready"), 1)
                if 1 <= i <= N:
                    z = (i - 1) % 2
                    dve.wait_ge(sem("exp_done"), STEPS0 * L + i)
                    dve.reciprocal(stat[:, z, 2:3], stat[:, z, 1:2])
                    dve.drain()
                    dve.tensor_scalar(diag[:, z, :], ident[:, :], stat[:, z, 2:3], None, ALU.mult)\
                       .then_inc(sem("p_ready"), 1)
                if 2 <= i < N + 2:
                    j, g, q0, k0, kts, last = steps[i - 2]
                    for n in range(before[i - 2], before[i - 1]):
                        _, bank, c0, c1 = hv[n]
                        dve.wait_ge(sem("pt_hi"), (HALVES0 + 1) * L + 1 + n + 1)
                        dve.tensor_tensor(ptl[:, heads % 2, c0:c1, q0 - k0:q0 - k0 + P],
                                          ps[:, bank, 0:(c1 - c0) * P].rearrange("p (c n) -> p c n", n=P),
                                          pth[:, heads % 2, c0:c1, q0 - k0:q0 - k0 + P].bitcast(F32), ALU.subtract)\
                           .then_inc(sem("pt_lo"), 1)
                    if last:
                        heads += 1
                if i in shares and shares[i][4] and steps[shares[i][1]][1] == 1:
                    j, g, q0, k0, kts, last = steps[shares[i][1]]
                    nq = TX if k0 == 0 else TC
                    ht = j + (NQT if k0 else 0)
                    dve.wait_ge(sem("attn_hi"), 2 * NQT * L + ht + 1)
                    dve.tensor_tensor(hlo[:, j, k0:k0 + nq], ps[:, 6 + ht % 2, 0:nq],
                                      hhi[:, j, k0:k0 + nq].bitcast(F32), ALU.subtract).then_inc(sem("attn_out"), 1)
            for s, c0, nt_ in hsegs[L]:
                w = nt_ * P
                K = (L, s)
                for r in range(2):
                    m0 = V0 + V_MLP + 2 * r
                    dve.wait_ge(sem("h1_ready" if r == 0 else "h2_ready"), seg_nth(*K) + 1)
                    if r == 1:
                        dve.wait_ge(sem("h1_sin"), seg_nth(*K) + 1)
                    a, b = ha[0:64, 0:w], hb[0:64, 0:w]
                    dve.tensor_scalar(a, ps[0:64, 2 + r, 0:w], vec[0:64, m0:m0 + 1], vec[0:64, m0 + 1:m0 + 2],
                                      ALU.add, ALU.mult)
                    dve.drain()
                    dve.tensor_scalar(b, a, 1 / (2 * math.pi), MAGIC, ALU.mult, ALU.add)
                    dve.drain()
                    dve.tensor_scalar(b, b, MAGIC, None, ALU.subtract)
                    dve.drain()
                    dve.scalar_tensor_tensor(a, b, -TWO_PI_HI, a, ALU.mult, ALU.add)
                    dve.drain()
                    dve.scalar_tensor_tensor(a, b, -TWO_PI_LO, a, ALU.mult, ALU.add)
                    dve.drain()
                    dve.tensor_scalar(b, a, PI_IN, -PI_IN, ALU.min, ALU.max).then_inc(sem("harg"), 1)
                for q in range(nt_):
                    dve.wait_ge(sem("hf_ready"), tile_nth(*K) + q + 1)
                    dve.wait_ge(sem("dec_ready"), tile_nth(*K) + q + 1)
                    if q == 0:
                        dve.wait_ge(sem("h2_sin"), seg_nth(*K) + 1)
                        dve.memset(hsum[:, :], 0.0)
                    dve.tensor_tensor(hb[:, 0:256], ps[:, q % 2, 0:256], ha[:, 0:256], ALU.mult)
                    dve.tensor_tensor(hb[:, 256:512], ps[:, q % 2, 256:512], ha[:, 0:256], ALU.mult)\
                       .then_inc(sem("hf_taken"), 1)
                    dve.drain()
                    if q == 0:
                        dve.memset(hb[0:1, 256:512], 0.0)
                        dve.drain()
                    dve.tensor_tensor(hpm[:, q, 0:256], hb[:, 0:256], hb[:, 256:512], ALU.add)
                    dve.tensor_tensor(hpm[:, q, 256:512], hb[:, 0:256], hb[:, 256:512], ALU.subtract)
                    dve.scalar_tensor_tensor(hsp[:, 3, :], hb[:, :], -1.0, hb[:, :], ALU.mult, ALU.max)
                    dve.drain()
                    dve.tensor_tensor(hsum[:, :], hsum[:, :], hsp[:, 3, 0:256], ALU.add)
                    dve.drain()
                    m = dve.tensor_tensor(hsum[:, :], hsum[:, :], hsp[:, 3, 256:512], ALU.add)
                    if q == nt_ - 1:
                        m.then_inc(sem("hsum_ready"), 1)
                    dve.drain()
                dve.wait_ge(sem("hn_ready"), seg_nth(*K) + 1)
                dve.reciprocal(rnorm[:, :], ps[:, 2, 0:2])
                for f in range(nt_):
                    dve.wait_ge(sem("hu_ready"), tile_nth(*K) + f + 1)
                    dve.wait_ge(sem("hsp_ready"), tile_nth(*K) + f + 1)
                    u = 6 + f % 2
                    dve.tensor_tensor(hb[:, :], hsp[:, f, :], ps[:, u, :], ALU.mult)
                    dve.tensor_tensor(ha[:, 0:256], hsp[:, f, 0:256], ps[:, u, 256:512], ALU.mult)
                    dve.tensor_tensor(ha[:, 256:512], hsp[:, f, 256:512], ps[:, u, 0:256], ALU.mult)
                    dve.drain()
                    dve.tensor_tensor(hys[:, f, 0:256], hb[:, 0:256], hb[:, 256:512], ALU.subtract)
                    dve.tensor_tensor(hys[:, f, 256:512], ha[:, 0:256], ha[:, 256:512], ALU.add)\
                       .then_inc(sem("hys_ready"), 1)
                    dve.drain()
                for c in range(2):
                    dst = hub[:, c, c0:c0 + w]
                    dve.wait_ge(sem("hy_ready"), 2 * seg_nth(*K) + c + 1)
                    dve.scalar_tensor_tensor(dst, ps[:, c, 0:w], rnorm[:, c:c + 1], dst, ALU.mult, ALU.add)
                    dve.drain()
                    dve.tensor_tensor(dst, dst, pxh[:, c, c0:c0 + w], ALU.mult).then_inc(sem("hyf"), 1)
                for c in range(2):
                    dve.wait_ge(sem("hy_hi"), 2 * seg_nth(*K) + c + 1)
                    dve.tensor_tensor(hlo[:, 6 + c, c0:c0 + w], hub[:, c, c0:c0 + w],
                                      hhi[:, 6 + c, c0:c0 + w].bitcast(F32), ALU.subtract).then_inc(sem("hy_out"), 1)
            for s in range(OUT_T):
                add_squares(s, KT * mix_nth(L), W)
            dve.drain().then_inc(sem("ysum_ready"), 1)
            post_norm((L, "postmix"), L, 1, W)
            norm_dve((L, "preffn"), x, W)
            dve.memset(y[:, :, 0:W], 0.0)
            F0, G0 = S0 + IN_T + OUT_T, T0 + IN_T + OUT_T
            with dve.Fori(0, CHUNKS) as i:
                dve.wait_ge(acc_free, i * FFN_TILES + G0)
                dve.tensor_scalar(cconv[:, :, :].rearrange("p t v -> p (t v)"),
                                  vec[:, bass.ds(i * (UP_T * 4) + (V0 + V_FFC), UP_T * 4)], 1.0, None, ALU.mult)\
                   .then_inc(sem("cconv_ready"), 1)
                dve.drain()
                B = L * CHUNKS * PAIRS
                for p in range(PAIRS):
                    for z in range(2):
                        s = 2 * p + z
                        dve.wait_ge(sem("up_mid"), i * UP_T + (2 * B + s + 1))
                        shifts(up[:, p % 2, z, :], bank2(G0 + s), W, cconv[:, s, 0:1], cconv[:, s, 2:3])\
                            .then_inc(acc_free, 1)
                        if z == 0:
                            dve.drain().then_inc(sem("gate_ready"), 1)
                    dve.drain()
                    dve.wait_ge(sem("silu_done"), i * PAIRS + (B + p + 1))
                    dve.tensor_tensor(sil[:, 0:W], sil[:, 0:W], up[:, p % 2, 1, 0:W], ALU.mult)\
                       .then_inc(sem("prod_ready"), 1)
                    dve.wait_ge(sem("ahi_ready"), i * PAIRS + (B + p + 1))
                    dve.tensor_tensor(alo[:, p, 0:W], sil[:, 0:W], ahi[:, p, 0:W].bitcast(F32), ALU.subtract)\
                       .then_inc(sem("act_ready"), 1)
                for o in range(KT):
                    b = bank2(G0 + UP_T + o)
                    if o < KT - 1:
                        dve.wait_ge(down_ready, i * (KT - 1) + (L * CHUNKS * (KT - 1) + o + 1))
                    else:
                        dve.wait_ge(slab_done, i * FFN_SLABS + (F0 + FFN_SLABS))
                    dve.tensor_tensor(y[:, o, 0:W], y[:, o, 0:W], psf[:, b * 512:b * 512 + W], ALU.add)\
                       .then_inc(acc_free, 1)
                    if o:
                        add_squares(o - 1, i * KT + KT * ffn_nth(L), W)
                add_squares(KT - 1, i * KT + KT * ffn_nth(L), W)
            dve.drain().then_inc(sem("ysum_ready"), 1)
            post_norm((L, "postffn"), L, 3, W)

        norm_dve((2, "premix"), x, TX)
        for s in range(IN2_T):
            n, t = B2_SLAB + s, B2_TILE + s
            if s % 12 < 8:
                dve.wait_ge(sem("qk2_hi"), 8 * (s // 12) + s % 12 + 1)
                dve.scalar_tensor_tensor(px2r[:, s, :], ps[:, bank2(t), :], -SCALE if s % 12 < 4 else 1.0,
                                         qkh[:, 8 * (s // 12) + s % 12, :].bitcast(F32), ALU.mult, ALU.subtract)\
                   .then_inc(acc_free, 1)
            else:
                dve.wait_ge(slab_done, n + 1)
                dve.tensor_copy(px2[:, s, :], ps[:, bank2(t), :]).then_inc(acc_free, 1)
        for v in range(2):
            for g in range(2):
                other = slice(64 - 64 * g, 128 - 64 * g)
                dve.memset(vt2h[:, v, g, :, other].bitcast(F32), 0.0)
                dve.memset(vt2l[:, v, g, :, other].bitcast(F32), 0.0)
        dve.wait_ge(sem("namask_in"), 16)
        def prob_low(i):
            h, q = i // 4, i % 4
            dve.wait_ge(sem("pt2_hi"), i + 1)
            dst = pt2h[:, h % 2, :, q * P:q * P + P]
            dve.tensor_tensor(pt2l[:, h % 2, :, q * P:q * P + P],
                              ps[:, 2 + i % 2, :].rearrange("p (c n) -> p c n", c=4), dst.bitcast(F32),
                              ALU.subtract).then_inc(sem("pt2_ready"), 1)

        def divisor(i):
            dve.wait_ge(sem("exp2_done"), i + 1)
            dve.reciprocal(stat[:, i % 2, 2:3], stat[:, i % 2, 1:2])
            dve.drain()
            dve.tensor_scalar(diag[:, i % 2, :], ident[:, :], stat[:, i % 2, 2:3], None, ALU.mult)\
               .then_inc(sem("p2_ready"), 1)

        for i in range(4 * NH2):
            h, q = i // 4, i % 4
            tb = tab[:, h % 2, :]
            if q == 0:
                dve.wait_ge(sem("tab_in", h % 2), 32 * (h // 2 + 1))
                dve.drain()
            dve.wait_ge(sem("s2_done"), i + 1)
            if i >= 2:
                dve.wait_ge(sem("exp2_done"), i - 1)
            o = (3 - q) * P
            dve.tensor_tensor_reduce(s2[:, i % 2, :], ps[:, i % 2, :], tb[:, o:o + TX], 1.0, 3e38, ALU.add, ALU.min,
                                     stat[:, i % 2, 0:1]).then_inc(sem("s2_ready"), 1)
            if i:
                divisor(i - 1)
            if i >= 2:
                prob_low(i - 2)
            if i in V_STEPS:
                v = V_STEPS.index(i)
                dve.wait_ge(sem("vt2_hi"), v + 1)
                for g in range(2):
                    c = slice(64 * g, 64 * g + 64)
                    m = dve.tensor_tensor(vt2l[:, v % 2, g, :, c],
                                          ps[:, 4, :].rearrange("p (t n) -> p t n", t=4)[:, :, c],
                                          vt2h[:, v % 2, g, :, c].bitcast(F32), ALU.subtract)
                m.then_inc(sem("vt2_ready"), 1)
            if q == 2 and 8 <= h + 1 < NH2:
                dve.wait_ge(sem("tab_in", (h + 1) % 2), 32 * ((h + 1) // 2 + 1))
                t3 = tab[:, (h + 1) % 2, :].rearrange("p (r c) -> p r c", c=HD)
                dve.tensor_tensor(t3, namask[:, :].unsqueeze(1).to_broadcast([P, TABW // HD, HD]), t3, ALU.subtract)
        divisor(4 * NH2 - 1)
        prob_low(4 * NH2 - 2)
        prob_low(4 * NH2 - 1)
        for a in range(2):
            dve.wait_ge(sem("ostd_ready"), a + 1)
            dve.reciprocal(nrm2[:, a, :], nrm2[:, a, :])
            dve.drain()
            for k in range(4 * a, 4 * a + 4):
                src = px2[:, 12 * a + k % 4, :]
                dve.scalar_tensor_tensor(src, src, vec[:, V2_OUT + k:V2_OUT + k + 1], nrm2[:, a, :],
                                         ALU.mult, ALU.mult).then_inc(sem("ot_ready"), 1)
        dve.drain()
        for k in range(KT):
            dve.wait_ge(sem("ohi_ready"), k + 1)
            dve.tensor_tensor(hlo[:, k, 0:TX], px2[:, 12 * (k // 4) + k % 4, :], hhi[:, k, 0:TX].bitcast(F32),
                              ALU.subtract).then_inc(sem("out_h_ready"), 1)
        for s in range(OUT_T):
            n, t = B2_SLAB + IN2_T + s, B2_TILE + IN2_T + s
            dve.wait_ge(slab_done, n + 1)
            dve.tensor_tensor(x[:, s, 0:TX], x[:, s, 0:TX], ps[:, bank2(t), :], ALU.add).then_inc(acc_free, 1)
            dve.drain().then_inc(sem("x2_ready"), 1)
        K = (2, "preffn")
        inverse_rms(K, TX)
        for k in range(KT):
            dve.scalar_tensor_tensor(hf2[:, k, :], x[:, k, 0:TX], vec[:, V2_FFN + k:V2_FFN + k + 1], rbc[:, 0:TX],
                                     ALU.mult, ALU.mult).then_inc(sem("scaled_ready"), 1)
        dve.drain()
        for k in range(KT):
            dve.wait_ge(sem("full_ready"), KT * pre_nth(K) + k + 1)
            dve.tensor_tensor(hlo[:, k, 0:TX], hf2[:, k, :], hhi[:, k, 0:TX].bitcast(F32), ALU.subtract)\
               .then_inc(sem("h_ready"), 1)

        dve.wait_ge(sem("logits_done"), 1)
        lg = ps[:, 7, 0:128].rearrange("p (t n) -> p t n", t=4)
        first4 = consts[:, 8:12].unsqueeze(1).to_broadcast([P, 4, 4])

        def r(n, w=4, c=0):
            return rt[:, n, :, c:c + w]

        def wide(ap, w):
            return ap.to_broadcast([P, 4, w])

        def one_hot(dst, val, top, rank):
            dve.tensor_tensor(dst, val, wide(top, 4), ALU.is_equal)
            dve.drain()
            dve.tensor_tensor(dst, dst, first4, ALU.mult)
            dve.drain()
            dve.tensor_reduce(rank, dst, AX_X, ALU.max)
            dve.drain()
            dve.tensor_tensor(dst, dst, wide(rank, 4), ALU.is_equal)
            dve.drain()

        dve.tensor_tensor(r(1, 16), lg[:, :, 4:20], bgr[:, 4:20].unsqueeze(1).to_broadcast([P, 4, 16]), ALU.add)
        dve.tensor_tensor(r(2), lg[:, :, 0:4], bgr[:, 0:4].unsqueeze(1).to_broadcast([P, 4, 4]), ALU.add)
        dve.drain()
        dve.tensor_reduce(r(4, 1), r(2), AX_X, ALU.max)
        dve.drain()
        one_hot(r(5), r(2), r(4, 1), r(4, 1, 1))
        dve.tensor_tensor(r(2), r(2), wide(r(4, 1), 4), ALU.subtract).then_inc(sem("g_ready"), 1)
        e4 = rt[:, 1, :, :].rearrange("p t (g e) -> p t g e", g=4)
        w4 = rt[:, 7, :, :].rearrange("p t (g e) -> p t g e", g=4)
        dve.tensor_tensor(w4, e4, r(5).unsqueeze(3).to_broadcast([P, 4, 4, 4]), ALU.mult)
        dve.drain()
        dve.tensor_reduce(r(6), rt[:, 7, :, :].rearrange("p t (g e) -> p t e g", g=4), AX_X, ALU.add)
        dve.drain()
        dve.tensor_reduce(r(4, 1, 2), r(6), AX_X, ALU.max)
        dve.drain()
        one_hot(r(10), r(6), r(4, 1, 2), r(4, 1, 1))
        dve.scalar_tensor_tensor(r(11), r(10), -1e30, r(6), ALU.mult, ALU.add)
        dve.drain()
        dve.tensor_reduce(r(4, 1, 3), r(11), AX_X, ALU.max)
        dve.drain()
        one_hot(r(12), r(11), r(4, 1, 3), r(4, 1, 1))
        dve.tensor_tensor(r(8, 1), r(4, 1, 3), r(4, 1, 2), ALU.subtract).then_inc(sem("e_ready"), 1)
        dve.wait_ge(sem("g_exp"), 1)
        dve.tensor_reduce(r(4, 1, 4), r(3), AX_X, ALU.add)
        dve.wait_ge(sem("e_exp"), 1)
        dve.tensor_scalar(r(9, 1, 1), r(9, 1), 1.0, None, ALU.add)
        dve.drain()
        dve.tensor_tensor(r(9, 1, 1), r(9, 1, 1), r(4, 1, 4), ALU.mult)
        dve.drain()
        dve.reciprocal(r(9, 1, 2), r(9, 1, 1))
        dve.drain()
        dve.tensor_tensor(r(9, 1, 3), r(9, 1, 2), r(9, 1), ALU.mult)
        dve.tensor_tensor(r(10), r(10), wide(r(9, 1, 2), 4), ALU.mult)
        dve.drain()
        dve.tensor_tensor(r(12), r(12), wide(r(9, 1, 3), 4), ALU.mult)
        dve.drain()
        dve.tensor_tensor(r(10), r(10), r(12), ALU.add)
        dve.drain()
        c4 = rt[:, 0, :, :].rearrange("p t (g e) -> p t g e", g=4)
        dve.tensor_tensor(c4, r(5).unsqueeze(3).to_broadcast([P, 4, 4, 4]),
                          r(10).unsqueeze(2).to_broadcast([P, 4, 4, 4]), ALU.mult).then_inc(sem("comb_tok"), 1)
        E0, G0 = B2_SLAB + IN2_T + OUT_T, B2_TILE + IN2_T + OUT_T
        dve.wait_ge(sem("comb_ready"), NEXP)
        with dve.Fori(0, MOE_TURNS) as i:
            for p in range(2 * EPI):
                e = esil[:, p % 2, :]
                dve.wait_ge(sem("esil_ready"), i * (2 * EPI) + (p + 1))
                dve.tensor_tensor(e, e, comb[:, bass.ds(i * EPI + p // 2, 1), :].rearrange("p a n -> p (a n)"),
                                  ALU.mult).then_inc(acc_free, 1)
                dve.drain()
                dve.wait_ge(slab_done, i * MOE_SLABS + (E0 + 2 * p + 2))
                dve.tensor_tensor(e, e, ps[:, bank2(G0 + 2 * p + 1), :], ALU.mult).then_inc(acc_free, 1)
                dve.drain().then_inc(sem("eprod_ready"), 1)
                dve.wait_ge(sem("ehi_ready"), i * (2 * EPI) + (p + 1))
                dve.tensor_tensor(elo[:, p, :], e, ehi[:, p, :].bitcast(F32), ALU.subtract)\
                   .then_inc(sem("eact_ready"), 1)
            for o in range(KT):
                dve.wait_ge(slab_done, i * MOE_SLABS + (E0 + MOE_UP + o + 1))
                dve.tensor_tensor(x[:, o, 0:TX], x[:, o, 0:TX], ps[:, bank2(G0 + MOE_UP + o), :], ALU.add)\
                   .then_inc(acc_free, 1)
            dve.drain()
        dve.drain().then_inc(sem("moe_done"), 1)
        K = (2, "final")
        inverse_rms(K, TX)
        for k in range(KT):
            dve.scalar_tensor_tensor(y[:, k, 0:TX], x[:, k, 0:TX], vec[:, V2_FIN + k:V2_FIN + k + 1], rbc[:, 0:TX],
                                     ALU.mult, ALU.mult).then_inc(sem("out_ready"), 1)

    blk.close()


def shape_constants():
    f = np.float32
    c = {"ident": np.eye(P, dtype=f)}
    c["headones"] = np.kron(np.eye(2), np.ones((HD, HD))).astype(f)
    r = np.zeros((P, P), f)
    for p in range(P):
        r[p + 16 if p % 32 < 16 else p - 16, p] = -1.0 if p % 32 < 16 else 1.0
    c["rot"] = r
    inv = f(10000.0) ** (-np.arange(0, 32, 2, dtype=f) / f(32))
    tok = np.arange(TX)
    row, col = (tok // 64).astype(f), (tok % 64).astype(f)
    d = np.arange(P) % HD
    ang = np.where((d < 32)[:, None], row[None, :], col[None, :]) * inv[d % 16][:, None]
    c["rope"] = np.stack([np.cos(ang), np.sin(ang)], 1).astype(f)
    con = np.zeros((P, 16), f)
    con[:, 0] = EPS
    tt = {0: np.linspace(0.0, 1.0, TX, dtype=f), 1: np.linspace(0.0, 1.0, TC, dtype=f)}
    for q in range(4):
        con[:, 2 + q] = -tt[0][q * P:q * P + P]
    for q in range(2):
        con[:, 6 + q] = -tt[1][q * P:q * P + P]
    con[:, 8:12] = [4, 3, 2, 1]
    con[0:4, 12:14] = [[1, 0], [0, 1], [1, 0], [0, 1]]
    c["consts"] = con

    def tiles(m):
        return m.reshape(-1, P, m.shape[1]).transpose(1, 0, 2)

    for L in (TX, TC):
        n, k = np.arange(L)[:, None], np.arange(L)[None, :]
        a = 2 * np.pi * ((n * k) % L) / L
        c[f"four{L}"] = np.stack([tiles(np.cos(a)), tiles(np.sin(a))], 1) / math.sqrt(L * HD)
        a = 2 * np.pi * ((n * (2 * k + 1)) % (4 * L)) / (4 * L)
        fw = np.stack([tiles(np.cos(a)), tiles(np.sin(a))], 1)
        iv = np.stack([tiles(np.cos(a).T), tiles(np.sin(a).T)], 1) / L
        if L == TX:
            c["hyf512"], c["hyi512"] = fw, iv
        else:
            c["hy256"] = np.concatenate([fw, iv], 1)
    n = np.arange(HD)
    a = 2 * np.pi * ((n[:, None] * n[None, :]) % HD) / HD
    c["fourch"] = np.concatenate([np.kron(np.eye(2), np.cos(a)), -np.kron(np.eye(2), np.sin(a))], 1)
    bands = np.linspace(1e-4, 15, 16, dtype=f)
    for s, L in ((0, TX), (1, TC)):
        w = f(2 * math.pi) * np.arange(L, dtype=f)[:, None] / f(L) * bands[None, :]
        c[f"z{L}"] = np.concatenate([tt[s][:, None], np.cos(w), -np.sin(w)], -1).T
    de = np.abs(np.linspace(math.log(1e-2) / 1.5, math.log(1e-2) / 0.3, 256, dtype=f))
    c["deltas"] = np.broadcast_to(de, (P, 256))
    j = np.arange(TABW)[None, :] - 3 * P - np.arange(P)[:, None]
    m = (abs(j) <= 64) * 1 + ((j % 4 == 0) & (abs(j) <= 256)) * 1 + (j % 16 == 0) * 1
    lm = np.where(m > 0, np.log(np.maximum(m, 1)), -1e30)
    slopes = 2.0 ** (-np.arange(1, 9))
    c["alibi"] = slopes[:, None, None] * abs(j)[None] - lm[None]
    qc, kc = np.arange(P)[:, None] % 64, np.arange(64)[None, :]
    st = np.clip(qc - 8, 0, 48)
    c["namask"] = np.where((kc >= st) & (kc < st + 16), 0.0, 1e30)
    es = np.zeros((NEXP, NEXP, P))
    for e in range(NEXP):
        es[e, e] = 1.0
    c["esel"] = es
    return {k: np.ascontiguousarray(v, dtype=f) for k, v in c.items()}


def slab(w):
    return w.reshape(KT, P, P).transpose(1, 0, 2).reshape(P, SLAB)


def slabs(w):
    n = w.shape[1] // P
    return w.reshape(KT, P, n, P).transpose(2, 1, 0, 3).reshape(n, P, SLAB)


def blocks(w, kt):
    b = w.reshape(kt, P, KT, P).transpose(2, 0, 1, 3).reshape(-1, KT, P, P)
    return b.transpose(0, 2, 1, 3).reshape(-1, P, SLAB)


def cols(v):
    return v.reshape(-1, P).T


def layout(a):
    o = {}
    fm = lambda v: np.ascontiguousarray(v[0].T.reshape(KT, P, -1).transpose(1, 0, 2))
    o["xT"], o["ctxT"] = fm(a["x"]), fm(a["ctx"])
    o["cT"] = np.stack([cols(a["c"][0]), cols(a["c_ctx"])], 2)
    o["w_mod"] = a["w_mod"].reshape(DEPTH, 4, 2, P, 12, 512).transpose(0, 4, 1, 3, 2, 5).reshape(MOD_SLABS, P, SLAB)
    order = np.concatenate([np.r_[j * HD:(j + 1) * HD, (j + NQT) * HD:(j + NQT + 1) * HD] for j in range(NQT)])
    parts, vec = [], np.zeros((P, N_VEC), np.float32)
    for L in range(DEPTH):
        w = a["w_in"][L]
        parts.append(slabs(np.concatenate([w[:, 512:640], w[:, order], w[:, 640:768], w[:, 768:]], 1)))
        w = a["w_out"][L]
        parts.append(slabs(np.concatenate([w[order], w[512:]])))
        vc = np.concatenate([a["w_ffn_conv"][L], a["b_ffn_conv"][L][None]])
        vc = vc.reshape(4, 2, CHUNKS, PAIRS, P).transpose(4, 2, 3, 1, 0)
        for c in range(CHUNKS):
            r = slice(c * PAIRS * P, (c + 1) * PAIRS * P)
            up = a["w_up"][L].reshape(D, 2, FF)[:, :, r].reshape(D, 2, PAIRS, P).transpose(0, 2, 1, 3).reshape(D, -1)
            parts += [slabs(up), blocks(a["w_down"][L][r], PAIRS)]
        v = vec[:, L * V_LAYER:]
        for at, n in ((V_GPM, "g_pre_mix"), (V_GQM, "g_post_mix"), (V_GPF, "g_pre_ffn"), (V_GQF, "g_post_ffn")):
            v[:, at:at + KT] = cols(a[n][L])
        v[:, V_GQ], v[:, V_GK] = np.tile(a["g_q"][L], 2), np.tile(a["g_k"][L], 2)
        hc = np.concatenate([a["w_hy_conv"][L], a["b_hy_conv"][L][None]])
        v[:, V_HYC:V_HYC + 4 * NHY] = hc.reshape(4, NHY, P).transpose(2, 1, 0).reshape(P, -1)
        v[:, V_FFC:V_FFC + CHUNKS * UP_T * 4] = vc.reshape(P, -1)
        v[:, V_HYB:V_HYB + 2] = cols(a["hy_bias"][L])
        for q, n in enumerate(("hy_b1", "hy_fr1", "hy_b2", "hy_fr2")):
            v[0:HD, V_MLP + q] = a[n][L]
    o["bmod"] = np.repeat(np.concatenate([cols(a["b_mod"][L]) for L in range(DEPTH)], 1), 2, axis=1)
    w = a["w_in_2"][0]
    parts += [slabs(w), slabs(a["w_out_2"][0])]
    for i in range(MOE_TURNS):
        for e in range(EPI * i, EPI * i + EPI):
            g, u = slabs(a["w_gate_2"][0, e]), slabs(a["w_up_2"][0, e])
            parts += [g[0:1], u[0:1], g[1:2], u[1:2]]
        dn = a["w_down_2"][0, EPI * i:EPI * i + EPI].reshape(EPI * DEXP, D)
        parts.append(blocks(dn, KT))
    o["w_all"] = np.concatenate(parts)
    vec[:, V2_MIX:V2_MIX + KT] = cols(a["norm_mix_g_2"][0])
    vec[:, V2_OUT:V2_OUT + 4] = cols(a["g_out_dil_2"][0])
    vec[:, V2_OUT + 4:V2_OUT + 8] = cols(a["g_out_na_2"][0])
    vec[:, V2_FFN:V2_FFN + KT] = cols(a["norm_ffn_g_2"][0])
    vec[:, V2_FIN:V2_FIN + KT] = cols(a["norm_final_g_2"])
    o["vec"] = vec
    o["w_four"] = a["w_fourier"].reshape(DEPTH, 2, P, 256).transpose(0, 2, 1, 3)
    for n in ("hy_w1", "hy_w2", "hy_w3"):
        o[n] = a[n]
    o["wgr"] = np.concatenate([a["w_group_2"][0], a["w_router_2"][0]], 1).reshape(KT, P, 20).transpose(1, 0, 2)
    o["bgr"] = np.broadcast_to(np.concatenate([a["b_group_2"][0], a["b_router_2"][0]]), (P, 20))
    rp = np.pad(a["rpb_2"][0], ((0, 0), (0, 0), (48, 48)))
    o["rpbw"] = np.stack([rp[:, :, 63 - q:127 - q] for q in range(64)], 1).reshape(8, 64, 15 * HD)
    return {k: np.ascontiguousarray(v) for k, v in o.items()}


def kernel(**inputs):
    import concourse.bacc as bacc
    from concourse.bass_utils import run_bass_kernel_spmd

    arrays = layout({k: np.asarray(v) for k, v in inputs.items()}) | shape_constants()
    nc = bacc.Bacc("TRN2", target_bir_lowering=False, num_devices=1, dynamic_dma_scratch_size=1024)
    dram = {n: nc.dram_tensor(f"in_{n}", a.shape, F32, kind="ExternalInput").ap() for n, a in arrays.items()}
    out = nc.dram_tensor("out_x", (P, KT, TX), F32, kind="ExternalOutput").ap()
    program(nc, dram, out)
    r = run_bass_kernel_spmd(nc, [{f"in_{n}": a for n, a in arrays.items()}], core_ids=[0])
    y = r.results[0]["out_x"]
    return np.ascontiguousarray(y.transpose(2, 1, 0).reshape(1, TX, D))
```
